# Optimizing a Trainium2 kernel written in Bass

```python
import math
import jax, jax.numpy as jnp
from jax import lax
import numpy as np

D_MODEL = 1024
BATCH = 1
SEQ = 256
DEPTH = 2
DEC_BATCH = 8
DEC_SEQ = 8
PAST_LEN = 2048
PAGE_SIZE = 128

N_EVEN = (DEPTH + 1) // 2
N_ODD = DEPTH // 2
N_MLA_HEADS = 8
Q_LORA = 256
KV_LORA = 256
D_NOPE = 64
D_ROPE = 32
D_V = 64
ROPE_BASE = 10000.0
MLA_SCALE = (D_NOPE + D_ROPE) ** -0.5
SWA_GROUPS = ((128, 1), (512, 4), (2048, 16))
N_SWA_GROUPS = 3
SWA_HEADS_PER_GROUP = 4
N_SWA_HEADS = N_SWA_GROUPS * SWA_HEADS_PER_GROUP
SWA_HEAD_DIM = 128
SWA_SCALE = SWA_HEAD_DIM ** -0.5
N_BUCKETS = 32
MAX_DISTANCE = 2048
IN_ATTN = Q_LORA + KV_LORA + D_ROPE + 3 * N_SWA_HEADS * SWA_HEAD_DIM
OUT_ATTN = N_MLA_HEADS * D_V + SWA_HEADS_PER_GROUP * SWA_HEAD_DIM
D_CONV = D_MODEL
CONV_WIDTH = 3
N_MEM = 256
N_MEM_HEADS = 4
MEM_HEAD_DIM = D_MODEL // N_MEM_HEADS
MEM_SCALE = MEM_HEAD_DIM ** -0.5
N_KEYS = 128
N_EXPERTS = N_KEYS * N_KEYS
N_PEER_HEADS = 8
D_KEY = 256
D_KEY_HALF = D_KEY // 2
TOPK = 16
PEER_BLOCK = 128
Q_BLOCK = 128
LN_EPS = 1e-5
DEEPNORM_ALPHA = (2 * DEPTH) ** 0.25
DEEPNORM_BETA = (8 * DEPTH) ** -0.25

kernel_name = 'hybrid_mla_dilated_conv_peer_decode_step'

def layer_norm(x, g, b):
    xf = x.astype(jnp.float32)
    mu = jnp.mean(xf, axis=-1, keepdims=True)
    var = jnp.mean(jnp.square(xf - mu), axis=-1, keepdims=True)
    return ((xf - mu) * lax.rsqrt(var + LN_EPS) * g.astype(jnp.float32) + b.astype(jnp.float32)).astype(x.dtype)

def rms_norm(x, g):
    xf = x.astype(jnp.float32)
    return (xf * lax.rsqrt(jnp.mean(jnp.square(xf), axis=-1, keepdims=True) + LN_EPS) * g.astype(jnp.float32)).astype(x.dtype)

def apply_rope(x, pos):
    half = D_ROPE // 2
    inv = ROPE_BASE ** (-jnp.arange(half, dtype=jnp.float32) / half)
    ang = pos.astype(jnp.float32)[:, None] * inv[None, :]
    cos, sin = jnp.cos(ang)[:, None, :], jnp.sin(ang)[:, None, :]
    x1, x2 = x[..., :half].astype(jnp.float32), x[..., half:].astype(jnp.float32)
    return jnp.concatenate([x1 * cos - x2 * sin, x2 * cos + x1 * sin], axis=-1).astype(x.dtype)

def t5_bucket(dist):
    max_exact = N_BUCKETS // 2
    d = jnp.maximum(dist.astype(jnp.float32), 1.0)
    large = max_exact + (jnp.log(d / max_exact) / math.log(MAX_DISTANCE / max_exact) * (N_BUCKETS - max_exact)).astype(jnp.int32)
    large = jnp.minimum(large, N_BUCKETS - 1)
    return jnp.where(dist < max_exact, dist, large)

def map_query_blocks(fn, q_pos, *qs):
    sq = q_pos.shape[0]
    if sq <= Q_BLOCK:
        return fn(q_pos, *qs)
    nb = sq // Q_BLOCK
    pos_b = q_pos.reshape(nb, Q_BLOCK)
    qs_b = [jnp.moveaxis(q.reshape((q.shape[0], nb, Q_BLOCK) + q.shape[2:]), 1, 0) for q in qs]
    out = lax.map(lambda a: fn(*a), (pos_b, *qs_b))
    return jax.tree_util.tree_map(
        lambda o: jnp.moveaxis(o, 0, 1).reshape((o.shape[1], sq) + o.shape[3:]), out)

def mla_attend(q_pos, q_lat, q_rope, ckv, krope, k_pos):
    s = jnp.einsum('bqhc,bkc->bhqk', q_lat, ckv) + jnp.einsum('bqhr,bkr->bhqk', q_rope, krope)
    s = s.astype(jnp.float32) * MLA_SCALE
    s = jnp.where((k_pos[None, :] <= q_pos[:, None])[None, None], s, -jnp.inf)
    p = jax.nn.softmax(s, axis=-1).astype(ckv.dtype)
    return jnp.einsum('bhqk,bkc->bqhc', p, ckv)

def dilated_group_attend(q_pos, q, kv_all, row0_pos, win, dil, bias):
    nk = win // dil + 1
    dist = jnp.arange(nk, dtype=jnp.int32) * dil
    key_pos = q_pos[:, None] - dist[None, :]
    kv = jnp.take(kv_all, key_pos - row0_pos, axis=1)
    s = jnp.einsum('bqhd,bqjhd->bhqj', q, kv[:, :, :, 0]).astype(jnp.float32) * SWA_SCALE
    s = s + bias.astype(jnp.float32).T[None, :, None, :]
    s = jnp.where((key_pos >= 0)[None, None], s, -jnp.inf)
    m = jnp.max(s, axis=-1, keepdims=True)
    e = jnp.exp(s - m)
    den = jnp.sum(e, axis=-1, keepdims=True)
    o = jnp.einsum('bhqj,bqjhd->bqhd', (e / den).astype(q.dtype), kv[:, :, :, 1])
    lse = jnp.transpose((m + jnp.log(den))[..., 0], (0, 2, 1))
    return o, lse

def even_mixer(x, pos, past_len, mla_past, swa_past, w_in, q_norm_g, kv_norm_g, w_uq, w_uk, w_uv, w_out, rel_bias):
    B, S, _ = x.shape
    c_q, c_kv, k_r, swa_qkv = jnp.split(
        x @ w_in, [Q_LORA, Q_LORA + KV_LORA, Q_LORA + KV_LORA + D_ROPE], axis=-1)
    q = (rms_norm(c_q, q_norm_g) @ w_uq).reshape(B, S, N_MLA_HEADS, D_NOPE + D_ROPE)
    q_lat = jnp.einsum('bshn,chn->bshc', q[..., :D_NOPE], w_uk)
    q_rope = apply_rope(q[..., D_NOPE:], pos)
    rows = jnp.concatenate(
        [rms_norm(c_kv, kv_norm_g), apply_rope(k_r[:, :, None, :], pos)[:, :, 0]], axis=-1)
    kv_all = rows if mla_past is None else jnp.concatenate([mla_past.astype(rows.dtype), rows], axis=1)
    ckv_all, kr_all = kv_all[..., :KV_LORA], kv_all[..., KV_LORA:]
    k_pos = jnp.arange(past_len + S, dtype=jnp.int32)
    o_lat = map_query_blocks(
        lambda qp, ql, qr: mla_attend(qp, ql, qr, ckv_all, kr_all, k_pos), pos, q_lat, q_rope)
    o_mla = jnp.einsum('bshc,chv->bshv', o_lat, w_uv).reshape(B, S, N_MLA_HEADS * D_V)
    qkv = swa_qkv.reshape(B, S, 3, N_SWA_GROUPS, SWA_HEADS_PER_GROUP, SWA_HEAD_DIM)
    outs, lses, new_bufs = [], [], []
    for g, (win, dil) in enumerate(SWA_GROUPS):
        kv_new = qkv[:, :, 1:, g]
        if swa_past is None:
            prefix = jnp.zeros((B, win) + kv_new.shape[2:], kv_new.dtype)
        else:
            prefix = swa_past[g].astype(kv_new.dtype)
        kv_g = jnp.concatenate([prefix, kv_new], axis=1)
        new_bufs.append(kv_g[:, -win:])
        bias = rel_bias[t5_bucket(jnp.arange(win // dil + 1, dtype=jnp.int32) * dil),
                        g * SWA_HEADS_PER_GROUP:(g + 1) * SWA_HEADS_PER_GROUP]
        o, lse = map_query_blocks(
            lambda qp, qg: dilated_group_attend(qp, qg, kv_g, past_len - win, win, dil, bias),
            pos, qkv[:, :, 0, g])
        outs.append(o)
        lses.append(lse)
    wgt = jax.nn.softmax(jnp.stack(lses), axis=0)
    o_swa = jnp.einsum('gbsh,gbshd->bshd', wgt, jnp.stack(outs).astype(jnp.float32))
    o_swa = o_swa.astype(x.dtype).reshape(B, S, SWA_HEADS_PER_GROUP * SWA_HEAD_DIM)
    y = jnp.concatenate([o_mla, o_swa], axis=-1) @ w_out
    return y, rows, new_bufs

def odd_mixer(x, conv_state, w_in, conv_w, w_out):
    B, S, _ = x.shape
    b_gate, c_gate, h = jnp.split(x @ w_in, 3, axis=-1)
    u = c_gate * h
    prefix = jnp.zeros((B, CONV_WIDTH - 1, D_CONV), u.dtype) if conv_state is None else conv_state.astype(u.dtype)
    u_all = jnp.concatenate([prefix, u], axis=1)
    conv = conv_w[0] * u_all[:, 0:S]
    for k in range(1, CONV_WIDTH):
        conv = conv + conv_w[k] * u_all[:, k:k + S]
    return (b_gate * conv) @ w_out, u_all[:, -(CONV_WIDTH - 1):]

def mem_kv_proj(mem, wk, wv):
    B = mem.shape[0]
    k = (mem @ wk).reshape(B, N_MEM, N_MEM_HEADS, MEM_HEAD_DIM)
    v = (mem @ wv).reshape(B, N_MEM, N_MEM_HEADS, MEM_HEAD_DIM)
    return jnp.stack([k, v], axis=2)

def mem_attend(x, kv, wq, wo):
    B, S, _ = x.shape
    q = (x @ wq).reshape(B, S, N_MEM_HEADS, MEM_HEAD_DIM)
    s = jnp.einsum('bshd,bmhd->bhsm', q, kv[:, :, 0].astype(q.dtype)).astype(jnp.float32) * MEM_SCALE
    p = jax.nn.softmax(s, axis=-1).astype(x.dtype)
    o = jnp.einsum('bhsm,bmhd->bshd', p, kv[:, :, 1].astype(x.dtype)).reshape(B, S, D_MODEL)
    return o @ wo

def peer(x, wq, subkeys, u, v):
    B, S, D = x.shape
    t = x.reshape(B * S, D)
    T = t.shape[0]
    nb = -(-T // PEER_BLOCK)
    t = jnp.pad(t, ((0, nb * PEER_BLOCK - T), (0, 0))).reshape(nb, PEER_BLOCK, D)

    def block(tb):
        q = (tb @ wq).reshape(PEER_BLOCK, N_PEER_HEADS, 2, D_KEY_HALF)
        s = jnp.einsum('thpk,hpnk->thpn', q, subkeys).astype(jnp.float32)
        s_top, i_top = lax.top_k(s, TOPK)
        cand = (s_top[:, :, 0, :, None] + s_top[:, :, 1, None, :]).reshape(PEER_BLOCK, N_PEER_HEADS, TOPK * TOPK)
        cand_idx = (i_top[:, :, 0, :, None] * N_KEYS + i_top[:, :, 1, None, :]).reshape(PEER_BLOCK, N_PEER_HEADS, TOPK * TOPK)
        best, sel = lax.top_k(cand, TOPK)
        experts = jnp.take_along_axis(cand_idx, sel, axis=-1)
        g = jax.nn.softmax(best, axis=-1).astype(tb.dtype)
        act = jax.nn.gelu(jnp.einsum('td,thkd->thk', tb, u[experts]), approximate=False)
        return jnp.einsum('thk,thkd->td', g * act, v[experts])

    y = lax.map(block, t)
    return y.reshape(nb * PEER_BLOCK, D)[:T].reshape(B, S, D)

def trunk(x, past_len, cache_mla, page_table, swa_past, conv_past, mem_kv, w):
    B, S, _ = x.shape
    pos = past_len + jnp.arange(S, dtype=jnp.int32)
    mla_rows, swa_bufs, conv_rows = [], [[] for _ in SWA_GROUPS], []
    for layer in range(DEPTH):
        i = layer // 2
        if layer % 2 == 0:
            mla_past = None if cache_mla is None else cache_mla[i][page_table].reshape(B, past_len, KV_LORA + D_ROPE)
            bufs = None if swa_past is None else [c[i] for c in swa_past]
            h, rows, new_bufs = even_mixer(
                x, pos, past_len, mla_past, bufs, w['attn_w_in'][i], w['mla_q_norm'][i], w['mla_kv_norm'][i],
                w['mla_w_uq'][i], w['mla_w_uk'][i], w['mla_w_uv'][i], w['attn_w_out'][i], w['rel_bias'])
            mla_rows.append(rows)
            for g in range(N_SWA_GROUPS):
                swa_bufs[g].append(new_bufs[g])
        else:
            st = None if conv_past is None else conv_past[i]
            h, new_st = odd_mixer(x, st, w['conv_w_in'][i], w['conv_w'][i], w['conv_w_out'][i])
            conv_rows.append(new_st)
        x = layer_norm(DEEPNORM_ALPHA * x + h, w['ln_mix_g'][layer], w['ln_mix_b'][layer])
        x = layer_norm(DEEPNORM_ALPHA * x + mem_attend(x, mem_kv[layer], w['mem_wq'][layer], w['mem_wo'][layer]),
                       w['ln_mem_g'][layer], w['ln_mem_b'][layer])
        x = layer_norm(DEEPNORM_ALPHA * x + peer(x, w['peer_wq'][layer], w['peer_subkeys'][layer],
                                                w['peer_u'][layer], w['peer_v'][layer]),
                       w['ln_ffn_g'][layer], w['ln_ffn_b'][layer])
    return x, jnp.stack(mla_rows), [jnp.stack(b) for b in swa_bufs], jnp.stack(conv_rows)

def setup_inputs(seed: int = 0) -> dict:
    key = jax.random.key(seed)
    keys = iter(jax.random.split(key, 48))

    def nrm(shape, scale=1.0):
        return jax.random.normal(next(keys), shape, jnp.float32) * scale

    n_pages = PAST_LEN // PAGE_SIZE
    n_pool = (DEC_BATCH * n_pages * 5) // 4
    page_table = jax.random.permutation(next(keys), n_pool)[:DEC_BATCH * n_pages]
    page_table = page_table.reshape(DEC_BATCH, n_pages).astype(jnp.int32)
    swa = [nrm((N_EVEN, DEC_BATCH, win, 2, SWA_HEADS_PER_GROUP, SWA_HEAD_DIM)) for win, _ in SWA_GROUPS]
    return {
        'x_prompt': nrm((BATCH, SEQ, D_MODEL)),
        'x_sample': nrm((DEC_BATCH, DEC_SEQ, D_MODEL)),
        'cache_mla': nrm((N_EVEN, n_pool, PAGE_SIZE, KV_LORA + D_ROPE)),
        'page_table': page_table,
        'cache_swa_w128': swa[0],
        'cache_swa_w512': swa[1],
        'cache_swa_w2048': swa[2],
        'state_conv': nrm((N_ODD, DEC_BATCH, CONV_WIDTH - 1, D_CONV)),
        'cache_mem_kv': nrm((DEPTH, DEC_BATCH, N_MEM, 2, N_MEM_HEADS, MEM_HEAD_DIM)),
        'mem_prompt': nrm((BATCH, N_MEM, D_MODEL)),
        'attn_w_in': nrm((N_EVEN, D_MODEL, IN_ATTN), D_MODEL ** -0.5),
        'mla_q_norm': 1.0 + nrm((N_EVEN, Q_LORA), 0.02),
        'mla_kv_norm': 1.0 + nrm((N_EVEN, KV_LORA), 0.02),
        'mla_w_uq': nrm((N_EVEN, Q_LORA, N_MLA_HEADS * (D_NOPE + D_ROPE)), Q_LORA ** -0.5),
        'mla_w_uk': nrm((N_EVEN, KV_LORA, N_MLA_HEADS, D_NOPE), KV_LORA ** -0.5),
        'mla_w_uv': nrm((N_EVEN, KV_LORA, N_MLA_HEADS, D_V), KV_LORA ** -0.5),
        'attn_w_out': nrm((N_EVEN, OUT_ATTN, D_MODEL), OUT_ATTN ** -0.5 * DEEPNORM_BETA),
        'rel_bias': nrm((N_BUCKETS, N_SWA_HEADS), 0.5),
        'conv_w_in': nrm((N_ODD, D_MODEL, 3 * D_CONV), D_MODEL ** -0.5),
        'conv_w': nrm((N_ODD, CONV_WIDTH, D_CONV), CONV_WIDTH ** -0.5),
        'conv_w_out': nrm((N_ODD, D_CONV, D_MODEL), D_CONV ** -0.5 * DEEPNORM_BETA),
        'mem_wq': nrm((DEPTH, D_MODEL, D_MODEL), D_MODEL ** -0.5),
        'mem_wk': nrm((DEPTH, D_MODEL, D_MODEL), D_MODEL ** -0.5),
        'mem_wv': nrm((DEPTH, D_MODEL, D_MODEL), D_MODEL ** -0.5),
        'mem_wo': nrm((DEPTH, D_MODEL, D_MODEL), D_MODEL ** -0.5 * DEEPNORM_BETA),
        'ln_mix_g': 1.0 + nrm((DEPTH, D_MODEL), 0.02),
        'ln_mix_b': nrm((DEPTH, D_MODEL), 0.02),
        'ln_mem_g': 1.0 + nrm((DEPTH, D_MODEL), 0.02),
        'ln_mem_b': nrm((DEPTH, D_MODEL), 0.02),
        'ln_ffn_g': 1.0 + nrm((DEPTH, D_MODEL), 0.02),
        'ln_ffn_b': nrm((DEPTH, D_MODEL), 0.02),
        'peer_wq': nrm((DEPTH, D_MODEL, N_PEER_HEADS * D_KEY), D_MODEL ** -0.5),
        'peer_subkeys': nrm((DEPTH, N_PEER_HEADS, 2, N_KEYS, D_KEY_HALF), D_KEY_HALF ** -0.5),
        'peer_u': nrm((DEPTH, N_EXPERTS, D_MODEL), D_MODEL ** -0.5),
        'peer_v': nrm((DEPTH, N_EXPERTS, D_MODEL), N_PEER_HEADS ** -0.5 * DEEPNORM_BETA),
    }

def reference(x_prompt, x_sample, cache_mla, page_table, cache_swa_w128, cache_swa_w512, cache_swa_w2048,
              state_conv, cache_mem_kv, mem_prompt, attn_w_in, mla_q_norm, mla_kv_norm, mla_w_uq, mla_w_uk,
              mla_w_uv, attn_w_out, rel_bias, conv_w_in, conv_w, conv_w_out, mem_wq, mem_wk, mem_wv, mem_wo,
              ln_mix_g, ln_mix_b, ln_mem_g, ln_mem_b, ln_ffn_g, ln_ffn_b, peer_wq, peer_subkeys, peer_u, peer_v):
    w = dict(attn_w_in=attn_w_in, mla_q_norm=mla_q_norm, mla_kv_norm=mla_kv_norm, mla_w_uq=mla_w_uq,
             mla_w_uk=mla_w_uk, mla_w_uv=mla_w_uv, attn_w_out=attn_w_out, rel_bias=rel_bias,
             conv_w_in=conv_w_in, conv_w=conv_w, conv_w_out=conv_w_out, mem_wq=mem_wq, mem_wo=mem_wo,
             ln_mix_g=ln_mix_g, ln_mix_b=ln_mix_b, ln_mem_g=ln_mem_g, ln_mem_b=ln_mem_b,
             ln_ffn_g=ln_ffn_g, ln_ffn_b=ln_ffn_b, peer_wq=peer_wq, peer_subkeys=peer_subkeys,
             peer_u=peer_u, peer_v=peer_v)
    mem_kv_prompt = jnp.stack([mem_kv_proj(mem_prompt, mem_wk[l], mem_wv[l]) for l in range(DEPTH)])
    y_prompt, mla_p, swa_p, conv_p = trunk(x_prompt, 0, None, None, None, None, mem_kv_prompt, w)
    y_sample, mla_s, swa_s, conv_s = trunk(
        x_sample, PAST_LEN, cache_mla, page_table, [cache_swa_w128, cache_swa_w512, cache_swa_w2048],
        state_conv, cache_mem_kv, w)
    return (y_prompt, y_sample, mla_p, mla_s, swa_p[0], swa_s[0], swa_p[1], swa_s[1], swa_p[2], swa_s[2],
            conv_p, conv_s, mem_kv_prompt)


_drawn_inputs = setup_inputs


def setup_inputs(seed=0):
    import zlib

    import numpy as np

    out = dict(_drawn_inputs(seed))
    spreads = {}
    factors = {'cache_mla': 3.48, 'mla_q_norm': 8.0, 'mla_kv_norm': 3.119, 'rel_bias': 3.039}
    for name, (base, spread) in spreads.items():
        noise = np.random.default_rng([zlib.crc32(name.encode()), seed]).standard_normal(out[name].shape)
        drawn = base * np.exp(spread * noise) if base else spread * noise
        out[name] = __import__('jax').numpy.asarray(drawn.astype(out[name].dtype))
    for name, factor in factors.items():
        out[name] = (out[name] * factor).astype(out[name].dtype)
    return out
```

```python
import math

import numpy as np
import concourse.bass as bass
from concourse import mybir
from contextlib import ExitStack, contextmanager

F32 = mybir.dt.float32
I32 = mybir.dt.int32
U32 = mybir.dt.uint32
ALU = mybir.AluOpType
ACT = mybir.ActivationFunctionType
AX = mybir.AxisListType.X
ds = bass.ds

P = 128
D = 1024
KC = D // P
SEQ = 256
DEC_B, DEC_S = 8, 8
T = SEQ + DEC_B * DEC_S
TILES = [(0, 128), (128, 128), (256, 64)]
PROMPT_TILES = TILES[:2]
DEPTH = 2
PAST = 2048
PAGE = 128
N_PAGES = PAST // PAGE
Q_LORA = KV_LORA = 256
NOPE, ROPE, D_V = 64, 32, 64
MLA_H = 8
MLA_SCALE = (NOPE + ROPE) ** -0.5
MLA_ROW = KV_LORA + ROPE
SWA_GROUPS = ((128, 1), (512, 4), (2048, 16))
SWA_H, SWA_D = 4, 128
SWA_SCALE = SWA_D ** -0.5
GW = SWA_H * SWA_D
N_BUCKETS, MAX_DIST = 32, 2048
N_MEM, MEM_H, MEM_D = 256, 4, 256
MEM_SCALE = MEM_D ** -0.5
N_KEYS = 128
N_EXPERTS = N_KEYS * N_KEYS
PEER_H, TOPK = 8, 16
HK = PEER_H * TOPK
ALPHA = (2 * DEPTH) ** 0.25
EPS = 1e-5
DISALLOWED = -1e30
LOWEST = -3e38
DIST_TOP = 2055
N_DIST = 2312
REP0, REP_N = 1800, 512
PAD = 32
SWA_TILES = [(0, 0)] + [(1, i) for i in range(4)] + [(2, i) for i in range(8)]
SWA_CACHED = len(SWA_TILES) * P
SWA_KEYS = SWA_CACHED + 3 * DEC_S


def wait(eng, sem, n):
    if not isinstance(n, int) or n > 0:
        eng.wait_ge(sem, n)


def wait_apart(eng, sem, n, begun):
    if not isinstance(n, int) or n > 0:
        eng.wait_ge(sem, n)
        eng.sem_inc(begun, 1)


def repeat(eng, n, body):
    body(0)
    if n == 2:
        body(1)
    elif n > 2:
        with eng.Fori(1, n) as i:
            body(i)


def repeat_ends(eng, n, body):
    body(0, False)
    if n == 3:
        body(1, False)
    elif n > 3:
        with eng.Fori(1, n - 1) as i:
            body(i, False)
    body(n - 1, True)


class Chain:

    def __init__(self, eng, sem, start=0):
        self.eng, self.sem, self.n, self.start = eng, sem, 0, start

    def __call__(self, ins):
        self.n += 1
        ins.then_inc(self.sem, 1)
        self.eng.wait_ge(self.sem, self.start + self.n)


class Kernel:

    def __init__(self, nc, ctx, io):
        self.nc, self.ctx, self.io = nc, ctx, io
        self.copied = ctx.enter_context(nc.semaphore("swa_copied"))
        self.held, self.bank, self.blocks, self.bank_size = [], 0, 0, 46
        names = ["page_landed0", "page_landed1", "window_v_landed0", "window_v_landed1"]
        names += [f"{r}_rows_landed{g}" for r in "uv" for g in range(4)]
        self.gathered = {n: ctx.enter_context(nc.semaphore(n)) for n in names}
        self.first_sem = max(s.num for s in self.gathered.values()) + 1
        self.ps = ctx.enter_context(nc.psum_tensor("ps", [P, 8, 512], F32))
        self.ident = self.sb(ctx, "ident", [P, P])
        self.x = self.sb(ctx, "x_tok", [P, 3, D])
        self.h = self.sb(ctx, "h_tok", [P, 3, D])
        self.xT = self.sb(ctx, "xT", [P, KC, T])
        self.memT = self.sb(ctx, "memT", [P, KC, N_MEM])

    def sb(self, ctx, name, shape, dt=F32):
        return ctx.enter_context(self.nc.sbuf_tensor(name, shape, dt))

    def sem(self, name):
        num = self.first_sem + self.bank * self.bank_size + len(self.held)
        assert len(self.held) < self.bank_size
        self.held.append(self.nc.alloc_semaphore(name=name, num=num))
        return self.held[-1]

    @contextmanager
    def block(self):
        if self.blocks >= 2:
            first = self.first_sem + (self.bank + 1) % 3 * self.bank_size
            self.nc.sync.sem_clear(range(first, first + self.bank_size))
        with self.nc.Block() as block:
            yield block
        for handle in self.held:
            self.nc.release_semaphore(handle)
        self.held, self.bank, self.blocks = [], (self.bank + 1) % 3, self.blocks + 1


def start_stage(k):
    nc, io = k.nc, k.io
    with ExitStack() as ctx:
        mem = k.sb(ctx, "mem_tok", [P, 2, D])
        loaded, turned, bank_free = k.sem("st_loaded"), k.sem("st_turned"), k.sem("st_free")
        block = ctx.enter_context(k.block())
        jobs = []
        for i, (t0, n) in enumerate(TILES):
            jobs += [(k.x[0:n, i, :], n, k.xT, t0, half) for half in range(2)]
        for i in range(2):
            jobs += [(mem[:, i, :], P, k.memT, i * P, half) for half in range(2)]

        @block.sync
        def _(sp):
            sp.dma_start(k.ident[:, :], io["ident"]).then_inc(loaded, 16)
            sp.dma_start(k.x[:, 0:2, :], io["x_prompt"][0].rearrange("(i p) d -> p i d", p=P)).then_inc(loaded, 16)
            sp.dma_start(k.x[0:64, 2, :], io["x_sample"].rearrange("b s d -> (b s) d")).then_inc(loaded, 16)
            sp.dma_start(mem[:, :, :], io["mem_prompt"][0].rearrange("(i p) d -> p i d", p=P)).then_inc(loaded, 16)

        @block.tensor
        def _(pe):
            pe.wait_ge(loaded, 64)
            for n, (src, rows, _, _, half) in enumerate(jobs):
                wait(pe, bank_free, n - 1)
                for j in range(4):
                    c = half * 4 + j
                    last = pe.transpose(k.ps[:, n % 2, j * P:j * P + rows], src[:, c * P:(c + 1) * P],
                                        k.ident[0:rows, 0:rows])
                last.then_inc(turned, 1)

        @block.scalar
        def _(act):
            for n, (_, rows, dst, t0, half) in enumerate(jobs):
                act.wait_ge(turned, n + 1)
                bank = k.ps[:, n % 2, :].rearrange("p (j t) -> p j t", j=4)
                act.activation(dst[:, half * 4:half * 4 + 4, t0:t0 + rows], bank[:, :, 0:rows],
                               ACT.Copy).then_inc(bank_free, 1)


def gemm_stage(k, name, jobs):
    nc = k.nc
    with ExitStack() as ctx:
        ring = k.sb(ctx, name + "_w", [P, 2, KC * 512])
        landed = [k.sem(f"{name}_w_landed{s}") for s in range(2)]
        chunk_done, bank_free = k.sem(name + "_chunk_done"), k.sem(name + "_bank_free")
        block = ctx.enter_context(k.block())

        def plan():
            base = 0
            for kind, aT, w, chunk, out in jobs:
                n = w.shape[1] // chunk
                assert n * chunk == w.shape[1] and n % 2 == 0
                yield kind, aT, w, chunk, out, n // 2, base
                base += n

        def parts(kind, aT, chunk):
            tokens = aT.shape[2]
            if kind == "tok":
                return [(t0, min(P, tokens - t0)) for t0 in range(0, tokens, P)]
            return list(range(chunk // P))

        def slot_view(s, kc, chunk):
            return ring[:, s, 0:kc * chunk].rearrange("p (c n) -> p c n", c=kc)

        @block.sync
        def _(sp):
            for kind, aT, w, chunk, out, pairs, base in plan():
                kc = aT.shape[1]

                def load(i):
                    for s in range(2):
                        n = base + 2 * i + s
                        wait(sp, chunk_done, n - 1)
                        src = w[:, ds((2 * i + s) * chunk, chunk)].rearrange("(c p) n -> p c n", p=P)
                        sp.dma_start(slot_view(s, kc, chunk), src).then_inc(landed[s], 16)
                repeat(sp, pairs, load)

        @block.tensor
        def _(pe):
            for kind, aT, w, chunk, out, pairs, base in plan():
                kc = aT.shape[1]

                def product(i):
                    for s in range(2):
                        n = base + 2 * i + s
                        pe.wait_ge(landed[s], (base // 2 + i) * 16 + 16)
                        wait(pe, bank_free, n - 1)
                        wv = slot_view(s, kc, chunk)
                        for j, part in enumerate(parts(kind, aT, chunk)):
                            for c in range(kc):
                                if kind == "tok":
                                    t0, rows = part
                                    mm = pe.matmul(k.ps[0:rows, 4 * s + j, 0:chunk], aT[:, c, t0:t0 + rows],
                                                   wv[:, c, :], start=(c == 0), stop=(c == kc - 1))
                                else:
                                    mm = pe.matmul(k.ps[:, 4 * s + j, 0:aT.shape[2]], wv[:, c, j * P:(j + 1) * P],
                                                   aT[:, c, :], start=(c == 0), stop=(c == kc - 1))
                        mm.then_inc(chunk_done, 1)
                repeat(pe, pairs, product)

        @block.scalar
        def _(act):
            for kind, aT, w, chunk, out, pairs, base in plan():

                def evacuate(i):
                    for s in range(2):
                        n = base + 2 * i + s
                        act.wait_ge(chunk_done, n + 1)
                        ps = parts(kind, aT, chunk)
                        for j, part in enumerate(ps):
                            if kind == "tok":
                                dst = out[0:part[1], j, ds((2 * i + s) * chunk, chunk)]
                                src = k.ps[0:part[1], 4 * s + j, 0:chunk]
                            else:
                                tn = aT.shape[2]
                                dst = out[:, ds(((2 * i + s) * len(ps) + j) * tn, tn)]
                                src = k.ps[:, 4 * s + j, 0:tn]
                            last = act.activation(dst, src, ACT.Copy)
                        last.then_inc(bank_free, 1)
                repeat(act, pairs, evacuate)


def norm_stage(k, name, g, b, y=None):
    nc = k.nc
    with ExitStack() as ctx:
        gain, shift = k.sb(ctx, name + "_gain", [P, D]), k.sb(ctx, name + "_shift", [P, D])
        stats = k.sb(ctx, name + "_stats", [P, 3, 2, 6])
        mv = k.sb(ctx, name + "_mean_var", [P, 3, 2])
        rstd = k.sb(ctx, name + "_rstd", [P, 3])
        landed, chain, var_ready = k.sem(name + "_landed"), k.sem(name + "_chain"), k.sem(name + "_var")
        root_ready, x_ready = k.sem(name + "_root"), k.sem(name + "_x")
        turned, bank_free, stored = k.sem(name + "_turned"), k.sem(name + "_free"), k.sem(name + "_stored")
        block = ctx.enter_context(k.block())

        @block.sync
        def _(sp):
            for dst, src in ((gain, g), (shift, b)):
                sp.dma_start(dst[:, :], bass.AP(src.tensor, src.offset, [[0, P], [1, D]])).then_inc(landed, 16)
            if y is not None:
                for i, (t0, n) in enumerate(TILES):
                    sp.wait_ge(x_ready, i + 1)
                    sp.dma_start(y[i], k.x[0:n, i, :]).then_inc(stored, 16)
                sp.wait_ge(stored, 16 * len(TILES))

        @block.vector
        def _(dve):
            count = 0
            for i, (_, n) in enumerate(TILES):
                dve.scalar_tensor_tensor(out=k.x[0:n, i, :], in0=k.x[0:n, i, :], scalar=ALPHA, in1=k.h[0:n, i, :],
                                         op0=ALU.mult, op1=ALU.add).then_inc(chain, 1)
            count += 3
            for i, (_, n) in enumerate(TILES):
                dve.wait_ge(chain, i + 1)
                for half in range(2):
                    dve.bn_stats(out=stats[0:n, i, half, :],
                                 in_=k.x[0:n, i, half * 512:(half + 1) * 512]).then_inc(chain, 1)
            count += 6
            for i, (_, n) in enumerate(TILES):
                dve.wait_ge(chain, 3 + 2 * (i + 1))
                dve.bn_aggr(out=mv[0:n, i, :], in_=stats[0:n, i, :, :]).then_inc(chain, 1)
            count += 3
            for i, (_, n) in enumerate(TILES):
                dve.wait_ge(chain, 9 + i + 1)
                dve.tensor_scalar(out=rstd[0:n, i:i + 1], in0=mv[0:n, i, 1:2], scalar1=EPS, scalar2=None,
                                  op0=ALU.add).then_inc(var_ready, 1)
            for i, (_, n) in enumerate(TILES):
                dve.wait_ge(root_ready, i + 1)
                dve.reciprocal(rstd[0:n, i:i + 1], rstd[0:n, i:i + 1]).then_inc(chain, 1)
            count += 3
            dve.wait_ge(chain, count)
            for i, (_, n) in enumerate(TILES):
                dve.tensor_scalar(out=k.x[0:n, i, :], in0=k.x[0:n, i, :], scalar1=mv[0:n, i, 0:1],
                                  scalar2=rstd[0:n, i:i + 1], op0=ALU.subtract, op1=ALU.mult).then_inc(chain, 1)
            dve.wait_ge(landed, 32)
            for i, (_, n) in enumerate(TILES):
                dve.wait_ge(chain, count + i + 1)
                dve.tensor_tensor(out=k.x[0:n, i, :], in0=k.x[0:n, i, :], in1=gain[0:n, :],
                                  op=ALU.mult).then_inc(chain, 1)
            for i, (_, n) in enumerate(TILES):
                dve.wait_ge(chain, count + 3 + i + 1)
                dve.tensor_tensor(out=k.x[0:n, i, :], in0=k.x[0:n, i, :], in1=shift[0:n, :],
                                  op=ALU.add).then_inc(x_ready, 1)

        @block.scalar
        def _(act):
            for i, (_, n) in enumerate(TILES):
                act.wait_ge(var_ready, i + 1)
                act.activation(rstd[0:n, i:i + 1], rstd[0:n, i:i + 1], ACT.Sqrt).then_inc(root_ready, 1)
            if y is None:
                for n2 in range(6):
                    i, half = divmod(n2, 2)
                    t0, n = TILES[i]
                    act.wait_ge(turned, n2 + 1)
                    bank = k.ps[:, n2 % 4, :].rearrange("p (j t) -> p j t", j=4)
                    act.activation(k.xT[:, half * 4:half * 4 + 4, t0:t0 + n], bank[:, :, 0:n],
                                   ACT.Copy).then_inc(bank_free, 1)

        @block.tensor
        def _(pe):
            if y is None:
                for n2 in range(6):
                    i, half = divmod(n2, 2)
                    _, n = TILES[i]
                    pe.wait_ge(x_ready, i + 1)
                    wait(pe, bank_free, n2 - 3)
                    for j in range(4):
                        c = half * 4 + j
                        last = pe.transpose(k.ps[:, n2 % 4, j * P:j * P + n], k.x[0:n, i, c * P:(c + 1) * P],
                                            k.ident[0:n, 0:n])
                    last.then_inc(turned, 1)


def attend_prompt(k, name, units, cols, scale, mask_scales, out_n=P):
    nc = k.nc
    with ExitStack() as ctx:
        s = k.sb(ctx, name + "_s", [P, 2, cols])
        p = k.sb(ctx, name + "_p", [P, 2, cols])
        pT = k.sb(ctx, name + "_pT", [P, cols // P, P])
        stat = k.sb(ctx, name + "_stat", [P, 2, 4])
        scored, s_read, max_ready = k.sem(name + "_scored"), k.sem(name + "_s_read"), k.sem(name + "_max")
        exp_done, p_ready, chain = k.sem(name + "_exp"), k.sem(name + "_p_ready"), k.sem(name + "_chain")
        turned, pT_ready = k.sem(name + "_turned"), k.sem(name + "_pT_ready")
        o_ready, o_taken = k.sem(name + "_o_ready"), k.sem(name + "_o_taken")
        block = ctx.enter_context(k.block())
        U = len(units)
        psf = k.ps[:, :, :].rearrange("p b n -> p (b n)")

        def width(u):
            return sum(n for _, n, _ in units[u]["scores"])

        @block.tensor
        def _(pe):
            def scores(u):
                wait(pe, s_read, u - 1)
                for c0, n, prods in units[u]["scores"]:
                    for m, (lhsT, rhs) in enumerate(prods):
                        mm = pe.matmul(psf[:, (u % 2) * 1024 + c0:(u % 2) * 1024 + c0 + n], lhsT, rhs,
                                       start=(m == 0), stop=(m == len(prods) - 1))
                mm.then_inc(scored, 1)

            def values(u):
                pe.wait_ge(p_ready, u + 1)
                wait(pe, pT_ready, u)
                keys = units[u]["keys"]
                for j, (c0, _) in enumerate(keys):
                    mm = pe.transpose(psf[:, 2048 + j * P:2048 + (j + 1) * P], p[:, u % 2, c0:c0 + P], k.ident[:, :])
                mm.then_inc(turned, 1)
                pe.wait_ge(pT_ready, u + 1)
                wait(pe, o_taken, u - 1)
                for b in range(len(units[u]["outs"])):
                    for j, (_, vs) in enumerate(keys):
                        mm = pe.matmul(k.ps[:, 6 + u % 2, b * P:(b + 1) * P], vs[b], pT[:, j, :],
                                       start=(j == 0), stop=(j == len(keys) - 1))
                mm.then_inc(o_ready, 1)

            scores(0)
            for u in range(U):
                if u + 1 < U:
                    scores(u + 1)
                values(u)

        @block.vector
        def _(dve):
            link = Chain(dve, chain)

            def maxima(u):
                w = width(u)
                src, dst = psf[:, (u % 2) * 1024:(u % 2) * 1024 + w], s[:, u % 2, 0:w]
                dve.wait_ge(scored, u + 1)
                wait(dve, exp_done, u - 1)
                dve.scalar_tensor_tensor(out=dst, in0=src, scalar=mask_scales, in1=units[u]["bias"],
                                         op0=ALU.mult, op1=ALU.add).then_inc(s_read, 1) \
                    if units[u]["bias"] is not None else \
                    dve.tensor_copy(dst, src).then_inc(s_read, 1)
                dve.wait_ge(s_read, u + 1)
                link(dve.reduce_max(stat[:, u % 2, 0:1], dst, AX))
                dve.tensor_scalar(out=stat[:, u % 2, 1:2], in0=stat[:, u % 2, 0:1], scalar1=-scale, scalar2=None,
                                  op0=ALU.mult).then_inc(max_ready, 1)

            def finish(u):
                w = width(u)
                dve.wait_ge(exp_done, u + 1)
                link(dve.reciprocal(stat[:, u % 2, 3:4], stat[:, u % 2, 2:3]))
                dve.tensor_scalar(out=p[:, u % 2, 0:w], in0=p[:, u % 2, 0:w], scalar1=stat[:, u % 2, 3:4],
                                  scalar2=None, op0=ALU.mult).then_inc(p_ready, 1)

            def take(u):
                dve.wait_ge(o_ready, u + 1)
                for b, dst in enumerate(units[u]["outs"]):
                    last = dve.tensor_copy(dst, k.ps[:, 6 + u % 2, b * P:(b + 1) * P])
                last.then_inc(o_taken, 1)

            maxima(0)
            for u in range(U):
                finish(u)
                if u + 1 < U:
                    maxima(u + 1)
                take(u)

        @block.scalar
        def _(act):
            def exps(u):
                w = width(u)
                act.wait_ge(max_ready, u + 1)
                wait(act, turned, u - 1)
                act.activation(p[:, u % 2, 0:w], s[:, u % 2, 0:w], ACT.Exp, bias=stat[:, u % 2, 1:2], scale=scale,
                               accum_out=stat[:, u % 2, 2:3]).then_inc(exp_done, 1)

            exps(0)
            for u in range(U):
                if u + 1 < U:
                    exps(u + 1)
                act.wait_ge(turned, u + 1)
                wait(act, o_ready, u)
                nk = len(units[u]["keys"])
                act.activation(pT[:, 0:nk, :].rearrange("p a b -> p (a b)"), psf[:, 2048:2048 + nk * P],
                               ACT.Copy).then_inc(pT_ready, 1)


def attend_sample(k, name, a):
    nc = k.nc
    with ExitStack() as ctx:
        M = a["rows"]
        s = k.sb(ctx, name + "_s", [M, a["cols"]])
        p = k.sb(ctx, name + "_p", [M, a["cols"]])
        keys = a["keys"]
        NK = len(keys)
        pT = k.sb(ctx, name + "_pT", [P, NK, M])
        stat = k.sb(ctx, name + "_stat", [M, 4])
        kv_landed = [k.gathered[f"page_landed{i}"] if a.get("gather") else k.sem(f"{name}_kv_landed{i}") for i in range(2)]
        setup_done, staged = k.sem(name + "_setup"), k.sem(name + "_staged")
        turned, kT_ready = k.sem(name + "_turned"), k.sem(name + "_kT_ready")
        scored, s_taken, max_ready = k.sem(name + "_scored"), k.sem(name + "_s_taken"), k.sem(name + "_max")
        exp_done, p_ready, chain = k.sem(name + "_exp"), k.sem(name + "_p_ready"), k.sem(name + "_chain")
        p_turned, pT_ready = k.sem(name + "_p_turned"), k.sem(name + "_pT_ready")
        o_ready, o_taken = k.sem(name + "_o_ready"), k.sem(name + "_o_taken")
        idx_staged = k.sem(name + "_idx") if a.get("gather") else None
        begun_pool, begun_pe = k.sem(name + "_begun_pool"), k.sem(name + "_begun_pe")
        v_landed = [k.gathered[f"window_v_landed{i}"] if a.get("load_values") else k.sem(f"{name}_v_landed{i}")
                    for i in range(2)] if a.get("values_per_unit") else None
        block = ctx.enter_context(k.block())
        G, C = len(a["groups"]), len(a["chunks"])
        per_bank = 512 // M
        pgroups = [list(range(i, min(i + per_bank, NK))) for i in range(0, NK, per_bank)]
        PG = len(pgroups)
        NS = a["n_stage"]
        PAIRS = DEC_B // 2

        @block.sync
        def _(sp):
            if a.get("setup_loads"):
                a["setup_loads"](sp, setup_done)

            def body(i):
                for slot in range(2):
                    u = 2 * i + slot
                    if a.get("load_values"):
                        wait(sp, turned, G * u)
                    else:
                        wait(sp, o_ready, u - 1)
                    a["load"](sp, u, slot, v_landed[slot] if a.get("gather") else kv_landed[slot])
            repeat(sp, PAIRS, body)

        @block.gpsimd
        def _(pool):
            if a.get("setup_pool"):
                a["setup_pool"](pool, setup_done)

            def body(i):
                for slot in range(2):
                    u = 2 * i + slot
                    if a.get("gather"):
                        wait(pool, o_ready, u - 1)
                        a["gather"](pool, u, slot, kv_landed[slot], idx_staged, begun_pool)
                    wait(pool, scored, C * (u - 1))
                    a["stage"](pool, u, slot, staged)
                    if a.get("load_values"):
                        wait(pool, o_ready, u)
                        a["load_values"](pool, u, slot, v_landed[slot])
            repeat(pool, PAIRS, body)

        @block.tensor
        def _(pe):
            def turn_keys(u, half, slot):
                pe.wait_ge(kv_landed[slot], (half + 1) * a["landed_per_unit"])
                for g, blocks in enumerate(a["groups"]):
                    wait(pe, kT_ready, G * u + g - 1)
                    for j, (src, w) in enumerate(blocks):
                        mm = pe.transpose(k.ps[0:w, g % 2 if G % 2 == 0 else (g + slot) % 2, j * P:(j + 1) * P],
                                          src(slot), k.ident[:, :])
                    mm.then_inc(turned, 1)

            def body(i, last):
                for slot in range(2):
                    u = 2 * i + slot
                    pe.wait_ge(kT_ready, G * (u + 1))
                    pe.wait_ge(staged, NS * (u + 1))
                    if a["setup_count"]:
                        pe.wait_ge(setup_done, a["setup_count"])
                    for c, (c0, n, prods) in enumerate(a["chunks"]):
                        wait(pe, s_taken, C * u + c - 1)
                        bank = 2 + (c % 2 if C % 2 == 0 else (c + slot) % 2)
                        for m0, m, terms in prods:
                            for j, (lhsT, rhs) in enumerate(terms):
                                off, nn, l, r = 0, n, lhsT(slot), rhs(slot)
                                mm = pe.matmul(k.ps[m0:m0 + m, bank, 0:n], l, r, start=(j == 0),
                                               stop=(j == len(terms) - 1))
                        mm.then_inc(scored, 1)
                    if not (last and slot == 1):
                        turn_keys(u + 1, i + slot, 1 - slot)
                    wait_apart(pe, p_ready, u + 1, begun_pe)
                    for g, ks in enumerate(pgroups):
                        wait_apart(pe, pT_ready, PG * u + g - 1, begun_pe)
                        bank = 4 + (g % 2 if PG % 2 == 0 else (g + slot) % 2)
                        for j, kk in enumerate(ks):
                            c0, n, _ = keys[kk]
                            mm = pe.transpose(k.ps[0:n, bank, j * M:(j + 1) * M], p[:, c0:c0 + n], k.ident[0:M, 0:M])
                        mm.then_inc(p_turned, 1)
                    pe.wait_ge(pT_ready, PG * (u + 1))
                    wait(pe, o_taken, u - 1)
                    if a.get("values_per_unit"):
                        pe.wait_ge(v_landed[slot], (i + 1) * a["values_per_unit"])
                    for o0, n, col, pc in a["vblocks"]:
                        for kk, (_, rows, v) in enumerate(keys):
                            mm = pe.matmul(k.ps[:, 6 + slot, o0:o0 + n], v(slot, col), pT[0:rows, kk, pc:pc + n],
                                           start=(kk == 0), stop=(kk == NK - 1))
                    mm.then_inc(o_ready, 1)

            turn_keys(0, 0, 0)
            repeat_ends(pe, PAIRS, body)

        @block.scalar
        def _(act):
            def take_keys(u, slot, g):
                act.wait_ge(turned, G * u + g + 1)
                bank = g % 2 if G % 2 == 0 else (g + slot) % 2
                for n, (dst, src) in enumerate(a["key_copies"](g, k.ps[:, bank, :])):
                    last = act.activation(dst, src, ACT.Copy)
                last.then_inc(kT_ready, 1)

            def body(i, last):
                for slot in range(2):
                    u = 2 * i + slot
                    more = not (last and slot == 1)
                    if more:
                        act.wait_ge(scored, C * (u + 1))
                        for g in range(0, (G + 1) // 2):
                            take_keys(u + 1, 1 - slot, g)
                    act.wait_ge(max_ready, u + 1)
                    wait(act, p_turned, PG * u)
                    act.activation(p[:, :], s[:, :], ACT.Exp, bias=stat[:, 1:2], scale=a["scale"],
                                   accum_out=stat[:, 2:3]).then_inc(exp_done, 1)
                    if more:
                        for g in range((G + 1) // 2, G):
                            take_keys(u + 1, 1 - slot, g)
                    wait(act, o_ready, u)
                    for g, ks in enumerate(pgroups):
                        act.wait_ge(p_turned, PG * u + g + 1)
                        bank = 4 + (g % 2 if PG % 2 == 0 else (g + slot) % 2)
                        full = [kk for kk in ks if keys[kk][1] == P]
                        if full:
                            nf = len(full)
                            src = k.ps[:, bank, 0:nf * M].rearrange("p (a b) -> p a b", a=nf)
                            ins = act.activation(pT[:, full[0]:full[0] + nf, :], src, ACT.Copy)
                        if len(full) < len(ks):
                            j, nr = len(full), len(ks) - len(full)
                            rows = keys[ks[j]][1]
                            src = k.ps[0:rows, bank, j * M:(j + nr) * M].rearrange("p (a b) -> p a b", a=nr)
                            ins = act.activation(pT[0:rows, ks[j]:ks[j] + nr, :], src, ACT.Copy)
                        ins.then_inc(pT_ready, 1)

            for g in range(G):
                take_keys(0, 0, g)
            repeat_ends(act, PAIRS, body)

        @block.vector
        def _(dve):
            if a["setup_count"]:
                dve.wait_ge(setup_done, a["setup_count"])

            def body(i):
                for slot in range(2):
                    u = 2 * i + slot
                    wait(dve, exp_done, u)
                    for c, (c0, n, _) in enumerate(a["chunks"]):
                        dve.wait_ge(scored, C * u + c + 1)
                        bank = 2 + (c % 2 if C % 2 == 0 else (c + slot) % 2)
                        dst, src = s[:, c0:c0 + n], k.ps[0:M, bank, 0:n]
                        bias = a["bias"](c0, n)
                        if bias is None:
                            dve.tensor_copy(dst, src).then_inc(s_taken, 1)
                        else:
                            dve.scalar_tensor_tensor(out=dst, in0=src, scalar=a["bias_scale"], in1=bias,
                                                     op0=ALU.mult, op1=ALU.add).then_inc(s_taken, 1)
                    dve.wait_ge(s_taken, C * (u + 1))
                    link = Chain(dve, chain, 2 * u)
                    link(dve.reduce_max(stat[:, 0:1], s[:, :], AX))
                    dve.tensor_scalar(out=stat[:, 1:2], in0=stat[:, 0:1], scalar1=-a["scale"], scalar2=None,
                                      op0=ALU.mult).then_inc(max_ready, 1)
                    dve.wait_ge(exp_done, u + 1)
                    link(dve.reciprocal(stat[:, 3:4], stat[:, 2:3]))
                    dve.tensor_scalar(out=p[:, :], in0=p[:, :], scalar1=stat[:, 3:4], scalar2=None,
                                      op0=ALU.mult).then_inc(p_ready, 1)
                    dve.wait_ge(o_ready, u + 1)
                    dst, src = a["out"](u, k.ps[:, 6 + slot, :])
                    dve.tensor_copy(dst, src).then_inc(o_taken, 1)
            repeat(dve, PAIRS, body)


def latent_stage(k, e):
    nc, io = k.nc, k.io
    with ExitStack() as ctx:
        lat = e["latent"]
        gq, gkv = k.sb(ctx, "lt_gq", [P, Q_LORA]), k.sb(ctx, "lt_gkv", [P, KV_LORA])
        cs = k.sb(ctx, "lt_cs", [P, 3, 2, 16])
        sq = k.sb(ctx, "lt_sq", [P, 256])
        ms = k.sb(ctx, "lt_ms", [P, 3, 2])
        cq = k.sb(ctx, "lt_cq", [P, 3, Q_LORA])
        rot = k.sb(ctx, "lt_rot", [P, 3, 4, 16])
        landed, squares, chain = k.sem("lt_landed"), k.sem("lt_squares"), k.sem("lt_chain")
        ms_ready, root_ready, rows_ready = k.sem("lt_ms_ready"), k.sem("lt_root"), k.sem("lt_rows")
        turned, bank_free, stored = k.sem("lt_turned"), k.sem("lt_free"), k.sem("lt_stored")
        block = ctx.enter_context(k.block())
        rows = e["rows"]

        @block.sync
        def _(sp):
            for dst, src in ((gq, io["mla_q_norm"]), (gkv, io["mla_kv_norm"])):
                sp.dma_start(dst[:, :], bass.AP(src.tensor, src.offset, [[0, P], [1, 256]])).then_inc(landed, 16)
            sp.dma_start(cs[:, 0:2, :, :], io["rope_tok"][0:SEQ].rearrange("(i p) a c -> p i a c", p=P)).then_inc(landed, 16)
            sp.dma_start(cs[0:64, 2, :, :], io["rope_tok"][SEQ:T]).then_inc(landed, 16)
            sp.wait_ge(rows_ready, 3)
            sp.dma_start(io["mla_rows_prompt"][0, 0].rearrange("(i p) c -> p i c", p=P), rows[:, 0:2, :]).then_inc(stored, 16)
            sp.dma_start(io["mla_rows_sample"][0].rearrange("b s c -> (b s) c"), rows[0:64, 2, :]).then_inc(stored, 16)
            sp.wait_ge(stored, 32)

        @block.scalar
        def _(act):
            n2 = 0
            for i, (_, n) in enumerate(TILES):
                for j in range(2):
                    wait(act, squares, n2)
                    act.activation(sq[0:n, :], lat[0:n, i, j * 256:(j + 1) * 256], ACT.Square,
                                   accum_out=ms[0:n, i, j:j + 1]).then_inc(squares, 1)
                    n2 += 1
            act.wait_ge(ms_ready, 3)
            for i, (_, n) in enumerate(TILES):
                act.activation(ms[0:n, i, :], ms[0:n, i, :], ACT.Sqrt).then_inc(root_ready, 1)
            for i, (t0, n) in enumerate(TILES):
                act.wait_ge(turned, 2 * i + 1)
                act.activation(e["cqT"][:, :, t0:t0 + n],
                               k.ps[:, 0, 0:256].rearrange("p (a t) -> p a t", a=2)[:, :, 0:n], ACT.Copy).then_inc(bank_free, 1)
                act.wait_ge(turned, 2 * i + 2)
                act.activation(e["ckvT"][:, :, t0:t0 + n],
                               k.ps[:, 1, 0:256].rearrange("p (a t) -> p a t", a=2)[:, :, 0:n], ACT.Copy).then_inc(bank_free, 1)
                act.activation(e["krT"][:, t0:t0 + n], k.ps[0:ROPE, 1, 256:256 + n], ACT.Copy).then_inc(bank_free, 1)

        @block.vector
        def _(dve):
            dve.wait_ge(squares, 6)
            for i, (_, n) in enumerate(TILES):
                dve.tensor_scalar(out=ms[0:n, i, :], in0=ms[0:n, i, :], scalar1=1.0 / 256, scalar2=EPS,
                                  op0=ALU.mult, op1=ALU.add).then_inc(ms_ready, 1)
            dve.wait_ge(landed, 64)
            link = Chain(dve, chain)
            for i, (_, n) in enumerate(TILES):
                dve.wait_ge(root_ready, i + 1)
                link(dve.reciprocal(ms[0:n, i, :], ms[0:n, i, :]))
                dve.scalar_tensor_tensor(out=cq[0:n, i, :], in0=lat[0:n, i, 0:256], scalar=ms[0:n, i, 0:1],
                                         in1=gq[0:n, :], op0=ALU.mult, op1=ALU.mult)
                dve.scalar_tensor_tensor(out=rows[0:n, i, 0:256], in0=lat[0:n, i, 256:512], scalar=ms[0:n, i, 1:2],
                                         in1=gkv[0:n, :], op0=ALU.mult, op1=ALU.mult)
                x1, x2 = lat[0:n, i, 512:528], lat[0:n, i, 528:544]
                cos, sin = cs[0:n, i, 0, :], cs[0:n, i, 1, :]
                dve.tensor_tensor(out=rot[0:n, i, 0, :], in0=x1, in1=cos, op=ALU.mult)
                dve.tensor_tensor(out=rot[0:n, i, 1, :], in0=x2, in1=sin, op=ALU.mult)
                dve.tensor_tensor(out=rot[0:n, i, 2, :], in0=x2, in1=cos, op=ALU.mult)
                link(dve.tensor_tensor(out=rot[0:n, i, 3, :], in0=x1, in1=sin, op=ALU.mult))
                dve.tensor_tensor(out=rows[0:n, i, 256:272], in0=rot[0:n, i, 0, :], in1=rot[0:n, i, 1, :], op=ALU.subtract)
                dve.tensor_tensor(out=rows[0:n, i, 272:288], in0=rot[0:n, i, 2, :], in1=rot[0:n, i, 3, :],
                                  op=ALU.add).then_inc(rows_ready, 1)

        @block.tensor
        def _(pe):
            for i, (_, n) in enumerate(TILES):
                pe.wait_ge(rows_ready, i + 1)
                wait(pe, bank_free, 3 * i)
                for j in range(2):
                    mm = pe.transpose(k.ps[:, 0, j * P:j * P + n], cq[0:n, i, j * P:(j + 1) * P], k.ident[0:n, 0:n])
                mm.then_inc(turned, 1)
                for j in range(2):
                    pe.transpose(k.ps[:, 1, j * P:j * P + n], rows[0:n, i, j * P:(j + 1) * P], k.ident[0:n, 0:n])
                pe.transpose(k.ps[0:ROPE, 1, 256:256 + n], rows[0:n, i, 256:288], k.ident[0:n, 0:n]).then_inc(turned, 1)


def window_outputs_stage(k, kv):
    nc, io = k.nc, k.io
    with ExitStack() as ctx:
        stored = k.sem("wo_stored")
        block = ctx.enter_context(k.block())

        @block.sync
        def _(sp):
            n = 0
            sp.dma_start(io["kv_new"], kv[0:64, 2, :]).then_inc(stored, 16)
            n += 1
            for g, (w, _) in enumerate(SWA_GROUPS):
                for c in range(2):
                    cols = slice((c * 3 + g) * GW, (c * 3 + g + 1) * GW)
                    dst = io[f"swa_prompt{g}"][0, 0, :, c].rearrange("w h d -> w (h d)")
                    for i in range(2):
                        r = w - SEQ + i * P
                        if r >= 0:
                            sp.dma_start(dst[r:r + P, :], kv[:, i, cols]).then_inc(stored, 16)
                            n += 1
                    for b in range(DEC_B):
                        dst_s = io[f"swa_sample{g}"][0, b, w - DEC_S:w, c].rearrange("w h d -> w (h d)")
                        sp.dma_start(dst_s, kv[8 * b:8 * b + 8, 2, cols]).then_inc(stored, 16)
                        n += 1
            sp.wait_ge(stored, 16 * n)


def query_stage(k, e):
    nc, io = k.nc, k.io
    with ExitStack() as ctx:
        wuq = k.sb(ctx, "qs_wuq", [P, 2, MLA_H * (NOPE + ROPE)])
        wsw = k.sb(ctx, "qs_wsw", [P, 2, MLA_H, ROPE])
        wuk = k.sb(ctx, "qs_wuk", [P, 2, MLA_H * NOPE])
        wukT = k.sb(ctx, "qs_wukT", [P, 4, KV_LORA])
        nopeT = k.sb(ctx, "qs_nopeT", [P, 4, T])
        csT = k.sb(ctx, "qs_csT", [ROPE, 2, T])
        rot = k.sb(ctx, "qs_rot", [ROPE, 2, T])
        landed, turned, uk_ready = k.sem("qs_landed"), k.sem("qs_turned"), k.sem("qs_uk")
        made, taken = k.sem("qs_made"), k.sem("qs_taken")
        rmade, rchain, rtaken = k.sem("qs_rope_made"), k.sem("qs_rope_chain"), k.sem("qs_rope_taken")
        lmade, ltaken = k.sem("qs_lat_made"), k.sem("qs_lat_taken")
        block = ctx.enter_context(k.block())
        cqT = e["cqT"]
        uq = io["mla_w_uq"][0].rearrange("(c p) (h n) -> p c h n", p=P, h=MLA_H)

        @block.sync
        def _(sp):
            sp.dma_start(wuk[:, :, :], io["mla_w_uk"][0].rearrange("(c p) h n -> p c (h n)", p=P)).then_inc(landed, 16)
            sp.dma_start(wuq[:, :, :], io["mla_w_uq"][0].rearrange("(c p) n -> p c n", p=P)).then_inc(landed, 16)
            for c in range(2):
                sp.dma_start(wsw[:, c, :, 0:16], uq[:, c, :, NOPE + 16:NOPE + 32]).then_inc(landed, 16)
                sp.dma_start(wsw[:, c, :, 16:32], uq[:, c, :, NOPE:NOPE + 16]).then_inc(landed, 16)
            sp.dma_start(csT[:, :, :], io["rope_feat"]).then_inc(landed, 16)

        wq4 = wuq[:, :, :].rearrange("p c (h n) -> p c h n", h=MLA_H)

        @block.tensor
        def _(pe):
            pe.wait_ge(landed, 16 * 7)
            for pair in range(4):
                wait(pe, uk_ready, pair - 1)
                for c in range(2):
                    mm = pe.transpose(k.ps[:, pair % 2, c * P:(c + 1) * P], wuk[:, c, pair * P:(pair + 1) * P], k.ident[:, :])
                mm.then_inc(turned, 1)
            for pair in range(4):
                wait(pe, taken, pair - 1)
                for half in range(2):
                    for c in range(2):
                        mm = pe.matmul(k.ps[64 * half:64 * half + 64, 2 + pair % 2, 0:T],
                                       wq4[:, c, 2 * pair + half, 0:NOPE], cqT[:, c, :], start=(c == 0), stop=(c == 1))
                mm.then_inc(made, 1)
            for h in range(MLA_H):
                wait(pe, rtaken, h - 1)
                for v in range(2):
                    for c in range(2):
                        lhsT = wq4[:, c, h, NOPE:NOPE + ROPE] if v == 0 else wsw[:, c, h, :]
                        mm = pe.matmul(k.ps[0:ROPE, 4 + 2 * (h % 2) + v, 0:T], lhsT, cqT[:, c, :],
                                       start=(c == 0), stop=(c == 1))
                mm.then_inc(rmade, 1)
            pe.wait_ge(taken, 4)
            pe.wait_ge(uk_ready, 4)
            for h in range(MLA_H):
                rows = slice(64 * (h % 2), 64 * (h % 2) + 64)
                for c in range(2):
                    n = 2 * h + c
                    wait(pe, ltaken, n - 1)
                    pe.matmul(k.ps[:, n % 2, 0:T], wukT[rows, h // 2, c * P:(c + 1) * P], nopeT[rows, h // 2, :],
                              start=True, stop=True).then_inc(lmade, 1)

        @block.scalar
        def _(act):
            for pair in range(4):
                act.wait_ge(turned, pair + 1)
                act.activation(wukT[:, pair, :], k.ps[:, pair % 2, 0:256], ACT.Copy).then_inc(uk_ready, 1)
            for pair in range(4):
                act.wait_ge(made, pair + 1)
                act.activation(nopeT[:, pair, :], k.ps[:, 2 + pair % 2, 0:T], ACT.Copy).then_inc(taken, 1)
            for n in range(2 * MLA_H):
                h, c = divmod(n, 2)
                act.wait_ge(lmade, n + 1)
                act.activation(e["qlatT"][:, c, h, :], k.ps[:, n % 2, 0:T], ACT.Copy).then_inc(ltaken, 1)

        @block.vector
        def _(dve):
            dve.wait_ge(landed, 16 * 7)
            for h in range(MLA_H):
                dve.wait_ge(rmade, h + 1)
                wait(dve, rtaken, h)
                for v in range(2):
                    last = dve.tensor_tensor(out=rot[:, v, :], in0=k.ps[0:ROPE, 4 + 2 * (h % 2) + v, 0:T],
                                             in1=csT[:, v, :], op=ALU.mult)
                last.then_inc(rchain, 1)
                dve.wait_ge(rchain, h + 1)
                dve.tensor_tensor(out=e["qrT"][:, h, :], in0=rot[:, 0, :], in1=rot[:, 1, :],
                                  op=ALU.add).then_inc(rtaken, 1)


def mla_values_stage(k, e):
    nc, io = k.nc, k.io
    with ExitStack() as ctx:
        wuv = k.sb(ctx, "mv_wuv", [P, 2, MLA_H, D_V])
        landed, made, taken = k.sem("mv_landed"), k.sem("mv_made"), k.sem("mv_taken")
        block = ctx.enter_context(k.block())

        @block.sync
        def _(sp):
            sp.dma_start(wuv[:, :, :, :], io["mla_w_uv"][0].rearrange("(c p) h n -> p c h n", p=P)).then_inc(landed, 16)

        @block.tensor
        def _(pe):
            pe.wait_ge(landed, 16)
            for pair in range(4):
                for half in range(2):
                    for c in range(2):
                        mm = pe.matmul(k.ps[64 * half:64 * half + 64, pair, 0:T], wuv[:, c, 2 * pair + half, :],
                                       e["olatT"][:, c, 2 * pair + half, :], start=(c == 0), stop=(c == 1))
                mm.then_inc(made, 1)

        @block.scalar
        def _(act):
            for pair in range(4):
                act.wait_ge(made, pair + 1)
                act.activation(e["oT"][:, pair, :], k.ps[:, pair, 0:T], ACT.Copy).then_inc(taken, 1)


def bias_stage(k, e):
    nc, io = k.nc, k.io
    with ExitStack() as ctx:
        hot = k.sb(ctx, "bs_hot", [N_BUCKETS + 1, 3, N_DIST])
        rel = k.sb(ctx, "bs_rel", [N_BUCKETS + 1, 12])
        byd = k.sb(ctx, "bs_by_dist", [SWA_H, 3, N_DIST])
        filled, landed, made, taken = k.sem("bs_filled"), k.sem("bs_landed"), k.sem("bs_made"), k.sem("bs_taken")
        stored, spread, zeroed, tabled = k.sem("bs_stored"), k.sem("bs_spread"), k.sem("bs_zeroed"), k.sem("bs_tabled")
        block = ctx.enter_context(k.block())
        chunks = [(c, min(512, N_DIST - c)) for c in range(0, N_DIST, 512)]
        by_dist, rep = io["bias_by_dist"], io["bias_rep"]
        Bp, Bs = e["bias_p"], e["bias_s"]

        @block.gpsimd
        def _(pool):
            pool.memset(rel[:, :], DISALLOWED).then_inc(filled, 1)
            pool.memset(Bs[:, :], 0.0).then_inc(zeroed, 1)

        @block.sync
        def _(sp):
            sp.dma_start(hot[:, :, :], io["bucket_hot"]).then_inc(landed, 16)
            sp.wait_ge(filled, 1)
            sp.dma_start(rel[0:N_BUCKETS, :], io["rel_bias"]).then_inc(landed, 16)
            sp.wait_ge(taken, 3 * len(chunks))
            sp.dma_start(by_dist.rearrange("g h n -> h g n"), byd[:, :, :]).then_inc(stored, 16)
            sp.wait_ge(stored, 16)
            for g in range(3):
                src = bass.AP(by_dist.tensor, g * SWA_H * N_DIST + REP0, [[N_DIST, SWA_H], [0, P], [1, REP_N]])
                sp.dma_start(rep[g], src).then_inc(spread, 16)
            sp.wait_ge(zeroed, 1)
            for q in range(DEC_S):
                new = bass.AP(by_dist.tensor, DIST_TOP - q, [[N_DIST, SWA_H], [SWA_H * N_DIST, 3], [1, DEC_S]])
                sp.dma_start(Bs[q:P:PAD, SWA_CACHED:SWA_KEYS].rearrange("p (g i) -> p g i", g=3), new).then_inc(tabled, 16)
                for g, (w, _) in enumerate(SWA_GROUPS):
                    base = g * SWA_H * N_DIST + DIST_TOP - w - q
                    if g < 2:
                        src = bass.AP(by_dist.tensor, base, [[N_DIST, SWA_H], [1, w]])
                        dst = Bs[q:P:PAD, g * P:g * P + w]
                    else:
                        src = bass.AP(by_dist.tensor, base, [[N_DIST, SWA_H], [16, P], [1, 8]])
                        dst = Bs[q:P:PAD, 5 * P:SWA_CACHED].rearrange("p (a i) -> p a i", i=8)
                    sp.dma_start(dst, src).then_inc(tabled, 16)
            sp.wait_ge(spread, 48)
            for g in range(3):
                for h in range(SWA_H):
                    for qb in range(2):
                        src = bass.AP(rep.tensor, (g * SWA_H + h) * P * REP_N + (DIST_TOP - REP0) - qb * P,
                                      [[REP_N - 1, P], [1, SEQ]])
                        sp.dma_start(Bp[:, h, qb, g, :], src).then_inc(tabled, 16)
            sp.wait_ge(tabled, 16 * (4 * DEC_S + 24))

        @block.tensor
        def _(pe):
            pe.wait_ge(landed, 32)
            n = 0
            for g in range(3):
                for c0, w in chunks:
                    wait(pe, taken, n - 3)
                    pe.matmul(k.ps[0:SWA_H, n % 4, 0:w], rel[:, 4 * g:4 * g + 4], hot[:, g, c0:c0 + w],
                              start=True, stop=True).then_inc(made, 1)
                    n += 1

        @block.scalar
        def _(act):
            n = 0
            for g in range(3):
                for c0, w in chunks:
                    act.wait_ge(made, n + 1)
                    act.activation(byd[:, g, c0:c0 + w], k.ps[0:SWA_H, n % 4, 0:w], ACT.Copy).then_inc(taken, 1)
                    n += 1


def turn_stage(k, name, jobs):
    nc = k.nc
    with ExitStack() as ctx:
        turned, taken = k.sem(name + "_turned"), k.sem(name + "_taken")
        block = ctx.enter_context(k.block())

        @block.tensor
        def _(pe):
            for n, (srcs, rows, dst) in enumerate(jobs):
                wait(pe, taken, n - 3)
                for j, src in enumerate(srcs):
                    mm = pe.transpose(k.ps[0:src.shape[1], n % 4, j * P:j * P + rows], src, k.ident[0:rows, 0:rows])
                mm.then_inc(turned, 1)

        @block.scalar
        def _(act):
            for n, (srcs, rows, dst) in enumerate(jobs):
                act.wait_ge(turned, n + 1)
                src = k.ps[0:srcs[0].shape[1], n % 4, :].rearrange("p (j t) -> p j t", j=4)[:, 0:len(srcs), 0:rows]
                act.activation(dst, src, ACT.Copy).then_inc(taken, 1)


def even_mixer(k):
    nc, io = k.nc, k.io
    w_in = io["attn_w_in"][0]
    first = Q_LORA + KV_LORA + ROPE
    with ExitStack() as ctx:
        e = {}
        e["oT"] = k.sb(ctx, "e_oT", [P, 8, T])
        with ExitStack() as c1:
            rows = e["rows"] = k.sb(c1, "e_rows", [P, 3, MLA_ROW])
            e["ckvT"] = k.sb(c1, "e_ckvT", [P, 2, T])
            e["krT"] = k.sb(c1, "e_krT", [ROPE, T])
            e["qlatT"] = k.sb(c1, "e_qlatT", [P, 2, MLA_H, T])
            e["qrT"] = k.sb(c1, "e_qrT", [ROPE, MLA_H, T])
            e["olatT"] = k.sb(c1, "e_olatT", [P, 2, MLA_H, T])
            with ExitStack() as c2:
                e["cqT"] = k.sb(c2, "e_cqT", [P, 2, T])
                e["latent"] = k.sb(c2, "e_latent", [P, 3, first])
                gemm_stage(k, "lat", [("tok", k.xT, w_in[:, 0:first], 272, e["latent"])])
                latent_stage(k, e)
                query_stage(k, e)
            with ExitStack() as c2:
                mask = k.sb(c2, "e_causal", [P, 2, SEQ])
                mla_prompt(k, e, mask)
            mla_sample(k, e)
            mla_values_stage(k, e)
        with ExitStack() as c1:
            swa_qT = k.sb(c1, "e_swa_qT", [P, 12, T])
            kT = k.sb(c1, "e_kT", [P, 12, T])
            e["bias_s"] = k.sb(c1, "e_bias_s", [P, SWA_KEYS])
            with ExitStack() as c2:
                kv = k.sb(c2, "e_kv", [P, 3, 6 * GW])
                gemm_stage(k, "win", [
                    ("tok", k.xT, w_in[:, first + 3 * GW:first + 9 * GW], 512, kv),
                    ("feat", k.xT, w_in[:, first:first + 3 * GW], 384, swa_qT[:, :, :].rearrange("p a t -> p (a t)")),
                ])
                window_outputs_stage(k, kv)
                turn_stage(k, "kturn", [
                    ([kv[0:n, i, g * GW + h * P:g * GW + (h + 1) * P] for h in range(SWA_H)], n,
                     kT[:, 4 * g:4 * g + 4, t0:t0 + n]) for g in range(3) for i, (t0, n) in enumerate(TILES)])
                Bp = e["bias_p"] = k.sb(c2, "e_bias_p", [P, SWA_H, 2, 3, SEQ])
                bias_stage(k, e)
                units = []
                for qb in range(2):
                    n = (qb + 1) * P
                    for h in range(SWA_H):
                        scores, keys = [], []
                        for g in range(3):
                            q = swa_qT[:, 4 * g + h, qb * P:(qb + 1) * P]
                            for kb in range(qb + 1):
                                c0 = g * n + kb * P
                                scores.append((c0, P, [(q, kT[:, 4 * g + h, kb * P:(kb + 1) * P])]))
                                v0 = (3 + g) * GW + h * P
                                keys.append((c0, [kv[:, kb, v0:v0 + P]]))
                        units.append({"scores": scores, "keys": keys, "bias": Bp[:, h, qb, :, 0:n],
                                      "outs": [e["oT"][:, 4 + h, qb * P:(qb + 1) * P]]})
                attend_prompt(k, "swp", units, 3 * SEQ, 1.0, SWA_SCALE)
            swa_sample(k, e, swa_qT, kT)
        gemm_stage(k, "aout", [("tok", e["oT"], io["attn_w_out"][0], 512, k.h)])


def mla_prompt(k, e, mask):
    nc, io = k.nc, k.io
    with ExitStack() as ctx:
        landed = k.sem("mp_mask_landed")
        block = ctx.enter_context(k.block())

        @block.sync
        def _(sp):
            sp.dma_start(mask[:, :, :], io["causal"]).then_inc(landed, 16)
            sp.wait_ge(landed, 16)
    units = []
    for qb in range(2):
        n = (qb + 1) * P
        qs = slice(qb * P, (qb + 1) * P)
        for h in range(MLA_H):
            prods = [(e["qlatT"][:, c, h, qs], e["ckvT"][:, c, 0:n]) for c in range(2)]
            prods.append((e["qrT"][:, h, qs], e["krT"][:, 0:n]))
            units.append({"scores": [(0, n, prods)], "bias": mask[:, qb, 0:n],
                          "keys": [(kb * P, [e["rows"][:, kb, c * P:(c + 1) * P] for c in range(2)])
                                   for kb in range(qb + 1)],
                          "outs": [e["olatT"][:, c, h, qs] for c in range(2)]})
    attend_prompt(k, "mlp", units, SEQ, MLA_SCALE, 1.0)


def mla_sample(k, e):
    nc, io = k.nc, k.io
    with ExitStack() as ctx:
        pages = k.sb(ctx, "ms_pages", [P, 2, N_PAGES, MLA_ROW])
        rnew = k.sb(ctx, "ms_rows_new", [DEC_S, 2, MLA_ROW])
        KT = k.sb(ctx, "ms_kT", [P, 2, PAST])
        KR = k.sb(ctx, "ms_krT", [ROPE, PAST])
        qst = k.sb(ctx, "ms_q", [P, 2, 2, MLA_H, DEC_S])
        qrst = k.sb(ctx, "ms_qr", [ROPE, 2, MLA_H, DEC_S])
        knew = k.sb(ctx, "ms_knew", [P, 2, 2, DEC_S])
        krnew = k.sb(ctx, "ms_krnew", [ROPE, 2, DEC_S])
        mask = k.sb(ctx, "ms_mask", [64, DEC_S])
        table = k.sb(ctx, "ms_table", [P, DEC_B * N_PAGES], I32)
        row = k.sb(ctx, "ms_row", [P, DEC_B * N_PAGES], I32)
        lane = k.sb(ctx, "ms_lane", [P, 1], I32)
        ist = k.sb(ctx, "ms_idx", [P, 2, N_PAGES], I32)
        cols = PAST + DEC_S
        table_landed, made = k.sem("ms_table_landed"), k.sem("ms_table_made")
        with ExitStack() as c2:
            block = c2.enter_context(k.block())

            @block.sync
            def _(sp):
                src = io["page_table"]
                sp.dma_start(table[:, :], bass.AP(src.tensor, 0, [[0, P], [1, DEC_B * N_PAGES]])).then_inc(table_landed, 16)
                sp.dma_start(mask[:, :], io["causal_new"]).then_inc(table_landed, 16)
                sp.wait_ge(table_landed, 32)

            @block.gpsimd
            def _(pool):
                pool.iota(lane[:, :], [[0, 1]], base=0, channel_multiplier=1).then_inc(made, 1)

            @block.vector
            def _(dve):
                dve.wait_ge(table_landed, 32)
                dve.wait_ge(made, 1)
                dve.tensor_scalar(out=row[:, :], in0=table[:, :], scalar1=float(PAGE), scalar2=None,
                                  op0=ALU.mult).then_inc(made, 1)
                dve.wait_ge(made, 2)
                dve.tensor_tensor(out=row[:, :], in0=row[:, :], in1=lane[:, 0:1].to_broadcast([P, DEC_B * N_PAGES]),
                                  op=ALU.add).then_inc(made, 1)

        pool_rows = io["cache_mla"].rearrange("e a p c -> (e a p) c")

        def gather(pool, u, slot, landed, idx_staged, begun):
            pool.tensor_copy(ist[:, slot, :], row[:, ds(u * N_PAGES, N_PAGES)]).then_inc(idx_staged, 1)
            wait_apart(pool, idx_staged, u + 1, begun)
            for j in range(N_PAGES):
                pool.indirect_dma_start(
                    out=pages[:, slot, j, :], out_offset=None, in_=pool_rows,
                    in_offset=bass.IndirectOffsetOnAxis(ap=ist[:, slot, j:j + 1], axis=0)).then_inc(landed, 16)

        def load(sp, u, slot, landed):
            sp.dma_start(rnew[:, slot, :], io["mla_rows_sample"][0, ds(u, 1)].rearrange("b s c -> (b s) c")).then_inc(landed, 16)

        def stage(pool, u, slot, staged):
            t = ds(SEQ + DEC_S * u, DEC_S)
            pool.tensor_copy(qst[:, slot, :, :, :], e["qlatT"][:, :, :, t]).then_inc(staged, 1)
            pool.tensor_copy(qrst[:, slot, :, :], e["qrT"][:, :, t]).then_inc(staged, 1)
            pool.tensor_copy(knew[:, slot, :, :], e["ckvT"][:, :, t]).then_inc(staged, 1)
            pool.tensor_copy(krnew[:, slot, :], e["krT"][:, t]).then_inc(staged, 1)

        def q(c):
            return lambda slot: qst[:, slot, c, :, :].rearrange("p h s -> p (h s)")

        def qr(slot):
            return qrst[:, slot, :, :].rearrange("p h s -> p (h s)")

        def cached(c, c0):
            return lambda slot: KT[:, c, c0:c0 + 512]

        chunks = [(c0, 512, [(0, 64, [(q(0), cached(0, c0)), (q(1), cached(1, c0)),
                                      (qr, lambda slot, c0=c0: KR[:, c0:c0 + 512])])]) for c0 in range(0, PAST, 512)]
        chunks.append((PAST, DEC_S, [(0, 64, [(q(0), lambda slot: knew[:, slot, 0, :]),
                                              (q(1), lambda slot: knew[:, slot, 1, :]),
                                              (qr, lambda slot: krnew[:, slot, :])])]))

        def page_block(j, c0, w):
            return lambda slot: pages[:, slot, j, c0:c0 + w]

        def key_copies(g, bank):
            yield KT[:, :, g * P:(g + 1) * P], bank[:, 0:2 * P].rearrange("p (a b) -> p a b", a=2)
            yield KR[:, g * P:(g + 1) * P], bank[0:ROPE, 2 * P:3 * P]

        attend_sample(k, "mls", {
            "rows": 64, "cols": cols, "scale": MLA_SCALE, "bias_scale": 1.0,
            "bias": lambda c0, n: mask[:, :] if c0 == PAST else None,
            "groups": [[(page_block(j, 0, P), P), (page_block(j, P, P), P), (page_block(j, 2 * P, ROPE), ROPE)]
                       for j in range(N_PAGES)],
            "key_copies": key_copies, "chunks": chunks,
            "keys": [(j * P, P, lambda slot, c, j=j: pages[:, slot, j, c * P:(c + 1) * P]) for j in range(N_PAGES)]
            + [(PAST, DEC_S, lambda slot, c: rnew[:, slot, c * P:(c + 1) * P])],
            "vblocks": [(c * 64, 64, c, 0) for c in range(2)],
            "load": load, "gather": gather, "stage": stage, "n_stage": 4, "landed_per_unit": 16 * N_PAGES, "values_per_unit": 16,
            "setup_count": 0,
            "out": lambda u, bank: (e["olatT"][:, :, :, ds(SEQ + DEC_S * u, DEC_S)],
                                    bank[:, 0:128].rearrange("p (c h s) -> p c h s", c=2, h=MLA_H)),
        })


def swa_sample(k, e, swa_qT, kT):
    nc, io = k.nc, k.io
    with ExitStack() as ctx:
        kcache = k.sb(ctx, "ss_kcache", [P, len(SWA_TILES), GW])
        vcache = k.sb(ctx, "ss_vcache", [P, len(SWA_TILES), GW])
        vnew = k.sb(ctx, "ss_vnew", [DEC_S, 3 * GW])
        KT = k.sb(ctx, "ss_kT", [P, SWA_H, SWA_CACHED])
        qst = k.sb(ctx, "ss_q", [P, 2, 12, PAD])
        knew = k.sb(ctx, "ss_knew", [P, 2, 12, DEC_S])

        def setup_pool(pool, done):
            pool.memset(qst[:, :, :, :], 0.0).then_inc(done, 1)
            pool.wait_ge(done, 1)

        def windows(eng, u, part, dst, landed):
            c = [io[n][0, ds(u, 1), :, part].rearrange("b w h d -> (b w) (h d)") for n in
                 ("cache_swa_w128", "cache_swa_w512", "cache_swa_w2048")]
            eng.dma_start(dst[:, 0, :], c[0]).then_inc(landed, 16)
            eng.dma_start(dst[:, 1:5, :], c[1].rearrange("(i p) n -> p i n", p=P)).then_inc(landed, 16)
            wide = c[2].rearrange("(i a r) n -> i a r n", i=8, r=16)
            for i in range(8):
                eng.dma_start(dst[:, 5 + i, :], wide[i, :, 0:8, :]).then_inc(landed, 16)

        def load(sp, u, slot, landed):
            windows(sp, u, 0, kcache, landed)

        def load_values(pool, u, slot, landed):
            windows(pool, u, 1, vcache, landed)
            pool.dma_start(vnew[:, :], io["kv_new"][ds(u * DEC_S, DEC_S), 3 * GW:6 * GW]).then_inc(landed, 16)

        def stage(pool, u, slot, staged):
            t = ds(SEQ + DEC_S * u, DEC_S)
            pool.tensor_copy(qst[:, slot, :, 0:DEC_S], swa_qT[:, :, t]).then_inc(staged, 1)
            pool.tensor_copy(knew[:, slot, :, :], kT[:, :, t]).then_inc(staged, 1)

        def q(g, h):
            return lambda slot: qst[:, slot, 4 * g + h, :]

        chunks = []
        c0 = 0
        while c0 < SWA_CACHED:
            g = SWA_TILES[c0 // P][0]
            n = P
            while n < 512 and c0 + n < SWA_CACHED and SWA_TILES[(c0 + n) // P][0] == g:
                n += P
            chunks.append((c0, n, [(PAD * h, PAD, [(q(g, h), lambda slot, h=h, c0=c0, n=n: KT[:, h, c0:c0 + n])])
                                   for h in range(SWA_H)]))
            c0 += n
        for g in range(3):
            chunks.append((SWA_CACHED + g * DEC_S, DEC_S,
                           [(PAD * h, PAD, [(q(g, h), lambda slot, g=g, h=h: knew[:, slot, 4 * g + h, :])])
                            for h in range(SWA_H)]))

        def key_copies(g, bank):
            yield KT[:, :, g * P:(g + 1) * P], bank.rearrange("p (a b) -> p a b", a=4)

        attend_sample(k, "sws", {
            "rows": P, "cols": SWA_KEYS, "scale": 1.0, "bias_scale": SWA_SCALE,
            "bias": lambda c0, n: e["bias_s"][:, c0:c0 + n],
            "groups": [[(lambda slot, j=j, h=h: kcache[:, j, h * P:(h + 1) * P], P) for h in range(SWA_H)]
                       for j in range(len(SWA_TILES))],
            "key_copies": key_copies, "chunks": chunks,
            "keys": [(j * P, P, lambda slot, h, j=j: vcache[:, j, h * P:(h + 1) * P])
                     for j in range(len(SWA_TILES))]
            + [(SWA_CACHED + g * DEC_S, DEC_S,
                lambda slot, h, g=g: vnew[:, g * GW + h * P:g * GW + (h + 1) * P]) for g in range(3)],
            "vblocks": [(8 * h, 8, h, PAD * h) for h in range(SWA_H)],
            "load": load, "stage": stage, "n_stage": 2, "landed_per_unit": 16 * 10,
            "load_values": load_values, "values_per_unit": 16 * 11,
            "setup_pool": setup_pool, "setup_count": 1,
            "out": lambda u, bank: (e["oT"][:, 4:8, ds(SEQ + DEC_S * u, DEC_S)],
                                    bank[:, 0:32].rearrange("p (h s) -> p h s", h=SWA_H)),
        })


def memory_attention(k, layer):
    nc, io = k.nc, k.io
    n_ = f"m{layer}"
    with ExitStack() as ctx:
        qT = k.sb(ctx, n_ + "_qT", [P, 8, T])
        oT = k.sb(ctx, n_ + "_oT", [P, 8, T])
        with ExitStack() as c1:
            mkv = k.sb(c1, n_ + "_mkv", [P, 2, 2 * D])
            kT = k.sb(c1, n_ + "_kT", [P, 8, N_MEM])
            gemm_stage(k, n_ + "in", [
                ("feat", k.xT, io["mem_wq"][layer], 512, qT[:, :, :].rearrange("p a t -> p (a t)")),
                ("tok", k.memT, io["mem_wk"][layer], 512, mkv[:, :, 0:D]),
                ("tok", k.memT, io["mem_wv"][layer], 512, mkv[:, :, D:2 * D]),
            ])
            turn_stage(k, n_ + "kturn", [
                ([mkv[:, i, (4 * half + j) * P:(4 * half + j + 1) * P] for j in range(4)], P,
                 kT[:, 4 * half:4 * half + 4, i * P:(i + 1) * P]) for i in range(2) for half in range(2)])
            with ExitStack() as c2:
                stored = k.sem(n_ + "_kv_stored")
                block = c2.enter_context(k.block())

                @block.sync
                def _(sp):
                    sp.dma_start(io["mem_kv_prompt"][layer, 0].rearrange("(i p) c h d -> p i (c h d)", p=P),
                                 mkv[:, :, :]).then_inc(stored, 16)
                    sp.wait_ge(stored, 16)
            units = []
            for qb in range(2):
                qs = slice(qb * P, (qb + 1) * P)
                for h in range(MEM_H):
                    units.append({
                        "scores": [(0, N_MEM, [(qT[:, 2 * h + c, qs], kT[:, 2 * h + c, :]) for c in range(2)])],
                        "bias": None,
                        "keys": [(kb * P, [mkv[:, kb, D + (2 * h + c) * P:D + (2 * h + c + 1) * P] for c in range(2)])
                                 for kb in range(2)],
                        "outs": [oT[:, 2 * h + c, qs] for c in range(2)]})
            attend_prompt(k, n_ + "p", units, N_MEM, MEM_SCALE, 1.0)
        with ExitStack() as c1:
            cache = k.sb(c1, n_ + "_cache", [P, 2, 2, 2 * D])
            KT = k.sb(c1, n_ + "_skT", [P, 8, N_MEM])
            qst = k.sb(c1, n_ + "_sq", [P, 2, 8, PAD])

            def setup_pool(pool, done):
                pool.memset(qst[:, :, :, :], 0.0).then_inc(done, 1)
                pool.wait_ge(done, 1)

            def load(sp, u, slot, landed):
                src = io["cache_mem_kv"][layer, ds(u, 1)].rearrange("b (i p) c h d -> p (b i) (c h d)", p=P)
                sp.dma_start(cache[:, slot, :, :], src).then_inc(landed, 16)

            def stage(pool, u, slot, staged):
                pool.tensor_copy(qst[:, slot, :, 0:DEC_S], qT[:, :, ds(SEQ + DEC_S * u, DEC_S)]).then_inc(staged, 1)

            def key_copies(g, bank):
                i, half = divmod(g, 2)
                yield KT[:, 4 * half:4 * half + 4, i * P:(i + 1) * P], bank.rearrange("p (a b) -> p a b", a=4)

            attend_sample(k, n_ + "s", {
                "rows": P, "cols": N_MEM, "scale": MEM_SCALE, "bias_scale": 1.0, "bias": lambda c0, n: None,
                "groups": [[(lambda slot, i=i, b=4 * half + j: cache[:, slot, i, b * P:(b + 1) * P], P)
                            for j in range(4)] for i in range(2) for half in range(2)],
                "key_copies": key_copies,
                "chunks": [(0, N_MEM, [(PAD * h, PAD, [
                    (lambda slot, b=2 * h + c: qst[:, slot, b, :], lambda slot, b=2 * h + c: KT[:, b, :])
                    for c in range(2)]) for h in range(MEM_H)])],
                "keys": [(i * P, P, lambda slot, b, i=i: cache[:, slot, i, D + b * P:D + (b + 1) * P]) for i in range(2)],
                "vblocks": [(8 * b, 8, b, PAD * (b // 2)) for b in range(8)],
                "load": load, "stage": stage, "n_stage": 1, "landed_per_unit": 16,
                "setup_pool": setup_pool, "setup_count": 1,
                "out": lambda u, bank: (oT[:, :, ds(SEQ + DEC_S * u, DEC_S)],
                                        bank[:, 0:64].rearrange("p (b s) -> p b s", b=8)),
            })
        gemm_stage(k, n_ + "out", [("tok", oT, io["mem_wo"][layer], 512, k.h)])


def odd_mixer(k):
    nc, io = k.nc, k.io
    with ExitStack() as ctx:
        prod = k.sb(ctx, "c_prod", [P, 24, T])
        cT = k.sb(ctx, "c_convT", [P, 8, T])
        gemm_stage(k, "cin", [("feat", k.xT, io["conv_w_in"][0], 512, prod[:, :, :].rearrange("p a t -> p (a t)"))])
        with ExitStack() as c1:
            up = k.sb(c1, "c_up", [P, 8, SEQ + 2])
            us = k.sb(c1, "c_us", [P, 8, DEC_B, DEC_S + 2])
            state = k.sb(c1, "c_state", [2 * DEC_B, D])
            taps = k.sb(c1, "c_taps", [3, D])
            tapT = k.sb(c1, "c_tapT", [P, 8, 3])
            tail = k.sb(c1, "c_tail", [P, 8, 32])
            tail_tok = k.sb(c1, "c_tail_tok", [18, D])
            landed, turned, taken = k.sem("c_landed"), k.sem("c_turned"), k.sem("c_taken")
            zeroed, u_ready, chain = k.sem("c_zeroed"), k.sem("c_u_ready"), k.sem("c_chain")
            tail_ready, tail_turned, tail_taken = k.sem("c_tail_ready"), k.sem("c_tail_turned"), k.sem("c_tail_taken")
            stored = k.sem("c_stored")
            block = c1.enter_context(k.block())

            @block.sync
            def _(sp):
                sp.dma_start(state[:, :], io["state_conv"][0].rearrange("b s d -> (b s) d")).then_inc(landed, 16)
                sp.dma_start(taps[:, :], io["conv_w"][0]).then_inc(landed, 16)
                sp.wait_ge(tail_taken, 2)
                sp.dma_start(io["conv_prompt"][0, 0], tail_tok[0:2, :]).then_inc(stored, 16)
                sp.dma_start(io["conv_sample"][0].rearrange("b s d -> (b s) d"), tail_tok[2:18, :]).then_inc(stored, 16)
                sp.wait_ge(stored, 32)

            @block.gpsimd
            def _(pool):
                pool.memset(up[:, :, 0:2], 0.0).then_inc(zeroed, 1)

            @block.tensor
            def _(pe):
                pe.wait_ge(landed, 32)
                for c in range(8):
                    pe.transpose(k.ps[:, 0, 16 * c:16 * c + 16], state[:, c * P:(c + 1) * P], k.ident[0:16, 0:16])
                for c in range(8):
                    mm = pe.transpose(k.ps[:, 1, 4 * c:4 * c + 3], taps[:, c * P:(c + 1) * P], k.ident[0:3, 0:3])
                mm.then_inc(turned, 1)
                pe.wait_ge(tail_ready, 1)
                for c in range(8):
                    mm = pe.transpose(k.ps[0:18, 2 + c // 4, (c % 4) * P:(c % 4 + 1) * P], tail[:, c, 0:18], k.ident[:, :])
                mm.then_inc(tail_turned, 1)

            @block.scalar
            def _(act):
                act.wait_ge(turned, 1)
                act.activation(us[:, :, :, 0:2], k.ps[:, 0, 0:128].rearrange("p (c b s) -> p c b s", c=8, b=DEC_B),
                               ACT.Copy).then_inc(taken, 1)
                act.activation(tapT[:, :, :], k.ps[:, 1, 0:32].rearrange("p (c s) -> p c s", c=8)[:, :, 0:3],
                               ACT.Copy).then_inc(taken, 1)
                act.wait_ge(tail_turned, 1)
                for half in range(2):
                    act.activation(tail_tok[:, half * 512:(half + 1) * 512], k.ps[0:18, 2 + half, :],
                                   ACT.Copy).then_inc(tail_taken, 1)

            @block.vector
            def _(dve):
                dve.tensor_tensor(out=up[:, :, 2:], in0=prod[:, 8:16, 0:SEQ], in1=prod[:, 16:24, 0:SEQ],
                                  op=ALU.mult).then_inc(u_ready, 1)
                for c in range(8):
                    dve.tensor_tensor(out=us[:, c, :, 2:],
                                      in0=prod[:, 8 + c, SEQ:T].rearrange("p (b s) -> p b s", b=DEC_B),
                                      in1=prod[:, 16 + c, SEQ:T].rearrange("p (b s) -> p b s", b=DEC_B),
                                      op=ALU.mult).then_inc(u_ready, 1)
                dve.wait_ge(u_ready, 9)
                dve.wait_ge(zeroed, 1)
                dve.wait_ge(taken, 2)
                dve.tensor_copy(tail[:, :, 0:2], up[:, :, SEQ:SEQ + 2])
                dve.tensor_copy(tail[:, :, 2:18].rearrange("p c (b s) -> p c b s", b=DEC_B),
                                us[:, :, :, DEC_S:DEC_S + 2]).then_inc(tail_ready, 1)
                n = 0
                for step in range(3):
                    for c in range(8):
                        w = tapT[:, c, step:step + 1]
                        outs = (cT[:, c, 0:SEQ], cT[:, c, SEQ:T].rearrange("p (b s) -> p b s", b=DEC_B))
                        ins = (up[:, c, step:step + SEQ], us[:, c, :, step:step + DEC_S])
                        for o, i_ in zip(outs, ins):
                            if step == 0:
                                last = dve.tensor_scalar(out=o, in0=i_, scalar1=w, scalar2=None, op0=ALU.mult)
                            else:
                                last = dve.scalar_tensor_tensor(out=o, in0=i_, scalar=w, in1=o, op0=ALU.mult, op1=ALU.add)
                    last.then_inc(chain, 1)
                    dve.wait_ge(chain, step + 1)
                dve.tensor_tensor(out=cT[:, :, :], in0=cT[:, :, :], in1=prod[:, 0:8, :], op=ALU.mult).then_inc(chain, 1)
        gemm_stage(k, "cout", [("tok", cT, io["conv_w_out"][0], 512, k.h)])


def choose_stage(k, name, layer, pqT, idx, gate):
    nc, io = k.nc, k.io
    H2 = 2 * PEER_H
    with ExitStack() as ctx:
        sub = k.sb(ctx, name + "_sub", [P, H2, P])
        subT = k.sb(ctx, name + "_subT", [P, H2, P])
        s = k.sb(ctx, name + "_s", [P, H2, N_KEYS])
        s2 = k.sb(ctx, name + "_s2", [P, H2, N_KEYS])
        v16 = k.sb(ctx, name + "_v16", [P, H2, TOPK])
        i16 = k.sb(ctx, name + "_i16", [P, H2, TOPK], U32)
        i16f = k.sb(ctx, name + "_i16f", [P, PEER_H, 2, TOPK])
        cand = k.sb(ctx, name + "_cand", [P, PEER_H, TOPK, TOPK])
        cand2 = k.sb(ctx, name + "_cand2", [P, PEER_H, TOPK, TOPK])
        best = k.sb(ctx, name + "_best", [P, PEER_H, TOPK])
        sel = k.sb(ctx, name + "_sel", [P, PEER_H, TOPK], U32)
        half = k.sb(ctx, name + "_half", [P, 2, HK], U32)
        halff = k.sb(ctx, name + "_halff", [P, 2, HK])
        part = k.sb(ctx, name + "_part", [P, 2, HK])
        iota16 = k.sb(ctx, name + "_iota16", [P, TOPK])
        den = k.sb(ctx, name + "_den", [P, PEER_H])
        landed, turned, sub_ready = k.sem(name + "_landed"), k.sem(name + "_turned"), k.sem(name + "_sub_ready")
        scored, s_ready, chain = k.sem(name + "_scored"), k.sem(name + "_s_ready"), k.sem(name + "_chain")
        s_used, diff_ready, exp_ready = k.sem(name + "_s_used"), k.sem(name + "_diff"), k.sem(name + "_exp")
        block = ctx.enter_context(k.block())

        @block.sync
        def _(sp):
            sp.dma_start(sub[:, :, :], io["peer_subkeys"][layer].rearrange("h a n k -> n (h a) k")).then_inc(landed, 16)
            sp.dma_start(iota16[:, :], bass.AP(io["iota16"].tensor, 0, [[0, P], [1, TOPK]])).then_inc(landed, 16)

        @block.tensor
        def _(pe):
            pe.wait_ge(landed, 32)
            for g in range(4):
                for j in range(4):
                    mm = pe.transpose(k.ps[:, g, j * P:(j + 1) * P], sub[:, 4 * g + j, :], k.ident[:, :])
                mm.then_inc(turned, 1)
            for i, (t0, n) in enumerate(TILES):
                pe.wait_ge(sub_ready, 4)
                wait(pe, s_ready, 4 * i)
                for g in range(4):
                    for j in range(4):
                        hp = 4 * g + j
                        mm = pe.matmul(k.ps[0:n, 4 + g, j * P:(j + 1) * P], pqT[:, hp, t0:t0 + n], subT[:, hp, :],
                                       start=True, stop=True)
                    mm.then_inc(scored, 1)

        @block.scalar
        def _(act):
            for g in range(4):
                act.wait_ge(turned, g + 1)
                act.activation(subT[:, 4 * g:4 * g + 4, :].rearrange("p a b -> p (a b)"), k.ps[:, g, :],
                               ACT.Copy).then_inc(sub_ready, 1)
            for i, (t0, n) in enumerate(TILES):
                wait(act, s_used, i)
                for g in range(4):
                    act.wait_ge(scored, 4 * i + g + 1)
                    act.activation(s[0:n, 4 * g:4 * g + 4, :].rearrange("p a b -> p (a b)"), k.ps[0:n, 4 + g, :],
                                   ACT.Copy).then_inc(s_ready, 1)
                act.wait_ge(diff_ready, i + 1)
                act.activation(best[0:n, :, :], best[0:n, :, :], ACT.Exp).then_inc(exp_ready, 1)

        @block.vector
        def _(dve):
            link = Chain(dve, chain)

            def top16(n, groups, src, spare, val, ind):
                for g in range(groups):
                    last = dve.max(val[0:n, g, 0:8], src(g))
                link(last)
                for g in range(groups):
                    dve.max_index(ind[0:n, g, 0:8], val[0:n, g, 0:8], src(g))
                    last = dve.match_replace(spare(g), val[0:n, g, 0:8], src(g), LOWEST)
                link(last)
                for g in range(groups):
                    last = dve.max(val[0:n, g, 8:16], spare(g))
                link(last)
                for g in range(groups):
                    last = dve.max_index(ind[0:n, g, 8:16], val[0:n, g, 8:16], spare(g))
                link(last)

            dve.wait_ge(landed, 32)
            for i, (t0, n) in enumerate(TILES):
                dve.wait_ge(s_ready, 4 * (i + 1))
                top16(n, H2, lambda g: s[0:n, g, :], lambda g: s2[0:n, g, :], v16, i16)
                dve.tensor_copy(i16f[0:n].rearrange("p h a t -> p (h a t)"),
                                i16[0:n].rearrange("p g t -> p (g t)")).then_inc(s_used, 1)
                v4 = v16[0:n, :, :].rearrange("p (h a) t -> p h a t", a=2)
                first = v4[:, :, 0, :].unsqueeze(3).to_broadcast([n, PEER_H, TOPK, TOPK])
                second = v4[:, :, 1, :].unsqueeze(2).to_broadcast([n, PEER_H, TOPK, TOPK])
                link(dve.tensor_tensor(out=cand[0:n], in0=first, in1=second, op=ALU.add))
                flat = [x[0:n].rearrange("p h a b -> p h (a b)") for x in (cand, cand2)]
                top16(n, PEER_H, lambda g: flat[0][:, g, :], lambda g: flat[1][:, g, :], best, sel)
                selv = sel[0:n].rearrange("p h t -> p (h t)")
                dve.tensor_scalar(out=half[0:n, 0, :], in0=selv, scalar1=4, scalar2=None, op0=ALU.logical_shift_right)
                link(dve.tensor_scalar(out=half[0:n, 1, :], in0=selv, scalar1=15, scalar2=None, op0=ALU.bitwise_and))
                link(dve.tensor_copy(halff[0:n], half[0:n]))
                dve.wait_ge(s_used, i + 1)
                for a in range(2):
                    hot = (cand, cand2)[a][0:n].rearrange("p h a b -> p (h a) b")
                    hot4 = (cand, cand2)[a][0:n]
                    link(dve.tensor_tensor(out=hot, in0=iota16[0:n, :].unsqueeze(1).to_broadcast([n, HK, TOPK]),
                                           in1=halff[0:n, a, :].unsqueeze(2).to_broadcast([n, HK, TOPK]),
                                           op=ALU.is_equal))
                    link(dve.tensor_tensor(out=hot4, in0=hot4,
                                           in1=i16f[0:n, :, a, :].unsqueeze(2).to_broadcast([n, PEER_H, TOPK, TOPK]),
                                           op=ALU.mult))
                    link(dve.tensor_reduce(out=part[0:n, a, :], in_=hot, axis=AX, op=ALU.add))
                link(dve.scalar_tensor_tensor(out=part[0:n, 0, :], in0=part[0:n, 0, :], scalar=float(N_KEYS),
                                              in1=part[0:n, 1, :], op0=ALU.mult, op1=ALU.add))
                link(dve.tensor_scalar(out=idx[0:n, i, :], in0=part[0:n, 0, :], scalar1=float(N_EXPERTS * layer),
                                       scalar2=None, op0=ALU.add))
                link(dve.tensor_copy(den[0:n, :], best[0:n, :, 0]))
                dve.tensor_tensor(out=best[0:n], in0=best[0:n],
                                  in1=den[0:n, :].unsqueeze(2).to_broadcast([n, PEER_H, TOPK]),
                                  op=ALU.subtract).then_inc(diff_ready, 1)
                dve.wait_ge(exp_ready, i + 1)
                link(dve.reduce_sum(den[0:n, :], best[0:n], AX))
                link(dve.reciprocal(den[0:n, :], den[0:n, :]))
                link(dve.tensor_tensor(out=gate[0:n, i, :].rearrange("p (h t) -> p h t", h=PEER_H), in0=best[0:n],
                                       in1=den[0:n, :].unsqueeze(2).to_broadcast([n, PEER_H, TOPK]), op=ALU.mult))


def experts_stage(k, name, layer, idx, gate):
    nc, io = k.nc, k.io
    GRP, PER = 4, 4
    with ExitStack() as ctx:
        ur = k.sb(ctx, name + "_u", [P, TOPK, D])
        vr = k.sb(ctx, name + "_v", [P, TOPK, D])
        ist = k.sb(ctx, name + "_idx", [P, 2, TOPK], I32)
        dots = k.sb(ctx, name + "_dots", [P, 2, TOPK])
        weight = k.sb(ctx, name + "_weight", [P, 2, TOPK])
        diag = k.sb(ctx, name + "_diag", [P, 2, PER, P])
        zero = k.sb(ctx, name + "_zero", [P, P])
        zeroed, idx_staged = k.sem(name + "_zeroed"), k.sem(name + "_idx_staged")
        u_landed = [k.gathered[f"u_rows_landed{g}"] for g in range(GRP)]
        v_landed = [k.gathered[f"v_rows_landed{g}"] for g in range(GRP)]
        before = layer * 16 * PER * len(TILES) * PEER_H
        u_used, v_used, dots_done = k.sem(name + "_u_used"), k.sem(name + "_v_used"), k.sem(name + "_dots_done")
        gelu_done, weight_ready, diag_ready = k.sem(name + "_gelu"), k.sem(name + "_weight_ready"), k.sem(name + "_diag_ready")
        begun, begun_pe = k.sem(name + "_begun_pool"), k.sem(name + "_begun_pe")
        sum_ready, sum_taken = k.sem(name + "_sum_ready"), k.sem(name + "_sum_taken")
        block = ctx.enter_context(k.block())
        u_rows = io["peer_u"].rearrange("l e d -> (l e) d")
        v_rows = io["peer_v"].rearrange("l e d -> (l e) d")
        PAIRS = PEER_H // 2

        def heads(eng, i, body):
            def pair(j):
                for par in range(2):
                    h = 2 * j + par
                    body(h, PEER_H * i + h, par)
            if i == 0:
                repeat(eng, PAIRS, pair)
            else:
                with eng.Fori(0, PAIRS) as j:
                    pair(j)

        @block.gpsimd
        def _(pool):
            pool.memset(zero[:, :], 0.0).then_inc(zeroed, 1)
            for i, (_, n) in enumerate(TILES):
                def body(h, H, par):
                    wait(pool, v_used, GRP * (H - 1))
                    pool.tensor_copy(ist[0:n, par, :], idx[0:n, i, ds(h * TOPK, TOPK)]).then_inc(idx_staged, 1)
                    wait_apart(pool, idx_staged, H + 1, begun)
                    for rows, ring, landed, used in ((u_rows, ur, u_landed, u_used), (v_rows, vr, v_landed, v_used)):
                        for g in range(GRP):
                            wait_apart(pool, used, GRP * (H - 1) + g + 1, begun)
                            for m in range(PER):
                                j = g * PER + m
                                pool.indirect_dma_start(
                                    out=ring[0:n, j, :], out_offset=None, in_=rows,
                                    in_offset=bass.IndirectOffsetOnAxis(ap=ist[0:n, par, j:j + 1], axis=0),
                                ).then_inc(landed[g], 16)
                heads(pool, i, body)

        @block.vector
        def _(dve):
            for i, (_, n) in enumerate(TILES):
                def body(h, H, par):
                    wait(dve, gelu_done, H - 1)
                    for g in range(GRP):
                        dve.wait_ge(u_landed[g], before + 16 * PER * (H + 1))
                        for m in range(PER):
                            j = g * PER + m
                            last = dve.tensor_tensor_reduce(
                                out=ur[0:n, j, :], in0=ur[0:n, j, :], in1=k.x[0:n, i, :], scale=1.0, scalar=0.0,
                                op0=ALU.mult, op1=ALU.add, accum_out=dots[0:n, par, j:j + 1])
                        last.then_inc(u_used, 1)
                    dve.wait_ge(gelu_done, H + 1)
                    wait(dve, diag_ready, GRP * (H - 1))
                    dve.tensor_tensor(out=weight[0:n, par, :], in0=dots[0:n, par, :],
                                      in1=gate[0:n, i, ds(h * TOPK, TOPK)], op=ALU.mult).then_inc(weight_ready, 1)
                heads(dve, i, body)

        @block.scalar
        def _(act):
            for i, (_, n) in enumerate(TILES):
                def body(h, H, par):
                    act.wait_ge(u_used, GRP * (H + 1))
                    act.activation(dots[0:n, par, :], dots[0:n, par, :], ACT.Gelu).then_inc(gelu_done, 1)
                    act.wait_ge(weight_ready, H + 1)
                    for g in range(GRP):
                        wait(act, v_used, GRP * H + g - 1)
                        for m in range(PER):
                            j = g * PER + m
                            last = act.activation(diag[0:n, g % 2, m, 0:n], k.ident[0:n, 0:n], ACT.Copy,
                                                  scale=weight[0:n, par, j:j + 1])
                        last.then_inc(diag_ready, 1)
                heads(act, i, body)
                act.wait_ge(sum_ready, i + 1)
                for half in range(2):
                    last = act.activation(k.h[0:n, i, half * 512:(half + 1) * 512],
                                          k.ps[0:n, 2 * (i % 2) + half, :], ACT.Copy)
                last.then_inc(sum_taken, 1)

        @block.tensor
        def _(pe):
            pe.wait_ge(zeroed, 1)
            for i, (_, n) in enumerate(TILES):
                wait(pe, sum_taken, i - 1)
                outs = [k.ps[0:n, 2 * (i % 2) + half, :] for half in range(2)]
                for o in outs:
                    pe.matmul(o, zero[0:n, 0:n], k.x[0:n, i, 0:512], start=True, stop=False)

                def body(h, H, par):
                    for g in range(GRP):
                        pe.wait_ge(v_landed[g], before + 16 * PER * (H + 1))
                        wait_apart(pe, diag_ready, GRP * H + g + 1, begun_pe)
                        for m in range(PER):
                            j = g * PER + m
                            for half in range(2):
                                mm = pe.matmul(outs[half], diag[0:n, g % 2, m, 0:n],
                                               vr[0:n, j, half * 512:(half + 1) * 512], start=False, stop=False)
                        mm.then_inc(v_used, 1)
                heads(pe, i, body)
                for o in outs:
                    mm = pe.matmul(o, zero[0:n, 0:n], k.x[0:n, i, 0:512], start=False, stop=True)
                mm.then_inc(sum_ready, 1)


def peer(k, layer):
    io = k.io
    name = f"p{layer}"
    with ExitStack() as ctx:
        idx = k.sb(ctx, name + "_experts", [P, 3, HK], I32)
        gate = k.sb(ctx, name + "_gates", [P, 3, HK])
        with ExitStack() as c1:
            pqT = k.sb(c1, name + "_qT", [P, 2 * PEER_H, T])
            gemm_stage(k, name + "q", [("feat", k.xT, io["peer_wq"][layer], 512,
                                        pqT[:, :, :].rearrange("p a t -> p (a t)"))])
            choose_stage(k, name + "c", layer, pqT, idx, gate)
        experts_stage(k, name + "e", layer, idx, gate)


def decode_step(nc, io):
    with ExitStack() as ctx:
        k = Kernel(nc, ctx, io)
        copied = k.copied
        zeros = k.sb(ctx, "zeros", [P, 512])
        zeroed = k.sem("zeros_ready")
        with ExitStack() as c1:
            block = c1.enter_context(k.block())

            @block.vector
            def _(dve):
                dve.memset(zeros[:, :], 0.0).then_inc(zeroed, 1)

            @block.scalar
            def _(act):
                act.wait_ge(zeroed, 1)
                for g, (w, _) in enumerate(SWA_GROUPS):
                    src = io[("cache_swa_w128", "cache_swa_w512", "cache_swa_w2048")[g]]
                    for b in range(DEC_B):
                        act.dma_start(io[f"swa_sample{g}"][0, b, 0:w - DEC_S].rearrange("w c h d -> w (c h d)"),
                                      src[0, b, DEC_S:w].rearrange("w c h d -> w (c h d)")).then_inc(copied, 16)
                    rows = w - SEQ
                    if rows > 0:
                        dst = io[f"swa_prompt{g}"][0, 0, 0:rows].rearrange("(i p) c h d -> p i (c h d)", p=P)
                        for i in range(rows // P):
                            for c in range(2):
                                act.dma_start(dst[:, i, c * 512:(c + 1) * 512], zeros[:, :]).then_inc(copied, 16)
        n_copied = 16 * (3 * DEC_B + 2 * sum((w - SEQ) // P for w, _ in SWA_GROUPS if w > SEQ))
        start_stage(k)
        y = [io["y_prompt"][0, 0:P], io["y_prompt"][0, P:SEQ], io["y_sample"].rearrange("b s d -> (b s) d")]
        for layer in range(DEPTH):
            even_mixer(k) if layer % 2 == 0 else odd_mixer(k)
            norm_stage(k, f"nx{layer}", io["ln_mix_g"][layer], io["ln_mix_b"][layer])
            memory_attention(k, layer)
            norm_stage(k, f"nm{layer}", io["ln_mem_g"][layer], io["ln_mem_b"][layer])
            peer(k, layer)
            norm_stage(k, f"nf{layer}", io["ln_ffn_g"][layer], io["ln_ffn_b"][layer], y if layer == DEPTH - 1 else None)
        with ExitStack() as c1:
            block = c1.enter_context(k.block())

            @block.scalar
            def _(act):
                act.wait_ge(copied, n_copied)


def constants():
    pos = np.concatenate([np.arange(SEQ), np.tile(PAST + np.arange(DEC_S), DEC_B)]).astype(np.float32)
    half = ROPE // 2
    inv = np.float32(10000.0) ** (-np.arange(half, dtype=np.float32) / np.float32(half))
    ang = (pos[:, None] * inv[None, :]).astype(np.float32)
    cos, sin = np.cos(ang), np.sin(ang)
    rope_tok = np.stack([cos, sin], axis=1)
    rope_feat = np.stack([np.concatenate([cos, cos], 1).T, np.concatenate([-sin, sin], 1).T], axis=1)
    dist = DIST_TOP - np.arange(N_DIST)
    exact = N_BUCKETS // 2
    d = np.maximum(dist, 1).astype(np.float32)
    large = exact + (np.log(d / exact) / np.float32(math.log(MAX_DIST / exact)) * (N_BUCKETS - exact)).astype(np.int32)
    bucket = np.where(dist < exact, dist, np.minimum(large, N_BUCKETS - 1))
    hot = np.zeros((N_BUCKETS + 1, 3, N_DIST), np.float32)
    for g, (w, dil) in enumerate(SWA_GROUPS):
        ok = (dist >= 0) & (dist <= w) & (dist % dil == 0)
        hot[np.where(ok, bucket, N_BUCKETS), g, np.arange(N_DIST)] = 1.0
    q = np.arange(P)[:, None, None] + P * np.arange(2)[None, :, None]
    causal = np.where(np.arange(SEQ)[None, None, :] <= q, 0.0, DISALLOWED)
    new = np.where(np.arange(DEC_S)[None, :] <= (np.arange(64) % DEC_S)[:, None], 0.0, DISALLOWED)
    out = {"ident": np.eye(P), "rope_tok": rope_tok, "rope_feat": rope_feat, "bucket_hot": hot, "causal": causal,
           "causal_new": new, "iota16": np.arange(TOPK)}
    return {n: np.ascontiguousarray(v.astype(np.float32)) for n, v in out.items()}


INPUTS = ["x_prompt", "x_sample", "cache_mla", "page_table", "cache_swa_w128", "cache_swa_w512", "cache_swa_w2048",
          "state_conv", "cache_mem_kv", "mem_prompt", "attn_w_in", "mla_q_norm", "mla_kv_norm", "mla_w_uq", "mla_w_uk",
          "mla_w_uv", "attn_w_out", "rel_bias", "conv_w_in", "conv_w", "conv_w_out", "mem_wq", "mem_wk", "mem_wv",
          "mem_wo", "ln_mix_g", "ln_mix_b", "ln_mem_g", "ln_mem_b", "ln_ffn_g", "ln_ffn_b", "peer_wq", "peer_subkeys",
          "peer_u", "peer_v"]
OUTPUTS = [("y_prompt", (1, SEQ, D)), ("y_sample", (DEC_B, DEC_S, D)), ("mla_rows_prompt", (1, 1, SEQ, MLA_ROW)),
           ("mla_rows_sample", (1, DEC_B, DEC_S, MLA_ROW))]
for _g, (_w, _) in enumerate(SWA_GROUPS):
    OUTPUTS += [(f"swa_prompt{_g}", (1, 1, _w, 2, SWA_H, SWA_D)), (f"swa_sample{_g}", (1, DEC_B, _w, 2, SWA_H, SWA_D))]
OUTPUTS += [("conv_prompt", (1, 1, 2, D)), ("conv_sample", (1, DEC_B, 2, D)),
            ("mem_kv_prompt", (DEPTH, 1, N_MEM, 2, MEM_H, MEM_D))]
SCRATCH = [("kv_new", (DEC_B * DEC_S, 6 * GW)), ("bias_by_dist", (3, SWA_H, N_DIST)), ("bias_rep", (3, SWA_H, P, REP_N))]


def kernel(**inputs):
    import numpy as _np
    import concourse.bacc as _bacc
    from concourse import mybir as _mybir
    from concourse.bass_utils import run_bass_kernel_spmd as _run

    nc = _bacc.Bacc("TRN2", target_bir_lowering=False, num_devices=1)
    arrays, io = {}, {}
    named = {n: _np.ascontiguousarray(inputs[n]) for n in INPUTS}
    named.update(constants())
    for n, a in named.items():
        arrays["in_" + n] = a
        io[n] = nc.dram_tensor("in_" + n, a.shape, _mybir.dt.from_np(a.dtype), kind="ExternalInput").ap()
    for n, shape in OUTPUTS:
        io[n] = nc.dram_tensor("out_" + n, shape, _mybir.dt.float32, kind="ExternalOutput").ap()
    for n, shape in SCRATCH:
        io[n] = nc.dram_tensor("scratch_" + n, shape, _mybir.dt.float32, kind="Internal").ap()
    decode_step(nc, io)
    r = _run(nc, [arrays], core_ids=[0])
    return tuple(r.results[0]["out_" + n] for n, _ in OUTPUTS)
```

```python
import math

import numpy as np
import concourse.bass as bass
from concourse import mybir
from contextlib import ExitStack, contextmanager

F32 = mybir.dt.float32
I32 = mybir.dt.int32
U32 = mybir.dt.uint32
ALU = mybir.AluOpType
ACT = mybir.ActivationFunctionType
AX = mybir.AxisListType.X
ds = bass.ds

STAGES = []
P = 128
D = 1024
KC = D // P
SEQ = 256
DEC_B, DEC_S = 8, 8
T = SEQ + DEC_B * DEC_S
TILES = [(0, 128), (128, 128), (256, 64)]
PROMPT_TILES = TILES[:2]
DEPTH = 2
PAST = 2048
PAGE = 128
N_PAGES = PAST // PAGE
Q_LORA = KV_LORA = 256
NOPE, ROPE, D_V = 64, 32, 64
MLA_H = 8
MLA_SCALE = (NOPE + ROPE) ** -0.5
MLA_ROW = KV_LORA + ROPE
SWA_GROUPS = ((128, 1), (512, 4), (2048, 16))
SWA_H, SWA_D = 4, 128
SWA_SCALE = SWA_D ** -0.5
GW = SWA_H * SWA_D
N_BUCKETS, MAX_DIST = 32, 2048
N_MEM, MEM_H, MEM_D = 256, 4, 256
MEM_SCALE = MEM_D ** -0.5
N_KEYS = 128
N_EXPERTS = N_KEYS * N_KEYS
PEER_H, TOPK = 8, 16
HK = PEER_H * TOPK
ALPHA = (2 * DEPTH) ** 0.25
EPS = 1e-5
DISALLOWED = -1e30
LOWEST = -3e38
DIST_TOP = 2055
N_DIST = 2312
REP0, REP_N = 1800, 512
PAD = 32
COPIES_PER_JOB = 5
SWA_TILES = [(0, 0)] + [(1, i) for i in range(4)] + [(2, i) for i in range(8)]
SWA_CACHED = len(SWA_TILES) * P
SWA_KEYS = SWA_CACHED + 3 * DEC_S


def wait(eng, sem, n):
    if not isinstance(n, int) or n > 0:
        eng.wait_ge(sem, n)


def wait_apart(eng, sem, n, begun):
    if not isinstance(n, int) or n > 0:
        eng.wait_ge(sem, n)
        eng.sem_inc(begun, 1)


def repeat(eng, n, body):
    body(0)
    if n == 2:
        body(1)
    elif n > 2:
        with eng.Fori(1, n) as i:
            body(i)


def repeat_ends(eng, n, body):
    body(0, False)
    if n == 3:
        body(1, False)
    elif n > 3:
        with eng.Fori(1, n - 1) as i:
            body(i, False)
    body(n - 1, True)


class Chain:

    def __init__(self, eng, sem, start=0):
        self.eng, self.sem, self.n, self.start = eng, sem, 0, start

    def __call__(self, ins):
        self.n += 1
        ins.then_inc(self.sem, 1)
        self.eng.wait_ge(self.sem, self.start + self.n)


class Kernel:

    def __init__(self, nc, ctx, io):
        self.nc, self.ctx, self.io = nc, ctx, io
        self.copied = ctx.enter_context(nc.semaphore("swa_copied"))
        self.zeros = self.sb(ctx, "zeros", [P, 512])
        self.copies, self.n_copied = self.plan_copies(), 0
        self.held, self.bank, self.blocks, self.bank_size = [], 0, 0, 46
        names = [f"{r}_rows_landed{g}" for r in "uv" for g in range(4)]
        self.gathered = {n: ctx.enter_context(nc.semaphore(n)) for n in names}
        self.first_sem = max(s.num for s in self.gathered.values()) + 1
        self.ps = ctx.enter_context(nc.psum_tensor("ps", [P, 8, 512], F32))
        self.ident = self.sb(ctx, "ident", [P, P])
        self.x = self.sb(ctx, "x_tok", [P, 3, D])
        self.h = self.sb(ctx, "h_tok", [P, 3, D])
        self.xT = self.sb(ctx, "xT", [P, KC, T])
        self.memT = self.sb(ctx, "memT", [P, KC, N_MEM])

    def sb(self, ctx, name, shape, dt=F32):
        return ctx.enter_context(self.nc.sbuf_tensor(name, shape, dt))

    def plan_copies(self):
        io, pieces = self.io, []
        for g, (w, _) in enumerate(SWA_GROUPS):
            src, dst = io[f"cache_swa_w{w}"][0], io[f"swa_sample{g}"][0]
            rows = w - DEC_S
            step = {120: 120, 504: 504, 2040: 510}[rows]
            for b in range(DEC_B):
                for r in range(0, rows, step):
                    pieces.append((dst[b, r:r + step].rearrange("w c h d -> w (c h d)"),
                                   src[b, r + DEC_S:r + DEC_S + step].rearrange("w c h d -> w (c h d)")))
            if w > SEQ:
                ahead = io[f"swa_prompt{g}"][0, 0, 0:w - SEQ].rearrange("(i p) c h d -> p i c (h d)", p=P)
                for i in range((w - SEQ) // P):
                    pieces.append((ahead[:, i], self.zeros[:, :].unsqueeze(1).to_broadcast([P, 2, 512])))
        return pieces

    def copy_some(self, eng, n):
        for _ in range(min(n, len(self.copies) - self.n_copied)):
            dst, src = self.copies[self.n_copied]
            eng.dma_start(dst, src).then_inc(self.copied, 16)
            self.n_copied += 1

    def sem(self, name):
        num = self.first_sem + self.bank * self.bank_size + len(self.held)
        assert len(self.held) < self.bank_size
        self.held.append(self.nc.alloc_semaphore(name=name, num=num))
        return self.held[-1]

    @contextmanager
    def block(self):
        STAGES.append(self.held[0].name if self.held else "-")
        if self.blocks >= 2:
            first = self.first_sem + (self.bank + 1) % 3 * self.bank_size
            self.nc.sync.sem_clear(range(first, first + self.bank_size))
        with self.nc.Block() as block:
            yield block
        for handle in self.held:
            self.nc.release_semaphore(handle)
        self.held, self.bank, self.blocks = [], (self.bank + 1) % 3, self.blocks + 1


def start_stage(k):
    nc, io = k.nc, k.io
    with ExitStack() as ctx:
        mem = k.sb(ctx, "mem_tok", [P, 2, D])
        zeroed = k.sem("st_zeroed")
        loaded, turned, bank_free = k.sem("st_loaded"), k.sem("st_turned"), k.sem("st_free")
        block = ctx.enter_context(k.block())
        jobs = []
        for i, (t0, n) in enumerate(TILES):
            jobs += [(k.x[0:n, i, :], n, k.xT, t0, half) for half in range(2)]
        for i in range(2):
            jobs += [(mem[:, i, :], P, k.memT, i * P, half) for half in range(2)]

        @block.sync
        def _(sp):
            sp.dma_start(k.ident[:, :], io["ident"]).then_inc(loaded, 16)
            sp.dma_start(k.x[:, 0:2, :], io["x_prompt"][0].rearrange("(i p) d -> p i d", p=P)).then_inc(loaded, 16)
            sp.dma_start(k.x[0:64, 2, :], io["x_sample"].rearrange("b s d -> (b s) d")).then_inc(loaded, 16)
            sp.dma_start(mem[:, :, :], io["mem_prompt"][0].rearrange("(i p) d -> p i d", p=P)).then_inc(loaded, 16)

        @block.vector
        def _(dve):
            dve.memset(k.zeros[:, :], 0.0).then_inc(zeroed, 1)

        @block.tensor
        def _(pe):
            pe.wait_ge(loaded, 64)
            for n, (src, rows, _, _, half) in enumerate(jobs):
                wait(pe, bank_free, n - 1)
                for j in range(4):
                    c = half * 4 + j
                    last = pe.transpose(k.ps[:, n % 2, j * P:j * P + rows], src[:, c * P:(c + 1) * P],
                                        k.ident[0:rows, 0:rows])
                last.then_inc(turned, 1)

        @block.scalar
        def _(act):
            for n, (_, rows, dst, t0, half) in enumerate(jobs):
                act.wait_ge(turned, n + 1)
                bank = k.ps[:, n % 2, :].rearrange("p (j t) -> p j t", j=4)
                act.activation(dst[:, half * 4:half * 4 + 4, t0:t0 + rows], bank[:, :, 0:rows],
                               ACT.Copy).then_inc(bank_free, 1)


def gemm_stage(k, name, jobs):
    nc = k.nc
    with ExitStack() as ctx:
        ring = k.sb(ctx, name + "_w", [P, 2, KC * 512])
        landed = [k.sem(f"{name}_w_landed{s}") for s in range(2)]
        chunk_done, bank_free = k.sem(name + "_chunk_done"), k.sem(name + "_bank_free")
        block = ctx.enter_context(k.block())

        def plan():
            base = 0
            for kind, aT, w, chunk, out in jobs:
                n = w.shape[1] // chunk
                assert n * chunk == w.shape[1] and n % 2 == 0
                yield kind, aT, w, chunk, out, n // 2, base
                base += n

        def parts(kind, aT, chunk):
            tokens = aT.shape[2]
            if kind == "tok":
                return [(t0, min(P, tokens - t0)) for t0 in range(0, tokens, P)]
            return list(range(chunk // P))

        def slot_view(s, kc, chunk):
            return ring[:, s, 0:kc * chunk].rearrange("p (c n) -> p c n", c=kc)

        @block.sync
        def _(sp):
            for kind, aT, w, chunk, out, pairs, base in plan():
                kc = aT.shape[1]

                def load(i):
                    for s in range(2):
                        n = base + 2 * i + s
                        wait(sp, chunk_done, n - 1)
                        src = w[:, ds((2 * i + s) * chunk, chunk)].rearrange("(c p) n -> p c n", p=P)
                        sp.dma_start(slot_view(s, kc, chunk), src).then_inc(landed[s], 16)
                load(0)
                k.copy_some(sp, COPIES_PER_JOB)
                if pairs > 1:
                    with sp.Fori(1, pairs) as i:
                        load(i)

        @block.tensor
        def _(pe):
            for kind, aT, w, chunk, out, pairs, base in plan():
                kc = aT.shape[1]

                def product(i):
                    for s in range(2):
                        n = base + 2 * i + s
                        pe.wait_ge(landed[s], (base // 2 + i) * 16 + 16)
                        wait(pe, bank_free, n - 1)
                        wv = slot_view(s, kc, chunk)
                        for j, part in enumerate(parts(kind, aT, chunk)):
                            for c in range(kc):
                                if kind == "tok":
                                    t0, rows = part
                                    mm = pe.matmul(k.ps[0:rows, 4 * s + j, 0:chunk], aT[:, c, t0:t0 + rows],
                                                   wv[:, c, :], start=(c == 0), stop=(c == kc - 1))
                                else:
                                    mm = pe.matmul(k.ps[:, 4 * s + j, 0:aT.shape[2]], wv[:, c, j * P:(j + 1) * P],
                                                   aT[:, c, :], start=(c == 0), stop=(c == kc - 1))
                        mm.then_inc(chunk_done, 1)
                repeat(pe, pairs, product)

        @block.scalar
        def _(act):
            for kind, aT, w, chunk, out, pairs, base in plan():

                def evacuate(i):
                    for s in range(2):
                        n = base + 2 * i + s
                        act.wait_ge(chunk_done, n + 1)
                        ps = parts(kind, aT, chunk)
                        for j, part in enumerate(ps):
                            if kind == "tok":
                                dst = out[0:part[1], j, ds((2 * i + s) * chunk, chunk)]
                                src = k.ps[0:part[1], 4 * s + j, 0:chunk]
                            else:
                                tn = aT.shape[2]
                                dst = out[:, ds(((2 * i + s) * len(ps) + j) * tn, tn)]
                                src = k.ps[:, 4 * s + j, 0:tn]
                            last = act.activation(dst, src, ACT.Copy)
                        last.then_inc(bank_free, 1)
                repeat(act, pairs, evacuate)


def norm_stage(k, name, g, b, y=None):
    nc = k.nc
    with ExitStack() as ctx:
        gain, shift = k.sb(ctx, name + "_gain", [P, D]), k.sb(ctx, name + "_shift", [P, D])
        stats = k.sb(ctx, name + "_stats", [P, 3, 2, 6])
        mv = k.sb(ctx, name + "_mean_var", [P, 3, 2])
        rstd = k.sb(ctx, name + "_rstd", [P, 3])
        landed, chain, var_ready = k.sem(name + "_landed"), k.sem(name + "_chain"), k.sem(name + "_var")
        root_ready, x_ready = k.sem(name + "_root"), k.sem(name + "_x")
        turned, bank_free, stored = k.sem(name + "_turned"), k.sem(name + "_free"), k.sem(name + "_stored")
        block = ctx.enter_context(k.block())

        @block.sync
        def _(sp):
            for dst, src in ((gain, g), (shift, b)):
                sp.dma_start(dst[:, :], bass.AP(src.tensor, src.offset, [[0, P], [1, D]])).then_inc(landed, 16)
            if y is not None:
                for i, (t0, n) in enumerate(TILES):
                    sp.wait_ge(x_ready, i + 1)
                    sp.dma_start(y[i], k.x[0:n, i, :]).then_inc(stored, 16)
                sp.wait_ge(stored, 16 * len(TILES))

        @block.vector
        def _(dve):
            count = 0
            for i, (_, n) in enumerate(TILES):
                dve.scalar_tensor_tensor(out=k.x[0:n, i, :], in0=k.x[0:n, i, :], scalar=ALPHA, in1=k.h[0:n, i, :],
                                         op0=ALU.mult, op1=ALU.add).then_inc(chain, 1)
            count += 3
            for i, (_, n) in enumerate(TILES):
                dve.wait_ge(chain, i + 1)
                for half in range(2):
                    dve.bn_stats(out=stats[0:n, i, half, :],
                                 in_=k.x[0:n, i, half * 512:(half + 1) * 512]).then_inc(chain, 1)
            count += 6
            for i, (_, n) in enumerate(TILES):
                dve.wait_ge(chain, 3 + 2 * (i + 1))
                dve.bn_aggr(out=mv[0:n, i, :], in_=stats[0:n, i, :, :]).then_inc(chain, 1)
            count += 3
            for i, (_, n) in enumerate(TILES):
                dve.wait_ge(chain, 9 + i + 1)
                dve.tensor_scalar(out=rstd[0:n, i:i + 1], in0=mv[0:n, i, 1:2], scalar1=EPS, scalar2=None,
                                  op0=ALU.add).then_inc(var_ready, 1)
            for i, (_, n) in enumerate(TILES):
                dve.wait_ge(root_ready, i + 1)
                dve.reciprocal(rstd[0:n, i:i + 1], rstd[0:n, i:i + 1]).then_inc(chain, 1)
            count += 3
            dve.wait_ge(chain, count)
            for i, (_, n) in enumerate(TILES):
                dve.tensor_scalar(out=k.x[0:n, i, :], in0=k.x[0:n, i, :], scalar1=mv[0:n, i, 0:1],
                                  scalar2=rstd[0:n, i:i + 1], op0=ALU.subtract, op1=ALU.mult).then_inc(chain, 1)
            dve.wait_ge(landed, 32)
            for i, (_, n) in enumerate(TILES):
                dve.wait_ge(chain, count + i + 1)
                dve.tensor_tensor(out=k.x[0:n, i, :], in0=k.x[0:n, i, :], in1=gain[0:n, :],
                                  op=ALU.mult).then_inc(chain, 1)
            for i, (_, n) in enumerate(TILES):
                dve.wait_ge(chain, count + 3 + i + 1)
                dve.tensor_tensor(out=k.x[0:n, i, :], in0=k.x[0:n, i, :], in1=shift[0:n, :],
                                  op=ALU.add).then_inc(x_ready, 1)

        @block.scalar
        def _(act):
            for i, (_, n) in enumerate(TILES):
                act.wait_ge(var_ready, i + 1)
                act.activation(rstd[0:n, i:i + 1], rstd[0:n, i:i + 1], ACT.Sqrt).then_inc(root_ready, 1)
            if y is None:
                for n2 in range(6):
                    i, half = divmod(n2, 2)
                    t0, n = TILES[i]
                    act.wait_ge(turned, n2 + 1)
                    bank = k.ps[:, n2 % 4, :].rearrange("p (j t) -> p j t", j=4)
                    act.activation(k.xT[:, half * 4:half * 4 + 4, t0:t0 + n], bank[:, :, 0:n],
                                   ACT.Copy).then_inc(bank_free, 1)

        @block.tensor
        def _(pe):
            if y is None:
                for n2 in range(6):
                    i, half = divmod(n2, 2)
                    _, n = TILES[i]
                    pe.wait_ge(x_ready, i + 1)
                    wait(pe, bank_free, n2 - 3)
                    for j in range(4):
                        c = half * 4 + j
                        last = pe.transpose(k.ps[:, n2 % 4, j * P:j * P + n], k.x[0:n, i, c * P:(c + 1) * P],
                                            k.ident[0:n, 0:n])
                    last.then_inc(turned, 1)


def attend_prompt(k, name, units, cols, scale, mask_scales, out_n=P):
    nc = k.nc
    with ExitStack() as ctx:
        s = k.sb(ctx, name + "_s", [P, 2, cols])
        p = k.sb(ctx, name + "_p", [P, 2, cols])
        pT = k.sb(ctx, name + "_pT", [P, cols // P, P])
        stat = k.sb(ctx, name + "_stat", [P, 2, 4])
        scored, s_read, max_ready = k.sem(name + "_scored"), k.sem(name + "_s_read"), k.sem(name + "_max")
        exp_done, p_ready, chain = k.sem(name + "_exp"), k.sem(name + "_p_ready"), k.sem(name + "_chain")
        turned, pT_ready = k.sem(name + "_turned"), k.sem(name + "_pT_ready")
        o_ready, o_taken = k.sem(name + "_o_ready"), k.sem(name + "_o_taken")
        block = ctx.enter_context(k.block())
        U = len(units)
        psf = k.ps[:, :, :].rearrange("p b n -> p (b n)")

        def width(u):
            return sum(n for _, n, _ in units[u]["scores"])

        @block.tensor
        def _(pe):
            def scores(u):
                wait(pe, s_read, u - 1)
                for c0, n, prods in units[u]["scores"]:
                    for m, (lhsT, rhs) in enumerate(prods):
                        mm = pe.matmul(psf[:, (u % 2) * 1024 + c0:(u % 2) * 1024 + c0 + n], lhsT, rhs,
                                       start=(m == 0), stop=(m == len(prods) - 1))
                mm.then_inc(scored, 1)

            def values(u):
                pe.wait_ge(p_ready, u + 1)
                wait(pe, pT_ready, u)
                keys = units[u]["keys"]
                for j, (c0, _) in enumerate(keys):
                    mm = pe.transpose(psf[:, 2048 + j * P:2048 + (j + 1) * P], p[:, u % 2, c0:c0 + P], k.ident[:, :])
                mm.then_inc(turned, 1)
                pe.wait_ge(pT_ready, u + 1)
                wait(pe, o_taken, u - 1)
                for b in range(len(units[u]["outs"])):
                    for j, (_, vs) in enumerate(keys):
                        mm = pe.matmul(k.ps[:, 6 + u % 2, b * P:(b + 1) * P], vs[b], pT[:, j, :],
                                       start=(j == 0), stop=(j == len(keys) - 1))
                mm.then_inc(o_ready, 1)

            scores(0)
            for u in range(U):
                if u + 1 < U:
                    scores(u + 1)
                values(u)

        @block.vector
        def _(dve):
            link = Chain(dve, chain)

            def maxima(u):
                w = width(u)
                src, dst = psf[:, (u % 2) * 1024:(u % 2) * 1024 + w], s[:, u % 2, 0:w]
                dve.wait_ge(scored, u + 1)
                wait(dve, exp_done, u - 1)
                dve.scalar_tensor_tensor(out=dst, in0=src, scalar=mask_scales, in1=units[u]["bias"],
                                         op0=ALU.mult, op1=ALU.add).then_inc(s_read, 1) \
                    if units[u]["bias"] is not None else \
                    dve.tensor_copy(dst, src).then_inc(s_read, 1)
                dve.wait_ge(s_read, u + 1)
                link(dve.reduce_max(stat[:, u % 2, 0:1], dst, AX))
                dve.tensor_scalar(out=stat[:, u % 2, 1:2], in0=stat[:, u % 2, 0:1], scalar1=-scale, scalar2=None,
                                  op0=ALU.mult).then_inc(max_ready, 1)

            def finish(u):
                w = width(u)
                dve.wait_ge(exp_done, u + 1)
                link(dve.reciprocal(stat[:, u % 2, 3:4], stat[:, u % 2, 2:3]))
                dve.tensor_scalar(out=p[:, u % 2, 0:w], in0=p[:, u % 2, 0:w], scalar1=stat[:, u % 2, 3:4],
                                  scalar2=None, op0=ALU.mult).then_inc(p_ready, 1)

            def take(u):
                dve.wait_ge(o_ready, u + 1)
                for b, dst in enumerate(units[u]["outs"]):
                    last = dve.tensor_copy(dst, k.ps[:, 6 + u % 2, b * P:(b + 1) * P])
                last.then_inc(o_taken, 1)

            maxima(0)
            for u in range(U):
                finish(u)
                if u + 1 < U:
                    maxima(u + 1)
                take(u)

        @block.scalar
        def _(act):
            def exps(u):
                w = width(u)
                act.wait_ge(max_ready, u + 1)
                wait(act, turned, u - 1)
                act.activation(p[:, u % 2, 0:w], s[:, u % 2, 0:w], ACT.Exp, bias=stat[:, u % 2, 1:2], scale=scale,
                               accum_out=stat[:, u % 2, 2:3]).then_inc(exp_done, 1)

            exps(0)
            for u in range(U):
                if u + 1 < U:
                    exps(u + 1)
                act.wait_ge(turned, u + 1)
                wait(act, o_ready, u)
                nk = len(units[u]["keys"])
                act.activation(pT[:, 0:nk, :].rearrange("p a b -> p (a b)"), psf[:, 2048:2048 + nk * P],
                               ACT.Copy).then_inc(pT_ready, 1)


def attend_sample(k, name, a):
    nc = k.nc
    with ExitStack() as ctx:
        s = k.sb(ctx, name + "_s", [P, a["cols"]])
        p = k.sb(ctx, name + "_p", [P, a["cols"]])
        blocks = a["blocks"]
        NK = len(blocks)
        pT = k.sb(ctx, name + "_pT", [P, NK, P])
        stat = k.sb(ctx, name + "_stat", [P, 6])
        o_tok = k.sb(ctx, name + "_o_tok", [P, a["out_cols"]])
        parts = a["key_parts"]
        k_landed = [[k.sem(f"{name}_k_landed{i}_{j}") for j in range(len(parts))] for i in range(2)]
        v_landed = [k.sem(f"{name}_v_landed{i}") for i in range(2)]
        setup_done, staged = k.sem(name + "_setup"), k.sem(name + "_staged")
        turned, kT_ready = k.sem(name + "_turned"), k.sem(name + "_kT_ready")
        scored, s_taken, max_ready = k.sem(name + "_scored"), k.sem(name + "_s_taken"), k.sem(name + "_max")
        exp_done, p_ready, chain = k.sem(name + "_exp"), k.sem(name + "_p_ready"), k.sem(name + "_chain")
        p_turned, pT_ready = k.sem(name + "_p_turned"), k.sem(name + "_pT_ready")
        o_ready, o_taken = k.sem(name + "_o_ready"), k.sem(name + "_o_taken")
        o_turned, out_done = k.sem(name + "_o_turned"), k.sem(name + "_out_done")
        begun_pe = k.sem(name + "_begun_pe")
        block = ctx.enter_context(k.block())
        G, C = len(a["groups"]), len(a["chunks"])
        per_bank = 512 // P
        pgroups = [list(range(i, min(i + per_bank, NK))) for i in range(0, NK, per_bank)]
        PG = len(pgroups)
        NS = a["n_stage"]
        PAIRS = DEC_B // 2

        def bank(first, n, slot, count):
            return first + (n if count % 2 == 0 else n + slot) % 2

        @block.sync
        def _(sp):
            def load_keys(u, slot):
                ready = [a["prepare_keys"](sp, u, j) if a.get("prepare_keys") else None for j in range(len(parts))]
                for j in range(len(parts)):
                    if a["shared"]:
                        wait(sp, o_ready, u - 1)
                    elif isinstance(u, int) and u < a["slots"]:
                        pass
                    else:
                        sp.wait_ge(turned, G * (u - a["slots"]) + sum(parts[:j + 1]))
                    a["load_keys"](sp, u, slot, j, k_landed[slot][j], ready[j])

            def body(i, last):
                for slot in range(2):
                    u = 2 * i + slot
                    if not (last and slot == 1):
                        load_keys(u + 1, 1 - slot)
                    wait(sp, o_ready, u + 1 - a["slots"])
                    a["load_values"](sp, u, slot, v_landed[slot])

            if a.get("setup_loads"):
                a["setup_loads"](sp)
            load_keys(0, 0)
            repeat_ends(sp, PAIRS, body)

        @block.gpsimd
        def _(pool):
            if a.get("setup_pool"):
                a["setup_pool"](pool, setup_done)

            def body(i):
                for slot in range(2):
                    u = 2 * i + slot
                    wait(pool, scored, C * (u - 1))
                    a["stage"](pool, u, slot, staged)
            repeat(pool, PAIRS, body)

        @block.tensor
        def _(pe):
            def turn_keys(u, half, slot):
                starts = [sum(parts[:j]) for j in range(len(parts))]
                for g, blocks in enumerate(a["groups"]):
                    if g in starts:
                        j = starts.index(g)
                        pe.wait_ge(k_landed[slot][j], (half + 1) * a["key_dmas"][j] * 16)
                    wait(pe, kT_ready, G * u + g - 1)
                    for j, (src, w) in enumerate(blocks):
                        mm = pe.transpose(k.ps[0:w, bank(0, g, slot, G), j * P:(j + 1) * P], src(slot), k.ident[:, :])
                    mm.then_inc(turned, 1)

            def score(u, slot):
                pe.wait_ge(staged, NS * (u + 1))
                for c, (c0, n, prods) in enumerate(a["chunks"]):
                    pe.wait_ge(kT_ready, G * u + min(G, a["groups_for"](c0 + n)))
                    wait(pe, s_taken, C * u + c - 1)
                    n_terms = len(prods[0][2])
                    for j in range(n_terms):
                        for m0, m, terms in prods:
                            lhsT, rhs = terms[j]
                            mm = pe.matmul(k.ps[m0:m0 + m, bank(2, c, slot, C), 0:n], lhsT(slot), rhs(slot),
                                           start=(j == 0), stop=(j == n_terms - 1))
                    mm.then_inc(scored, 1)

            def turn_out(u):
                wait(pe, out_done, u)
                pe.wait_ge(o_taken, u + 1)
                for j in range(0, a["out_cols"], P):
                    mm = pe.transpose(k.ps[:, 7, j:j + P], o_tok[:, j:j + P], k.ident[:, :])
                mm.then_inc(o_turned, 1)

            def body(i, last):
                for slot in range(2):
                    u = 2 * i + slot
                    if not (last and slot == 1):
                        turn_keys(u + 1, i + slot, 1 - slot)
                    if not (isinstance(u, int) and u == 0):
                        turn_out(u - 1)
                    if not (last and slot == 1):
                        score(u + 1, 1 - slot)
                    wait_apart(pe, p_ready, u + 1, begun_pe)
                    for g, ks in enumerate(pgroups):
                        wait_apart(pe, pT_ready, PG * u + g - 1, begun_pe)
                        for j, kk in enumerate(ks):
                            c0, n = blocks[kk]
                            mm = pe.transpose(k.ps[0:n, bank(4, g, slot, PG), j * P:(j + 1) * P], p[:, c0:c0 + n],
                                              k.ident[:, :])
                        mm.then_inc(p_turned, 1)
                    pe.wait_ge(pT_ready, PG * (u + 1))
                    wait(pe, o_taken, u)
                    pe.wait_ge(v_landed[slot], (i + 1) * a["value_dmas"] * 16)
                    seen = set()
                    terms = a["value_terms"]
                    lasts = {t[0]: n for n, t in enumerate(terms)}
                    for n, (m0, m, cols, kk, rows, col, v) in enumerate(terms):
                        mm = pe.matmul(k.ps[m0:m0 + m, 6, 0:cols], pT[0:rows, kk, col:col + m], v(slot),
                                       start=m0 not in seen, stop=lasts[m0] == n)
                        seen.add(m0)
                    mm.then_inc(o_ready, 1)

            if a["setup_count"]:
                pe.wait_ge(setup_done, a["setup_count"])
            turn_keys(0, 0, 0)
            score(0, 0)
            repeat_ends(pe, PAIRS, body)
            turn_out(DEC_B - 1)

        @block.scalar
        def _(act):
            def take_keys(u, slot):
                for g in range(G):
                    act.wait_ge(turned, G * u + g + 1)
                    for dst, src in a["key_copies"](g, k.ps[:, bank(0, g, slot, G), :]):
                        last = act.activation(dst, src, ACT.Copy)
                    last.then_inc(kT_ready, 1)

            def exponential(u):
                act.wait_ge(max_ready, u + 1)
                wait(act, p_turned, PG * u)
                act.activation(p[:, :], s[:, :], ACT.Exp, bias=stat[:, 1:2], scale=a["scale"],
                               accum_out=stat[:, 2:3]).then_inc(exp_done, 1)

            def body(i, last):
                for slot in range(2):
                    u = 2 * i + slot
                    more = not (last and slot == 1)
                    if more:
                        act.wait_ge(scored, C * (u + 1))
                        take_keys(u + 1, 1 - slot)
                    wait(act, o_ready, u)
                    for g, ks in enumerate(pgroups):
                        act.wait_ge(p_turned, PG * u + g + 1)
                        b = bank(4, g, slot, PG)
                        full = [kk for kk in ks if blocks[kk][1] == P]
                        if full:
                            nf = len(full)
                            src = k.ps[:, b, 0:nf * P].rearrange("p (a b) -> p a b", a=nf)
                            ins = act.activation(pT[:, full[0]:full[0] + nf, :], src, ACT.Copy)
                        if len(full) < len(ks):
                            j, nr = len(full), len(ks) - len(full)
                            rows = blocks[ks[j]][1]
                            src = k.ps[0:rows, b, j * P:(j + nr) * P].rearrange("p (a b) -> p a b", a=nr)
                            ins = act.activation(pT[0:rows, ks[j]:ks[j] + nr, :], src, ACT.Copy)
                        ins.then_inc(pT_ready, 1)
                    if more:
                        exponential(u + 1)

            take_keys(0, 0)
            exponential(0)
            repeat_ends(act, PAIRS, body)

        @block.vector
        def _(dve):
            def swapped(chained, dst, src):
                chained(dve.tensor_copy(stat[0:64, dst], stat[64:128, src]))
                chained(dve.tensor_copy(stat[64:128, dst], stat[0:64, src]))

            def maxima(u, slot):
                wait(dve, exp_done, u)
                for c, (c0, n, _) in enumerate(a["chunks"]):
                    dve.wait_ge(scored, C * u + c + 1)
                    dst, src = s[:, c0:c0 + n], k.ps[:, bank(2, c, slot, C), 0:n]
                    bias = a["bias"](c0, n)
                    if bias is None:
                        dve.tensor_copy(dst, src).then_inc(s_taken, 1)
                    else:
                        dve.scalar_tensor_tensor(out=dst, in0=src, scalar=a["bias_scale"], in1=bias,
                                                 op0=ALU.mult, op1=ALU.add).then_inc(s_taken, 1)
                dve.wait_ge(s_taken, C * (u + 1))
                chained = Chain(dve, chain, UNIT * u)
                chained(dve.reduce_max(stat[:, 0:1], s[:, :], AX))
                if a["halves"]:
                    swapped(chained, slice(4, 5), slice(0, 1))
                    chained(dve.tensor_max(stat[:, 0:1], stat[:, 0:1], stat[:, 4:5]))
                dve.tensor_scalar(out=stat[:, 1:2], in0=stat[:, 0:1], scalar1=-a["scale"], scalar2=None,
                                  op0=ALU.mult).then_inc(max_ready, 1)

            MAX_STEPS, UNIT = (4, 8) if a["halves"] else (1, 2)

            def put_out(u):
                dve.wait_ge(o_turned, u + 1)
                dst, src = a["out"](u, k.ps[:, 7, :])
                dve.tensor_copy(dst, src).then_inc(out_done, 1)

            def body(i, last):
                for slot in range(2):
                    u = 2 * i + slot
                    dve.wait_ge(exp_done, u + 1)
                    chained = Chain(dve, chain, UNIT * u + MAX_STEPS)
                    if a["halves"]:
                        swapped(chained, slice(5, 6), slice(2, 3))
                        chained(dve.tensor_add(stat[:, 2:3], stat[:, 2:3], stat[:, 5:6]))
                    chained(dve.reciprocal(stat[:, 3:4], stat[:, 2:3]))
                    dve.tensor_scalar(out=p[:, :], in0=p[:, :], scalar1=stat[:, 3:4], scalar2=None,
                                      op0=ALU.mult).then_inc(p_ready, 1)
                    if not (isinstance(u, int) and u == 0):
                        put_out(u - 1)
                    if not (last and slot == 1):
                        maxima(u + 1, 1 - slot)
                    dve.wait_ge(o_ready, u + 1)
                    wait(dve, o_turned, u)
                    dve.tensor_copy(o_tok[:, :], k.ps[:, 6, 0:a["out_cols"]]).then_inc(o_taken, 1)

            if a["setup_count"]:
                dve.wait_ge(setup_done, a["setup_count"])
            maxima(0, 0)
            repeat_ends(dve, PAIRS, body)
            put_out(DEC_B - 1)


def latent_stage(k, e):
    nc, io = k.nc, k.io
    with ExitStack() as ctx:
        lat = e["latent"]
        gq, gkv = k.sb(ctx, "lt_gq", [P, Q_LORA]), k.sb(ctx, "lt_gkv", [P, KV_LORA])
        cs = k.sb(ctx, "lt_cs", [P, 3, 2, 16])
        sq = k.sb(ctx, "lt_sq", [P, 256])
        ms = k.sb(ctx, "lt_ms", [P, 3, 2])
        cq = k.sb(ctx, "lt_cq", [P, 3, Q_LORA])
        rot = k.sb(ctx, "lt_rot", [P, 3, 4, 16])
        landed, squares, chain = k.sem("lt_landed"), k.sem("lt_squares"), k.sem("lt_chain")
        ms_ready, root_ready, rows_ready = k.sem("lt_ms_ready"), k.sem("lt_root"), k.sem("lt_rows")
        turned, bank_free, stored = k.sem("lt_turned"), k.sem("lt_free"), k.sem("lt_stored")
        block = ctx.enter_context(k.block())
        rows = e["rows"]

        @block.sync
        def _(sp):
            for dst, src in ((gq, io["mla_q_norm"]), (gkv, io["mla_kv_norm"])):
                sp.dma_start(dst[:, :], bass.AP(src.tensor, src.offset, [[0, P], [1, 256]])).then_inc(landed, 16)
            sp.dma_start(cs[:, 0:2, :, :], io["rope_tok"][0:SEQ].rearrange("(i p) a c -> p i a c", p=P)).then_inc(landed, 16)
            sp.dma_start(cs[0:64, 2, :, :], io["rope_tok"][SEQ:T]).then_inc(landed, 16)
            sp.wait_ge(rows_ready, 3)
            sp.dma_start(io["mla_rows_prompt"][0, 0].rearrange("(i p) c -> p i c", p=P), rows[:, 0:2, :]).then_inc(stored, 16)
            sp.dma_start(io["mla_rows_sample"][0].rearrange("b s c -> (b s) c"), rows[0:64, 2, :]).then_inc(stored, 16)
            sp.wait_ge(stored, 32)

        @block.scalar
        def _(act):
            n2 = 0
            for i, (_, n) in enumerate(TILES):
                for j in range(2):
                    wait(act, squares, n2)
                    act.activation(sq[0:n, :], lat[0:n, i, j * 256:(j + 1) * 256], ACT.Square,
                                   accum_out=ms[0:n, i, j:j + 1]).then_inc(squares, 1)
                    n2 += 1
            act.wait_ge(ms_ready, 3)
            for i, (_, n) in enumerate(TILES):
                act.activation(ms[0:n, i, :], ms[0:n, i, :], ACT.Sqrt).then_inc(root_ready, 1)
            for i, (t0, n) in enumerate(TILES):
                act.wait_ge(turned, 2 * i + 1)
                act.activation(e["cqT"][:, :, t0:t0 + n],
                               k.ps[:, 0, 0:256].rearrange("p (a t) -> p a t", a=2)[:, :, 0:n], ACT.Copy).then_inc(bank_free, 1)
                act.wait_ge(turned, 2 * i + 2)
                act.activation(e["ckvT"][:, :, t0:t0 + n],
                               k.ps[:, 1, 0:256].rearrange("p (a t) -> p a t", a=2)[:, :, 0:n], ACT.Copy).then_inc(bank_free, 1)
                act.activation(e["krT"][:, t0:t0 + n], k.ps[0:ROPE, 1, 256:256 + n], ACT.Copy).then_inc(bank_free, 1)

        @block.vector
        def _(dve):
            dve.wait_ge(squares, 6)
            for i, (_, n) in enumerate(TILES):
                dve.tensor_scalar(out=ms[0:n, i, :], in0=ms[0:n, i, :], scalar1=1.0 / 256, scalar2=EPS,
                                  op0=ALU.mult, op1=ALU.add).then_inc(ms_ready, 1)
            dve.wait_ge(landed, 64)
            link = Chain(dve, chain)
            for i, (_, n) in enumerate(TILES):
                dve.wait_ge(root_ready, i + 1)
                link(dve.reciprocal(ms[0:n, i, :], ms[0:n, i, :]))
                dve.scalar_tensor_tensor(out=cq[0:n, i, :], in0=lat[0:n, i, 0:256], scalar=ms[0:n, i, 0:1],
                                         in1=gq[0:n, :], op0=ALU.mult, op1=ALU.mult)
                dve.scalar_tensor_tensor(out=rows[0:n, i, 0:256], in0=lat[0:n, i, 256:512], scalar=ms[0:n, i, 1:2],
                                         in1=gkv[0:n, :], op0=ALU.mult, op1=ALU.mult)
                x1, x2 = lat[0:n, i, 512:528], lat[0:n, i, 528:544]
                cos, sin = cs[0:n, i, 0, :], cs[0:n, i, 1, :]
                dve.tensor_tensor(out=rot[0:n, i, 0, :], in0=x1, in1=cos, op=ALU.mult)
                dve.tensor_tensor(out=rot[0:n, i, 1, :], in0=x2, in1=sin, op=ALU.mult)
                dve.tensor_tensor(out=rot[0:n, i, 2, :], in0=x2, in1=cos, op=ALU.mult)
                link(dve.tensor_tensor(out=rot[0:n, i, 3, :], in0=x1, in1=sin, op=ALU.mult))
                dve.tensor_tensor(out=rows[0:n, i, 256:272], in0=rot[0:n, i, 0, :], in1=rot[0:n, i, 1, :], op=ALU.subtract)
                dve.tensor_tensor(out=rows[0:n, i, 272:288], in0=rot[0:n, i, 2, :], in1=rot[0:n, i, 3, :],
                                  op=ALU.add).then_inc(rows_ready, 1)

        @block.tensor
        def _(pe):
            for i, (_, n) in enumerate(TILES):
                pe.wait_ge(rows_ready, i + 1)
                wait(pe, bank_free, 3 * i)
                for j in range(2):
                    mm = pe.transpose(k.ps[:, 0, j * P:j * P + n], cq[0:n, i, j * P:(j + 1) * P], k.ident[0:n, 0:n])
                mm.then_inc(turned, 1)
                for j in range(2):
                    pe.transpose(k.ps[:, 1, j * P:j * P + n], rows[0:n, i, j * P:(j + 1) * P], k.ident[0:n, 0:n])
                pe.transpose(k.ps[0:ROPE, 1, 256:256 + n], rows[0:n, i, 256:288], k.ident[0:n, 0:n]).then_inc(turned, 1)


def window_outputs_stage(k, kv):
    nc, io = k.nc, k.io
    with ExitStack() as ctx:
        stored = k.sem("wo_stored")
        block = ctx.enter_context(k.block())

        @block.sync
        def _(sp):
            n = 0
            sp.dma_start(io["kv_new"], kv[0:64, 2, :]).then_inc(stored, 16)
            n += 1
            for g, (w, _) in enumerate(SWA_GROUPS):
                for c in range(2):
                    cols = slice((c * 3 + g) * GW, (c * 3 + g + 1) * GW)
                    dst = io[f"swa_prompt{g}"][0, 0, :, c].rearrange("w h d -> w (h d)")
                    for i in range(2):
                        r = w - SEQ + i * P
                        if r >= 0:
                            sp.dma_start(dst[r:r + P, :], kv[:, i, cols]).then_inc(stored, 16)
                            n += 1
                    for b in range(DEC_B):
                        dst_s = io[f"swa_sample{g}"][0, b, w - DEC_S:w, c].rearrange("w h d -> w (h d)")
                        sp.dma_start(dst_s, kv[8 * b:8 * b + 8, 2, cols]).then_inc(stored, 16)
                        n += 1
            sp.wait_ge(stored, 16 * n)


def query_stage(k, e):
    nc, io = k.nc, k.io
    with ExitStack() as ctx:
        wuq = k.sb(ctx, "qs_wuq", [P, 2, MLA_H * (NOPE + ROPE)])
        wsw = k.sb(ctx, "qs_wsw", [P, 2, MLA_H, ROPE])
        wuk = k.sb(ctx, "qs_wuk", [P, 2, MLA_H * NOPE])
        wukT = k.sb(ctx, "qs_wukT", [P, 4, KV_LORA])
        nopeT = k.sb(ctx, "qs_nopeT", [P, 4, T])
        csT = k.sb(ctx, "qs_csT", [ROPE, 2, T])
        rot = k.sb(ctx, "qs_rot", [ROPE, 2, T])
        landed, turned, uk_ready = k.sem("qs_landed"), k.sem("qs_turned"), k.sem("qs_uk")
        made, taken = k.sem("qs_made"), k.sem("qs_taken")
        rmade, rchain, rtaken = k.sem("qs_rope_made"), k.sem("qs_rope_chain"), k.sem("qs_rope_taken")
        lmade, ltaken = k.sem("qs_lat_made"), k.sem("qs_lat_taken")
        block = ctx.enter_context(k.block())
        cqT = e["cqT"]
        uq = io["mla_w_uq"][0].rearrange("(c p) (h n) -> p c h n", p=P, h=MLA_H)

        @block.sync
        def _(sp):
            sp.dma_start(wuk[:, :, :], io["mla_w_uk"][0].rearrange("(c p) h n -> p c (h n)", p=P)).then_inc(landed, 16)
            sp.dma_start(wuq[:, :, :], io["mla_w_uq"][0].rearrange("(c p) n -> p c n", p=P)).then_inc(landed, 16)
            for c in range(2):
                sp.dma_start(wsw[:, c, :, 0:16], uq[:, c, :, NOPE + 16:NOPE + 32]).then_inc(landed, 16)
                sp.dma_start(wsw[:, c, :, 16:32], uq[:, c, :, NOPE:NOPE + 16]).then_inc(landed, 16)
            sp.dma_start(csT[:, :, :], io["rope_feat"]).then_inc(landed, 16)

        wq4 = wuq[:, :, :].rearrange("p c (h n) -> p c h n", h=MLA_H)

        @block.tensor
        def _(pe):
            pe.wait_ge(landed, 16 * 7)
            for pair in range(4):
                wait(pe, uk_ready, pair - 1)
                for c in range(2):
                    mm = pe.transpose(k.ps[:, pair % 2, c * P:(c + 1) * P], wuk[:, c, pair * P:(pair + 1) * P], k.ident[:, :])
                mm.then_inc(turned, 1)
            for pair in range(4):
                wait(pe, taken, pair - 1)
                for half in range(2):
                    for c in range(2):
                        mm = pe.matmul(k.ps[64 * half:64 * half + 64, 2 + pair % 2, 0:T],
                                       wq4[:, c, 2 * pair + half, 0:NOPE], cqT[:, c, :], start=(c == 0), stop=(c == 1))
                mm.then_inc(made, 1)
            for h in range(MLA_H):
                wait(pe, rtaken, h - 1)
                for v in range(2):
                    for c in range(2):
                        lhsT = wq4[:, c, h, NOPE:NOPE + ROPE] if v == 0 else wsw[:, c, h, :]
                        mm = pe.matmul(k.ps[0:ROPE, 4 + 2 * (h % 2) + v, 0:T], lhsT, cqT[:, c, :],
                                       start=(c == 0), stop=(c == 1))
                mm.then_inc(rmade, 1)
            pe.wait_ge(taken, 4)
            pe.wait_ge(uk_ready, 4)
            for h in range(MLA_H):
                rows = slice(64 * (h % 2), 64 * (h % 2) + 64)
                for c in range(2):
                    n = 2 * h + c
                    wait(pe, ltaken, n - 1)
                    pe.matmul(k.ps[:, n % 2, 0:T], wukT[rows, h // 2, c * P:(c + 1) * P], nopeT[rows, h // 2, :],
                              start=True, stop=True).then_inc(lmade, 1)

        @block.scalar
        def _(act):
            for pair in range(4):
                act.wait_ge(turned, pair + 1)
                act.activation(wukT[:, pair, :], k.ps[:, pair % 2, 0:256], ACT.Copy).then_inc(uk_ready, 1)
            for pair in range(4):
                act.wait_ge(made, pair + 1)
                act.activation(nopeT[:, pair, :], k.ps[:, 2 + pair % 2, 0:T], ACT.Copy).then_inc(taken, 1)
            for n in range(2 * MLA_H):
                h, c = divmod(n, 2)
                act.wait_ge(lmade, n + 1)
                act.activation(e["qlatT"][:, c, h, :], k.ps[:, n % 2, 0:T], ACT.Copy).then_inc(ltaken, 1)

        @block.vector
        def _(dve):
            dve.wait_ge(landed, 16 * 7)
            for h in range(MLA_H):
                dve.wait_ge(rmade, h + 1)
                wait(dve, rtaken, h)
                for v in range(2):
                    last = dve.tensor_tensor(out=rot[:, v, :], in0=k.ps[0:ROPE, 4 + 2 * (h % 2) + v, 0:T],
                                             in1=csT[:, v, :], op=ALU.mult)
                last.then_inc(rchain, 1)
                dve.wait_ge(rchain, h + 1)
                dve.tensor_tensor(out=e["qrT"][:, h, :], in0=rot[:, 0, :], in1=rot[:, 1, :],
                                  op=ALU.add).then_inc(rtaken, 1)


def mla_values_stage(k, e):
    nc, io = k.nc, k.io
    with ExitStack() as ctx:
        wuv = k.sb(ctx, "mv_wuv", [P, 2, MLA_H, D_V])
        landed, made, taken = k.sem("mv_landed"), k.sem("mv_made"), k.sem("mv_taken")
        block = ctx.enter_context(k.block())

        @block.sync
        def _(sp):
            sp.dma_start(wuv[:, :, :, :], io["mla_w_uv"][0].rearrange("(c p) h n -> p c h n", p=P)).then_inc(landed, 16)

        @block.tensor
        def _(pe):
            pe.wait_ge(landed, 16)
            for pair in range(4):
                for half in range(2):
                    for c in range(2):
                        mm = pe.matmul(k.ps[64 * half:64 * half + 64, pair, 0:T], wuv[:, c, 2 * pair + half, :],
                                       e["olatT"][:, c, 2 * pair + half, :], start=(c == 0), stop=(c == 1))
                mm.then_inc(made, 1)

        @block.scalar
        def _(act):
            for pair in range(4):
                act.wait_ge(made, pair + 1)
                act.activation(e["oT"][:, pair, :], k.ps[:, pair, 0:T], ACT.Copy).then_inc(taken, 1)


def bias_stage(k, e):
    nc, io = k.nc, k.io
    with ExitStack() as ctx:
        hot = k.sb(ctx, "bs_hot", [N_BUCKETS + 1, 3, N_DIST])
        rel = k.sb(ctx, "bs_rel", [N_BUCKETS + 1, 12])
        byd = k.sb(ctx, "bs_by_dist", [SWA_H, 3, N_DIST])
        filled, landed, made, taken = k.sem("bs_filled"), k.sem("bs_landed"), k.sem("bs_made"), k.sem("bs_taken")
        stored, spread, zeroed, tabled = k.sem("bs_stored"), k.sem("bs_spread"), k.sem("bs_zeroed"), k.sem("bs_tabled")
        block = ctx.enter_context(k.block())
        chunks = [(c, min(512, N_DIST - c)) for c in range(0, N_DIST, 512)]
        by_dist, rep = io["bias_by_dist"], io["bias_rep"]
        Bp, Bs = e["bias_p"], e["bias_s"]

        @block.gpsimd
        def _(pool):
            pool.memset(rel[:, :], DISALLOWED).then_inc(filled, 1)
            pool.memset(Bs[:, :], 0.0).then_inc(zeroed, 1)

        @block.sync
        def _(sp):
            sp.dma_start(hot[:, :, :], io["bucket_hot"]).then_inc(landed, 16)
            sp.wait_ge(filled, 1)
            sp.dma_start(rel[0:N_BUCKETS, :], io["rel_bias"]).then_inc(landed, 16)
            sp.wait_ge(taken, 3 * len(chunks))
            sp.dma_start(by_dist.rearrange("g h n -> h g n"), byd[:, :, :]).then_inc(stored, 16)
            sp.wait_ge(stored, 16)
            for g in range(3):
                src = bass.AP(by_dist.tensor, g * SWA_H * N_DIST + REP0, [[N_DIST, SWA_H], [0, P], [1, REP_N]])
                sp.dma_start(rep[g], src).then_inc(spread, 16)
            sp.wait_ge(zeroed, 1)
            for q in range(DEC_S):
                new = bass.AP(by_dist.tensor, DIST_TOP - q, [[N_DIST, SWA_H], [SWA_H * N_DIST, 3], [1, DEC_S]])
                sp.dma_start(Bs[q:P:PAD, SWA_CACHED:SWA_KEYS].rearrange("p (g i) -> p g i", g=3), new).then_inc(tabled, 16)
                for g, (w, _) in enumerate(SWA_GROUPS):
                    base = g * SWA_H * N_DIST + DIST_TOP - w - q
                    if g < 2:
                        src = bass.AP(by_dist.tensor, base, [[N_DIST, SWA_H], [1, w]])
                        dst = Bs[q:P:PAD, g * P:g * P + w]
                    else:
                        src = bass.AP(by_dist.tensor, base, [[N_DIST, SWA_H], [16, P], [1, 8]])
                        dst = Bs[q:P:PAD, 5 * P:SWA_CACHED].rearrange("p (a i) -> p a i", i=8)
                    sp.dma_start(dst, src).then_inc(tabled, 16)
            sp.wait_ge(spread, 48)
            for g in range(3):
                for h in range(SWA_H):
                    for qb in range(2):
                        src = bass.AP(rep.tensor, (g * SWA_H + h) * P * REP_N + (DIST_TOP - REP0) - qb * P,
                                      [[REP_N - 1, P], [1, SEQ]])
                        sp.dma_start(Bp[:, h, qb, g, :], src).then_inc(tabled, 16)
            sp.wait_ge(tabled, 16 * (4 * DEC_S + 24))

        @block.tensor
        def _(pe):
            pe.wait_ge(landed, 32)
            n = 0
            for g in range(3):
                for c0, w in chunks:
                    wait(pe, taken, n - 3)
                    pe.matmul(k.ps[0:SWA_H, n % 4, 0:w], rel[:, 4 * g:4 * g + 4], hot[:, g, c0:c0 + w],
                              start=True, stop=True).then_inc(made, 1)
                    n += 1

        @block.scalar
        def _(act):
            n = 0
            for g in range(3):
                for c0, w in chunks:
                    act.wait_ge(made, n + 1)
                    act.activation(byd[:, g, c0:c0 + w], k.ps[0:SWA_H, n % 4, 0:w], ACT.Copy).then_inc(taken, 1)
                    n += 1


def turn_stage(k, name, jobs):
    nc = k.nc
    with ExitStack() as ctx:
        turned, taken = k.sem(name + "_turned"), k.sem(name + "_taken")
        block = ctx.enter_context(k.block())

        @block.tensor
        def _(pe):
            for n, (srcs, rows, dst) in enumerate(jobs):
                wait(pe, taken, n - 3)
                for j, src in enumerate(srcs):
                    mm = pe.transpose(k.ps[0:src.shape[1], n % 4, j * P:j * P + rows], src, k.ident[0:rows, 0:rows])
                mm.then_inc(turned, 1)

        @block.scalar
        def _(act):
            for n, (srcs, rows, dst) in enumerate(jobs):
                act.wait_ge(turned, n + 1)
                src = k.ps[0:srcs[0].shape[1], n % 4, :].rearrange("p (j t) -> p j t", j=4)[:, 0:len(srcs), 0:rows]
                act.activation(dst, src, ACT.Copy).then_inc(taken, 1)


def even_mixer(k):
    nc, io = k.nc, k.io
    w_in = io["attn_w_in"][0]
    first = Q_LORA + KV_LORA + ROPE
    with ExitStack() as ctx:
        e = {}
        e["oT"] = k.sb(ctx, "e_oT", [P, 8, T])
        with ExitStack() as c1:
            rows = e["rows"] = k.sb(c1, "e_rows", [P, 3, MLA_ROW])
            e["ckvT"] = k.sb(c1, "e_ckvT", [P, 2, T])
            e["krT"] = k.sb(c1, "e_krT", [ROPE, T])
            e["qlatT"] = k.sb(c1, "e_qlatT", [P, 2, MLA_H, T])
            e["qrT"] = k.sb(c1, "e_qrT", [ROPE, MLA_H, T])
            e["olatT"] = k.sb(c1, "e_olatT", [P, 2, MLA_H, T])
            with ExitStack() as c2:
                e["cqT"] = k.sb(c2, "e_cqT", [P, 2, T])
                e["latent"] = k.sb(c2, "e_latent", [P, 3, first])
                gemm_stage(k, "lat", [("tok", k.xT, w_in[:, 0:first], 272, e["latent"])])
                latent_stage(k, e)
                query_stage(k, e)
            with ExitStack() as c2:
                mask = k.sb(c2, "e_causal", [P, 2, SEQ])
                mla_prompt(k, e, mask)
            mla_sample(k, e)
            mla_values_stage(k, e)
        with ExitStack() as c1:
            swa_qT = k.sb(c1, "e_swa_qT", [P, 12, T])
            kT = k.sb(c1, "e_kT", [P, 12, T])
            e["bias_s"] = k.sb(c1, "e_bias_s", [P, SWA_KEYS])
            with ExitStack() as c2:
                kv = k.sb(c2, "e_kv", [P, 3, 6 * GW])
                gemm_stage(k, "win", [
                    ("tok", k.xT, w_in[:, first + 3 * GW:first + 9 * GW], 512, kv),
                    ("feat", k.xT, w_in[:, first:first + 3 * GW], 384, swa_qT[:, :, :].rearrange("p a t -> p (a t)")),
                ])
                window_outputs_stage(k, kv)
                turn_stage(k, "kturn", [
                    ([kv[0:n, i, g * GW + h * P:g * GW + (h + 1) * P] for h in range(SWA_H)], n,
                     kT[:, 4 * g:4 * g + 4, t0:t0 + n]) for g in range(3) for i, (t0, n) in enumerate(TILES)])
                Bp = e["bias_p"] = k.sb(c2, "e_bias_p", [P, SWA_H, 2, 3, SEQ])
                bias_stage(k, e)
                units = []
                for qb in range(2):
                    n = (qb + 1) * P
                    for h in range(SWA_H):
                        scores, keys = [], []
                        for g in range(3):
                            q = swa_qT[:, 4 * g + h, qb * P:(qb + 1) * P]
                            for kb in range(qb + 1):
                                c0 = g * n + kb * P
                                scores.append((c0, P, [(q, kT[:, 4 * g + h, kb * P:(kb + 1) * P])]))
                                v0 = (3 + g) * GW + h * P
                                keys.append((c0, [kv[:, kb, v0:v0 + P]]))
                        units.append({"scores": scores, "keys": keys, "bias": Bp[:, h, qb, :, 0:n],
                                      "outs": [e["oT"][:, 4 + h, qb * P:(qb + 1) * P]]})
                attend_prompt(k, "swp", units, 3 * SEQ, 1.0, SWA_SCALE)
            swa_sample(k, e, swa_qT, kT)
        gemm_stage(k, "aout", [("tok", e["oT"], io["attn_w_out"][0], 512, k.h)])


def mla_prompt(k, e, mask):
    nc, io = k.nc, k.io
    with ExitStack() as ctx:
        landed = k.sem("mp_mask_landed")
        block = ctx.enter_context(k.block())

        @block.sync
        def _(sp):
            sp.dma_start(mask[:, :, :], io["causal"]).then_inc(landed, 16)
            sp.wait_ge(landed, 16)
    units = []
    for qb in range(2):
        n = (qb + 1) * P
        qs = slice(qb * P, (qb + 1) * P)
        for h in range(MLA_H):
            prods = [(e["qlatT"][:, c, h, qs], e["ckvT"][:, c, 0:n]) for c in range(2)]
            prods.append((e["qrT"][:, h, qs], e["krT"][:, 0:n]))
            units.append({"scores": [(0, n, prods)], "bias": mask[:, qb, 0:n],
                          "keys": [(kb * P, [e["rows"][:, kb, c * P:(c + 1) * P] for c in range(2)])
                                   for kb in range(qb + 1)],
                          "outs": [e["olatT"][:, c, h, qs] for c in range(2)]})
    attend_prompt(k, "mlp", units, SEQ, MLA_SCALE, 1.0)


def mla_sample(k, e):
    nc, io = k.nc, k.io
    with ExitStack() as ctx:
        pages = k.sb(ctx, "ms_pages", [P, 2, N_PAGES, MLA_ROW])
        rnew = k.sb(ctx, "ms_rows_new", [DEC_S, 2, MLA_ROW])
        KT = k.sb(ctx, "ms_kT", [P, 2, PAST])
        KR = k.sb(ctx, "ms_krT", [ROPE, PAST])
        qst = k.sb(ctx, "ms_q", [P, 2, 2, MLA_H, DEC_S])
        qrst = k.sb(ctx, "ms_qr", [ROPE, 2, MLA_H, DEC_S])
        knew = k.sb(ctx, "ms_knew", [P, 2, 2, DEC_S])
        krnew = k.sb(ctx, "ms_krnew", [ROPE, 2, DEC_S])
        mask = k.sb(ctx, "ms_mask", [P, DEC_S])
        table = k.sb(ctx, "ms_table", [1, DEC_B * N_PAGES], I32)
        half = PAST // 2
        table_landed, masked = k.sem("ms_table_landed"), k.sem("ms_masked")
        with ExitStack() as c2:
            block = c2.enter_context(k.block())

            @block.sync
            def _(sp):
                sp.dma_start(table[:, :], io["page_table"].rearrange("b n -> (b n)").unsqueeze(0)).then_inc(table_landed, 16)
                sp.dma_start(mask[0:64, :], io["causal_new"]).then_inc(table_landed, 16)
                sp.wait_ge(table_landed, 32)

            @block.vector
            def _(dve):
                dve.memset(mask[64:128, :], DISALLOWED).then_inc(masked, 1)

        n_pool = io["cache_mla"].shape[1]

        def prepare_keys(sp, u, part):
            return [sp.value_load(table[0:1, ds(u * N_PAGES + j, 1)], min_val=0, max_val=n_pool - 1)
                    for j in range(4 * part, 4 * part + 4)]

        def load_keys(sp, u, slot, part, landed, page_numbers):
            for j, page in zip(range(4 * part, 4 * part + 4), page_numbers):
                sp.dma_start(pages[:, slot, j, :],
                             io["cache_mla"][0, ds(page, 1)].rearrange("a p c -> (a p) c")).then_inc(landed, 16)

        def load_values(sp, u, slot, landed):
            sp.dma_start(rnew[:, slot, :], io["mla_rows_sample"][0, ds(u, 1)].rearrange("b s c -> (b s) c")).then_inc(landed, 16)

        def stage(pool, u, slot, staged):
            t = ds(SEQ + DEC_S * u, DEC_S)
            pool.tensor_copy(qst[:, slot, :, :, :], e["qlatT"][:, :, :, t]).then_inc(staged, 1)
            pool.tensor_copy(qrst[:, slot, :, :], e["qrT"][:, :, t]).then_inc(staged, 1)
            pool.tensor_copy(knew[:, slot, :, :], e["ckvT"][:, :, t]).then_inc(staged, 1)
            pool.tensor_copy(krnew[:, slot, :], e["krT"][:, t]).then_inc(staged, 1)

        def q(c):
            return lambda slot: qst[:, slot, c, :, :].rearrange("p h s -> p (h s)")

        def qr(slot):
            return qrst[:, slot, :, :].rearrange("p h s -> p (h s)")

        def cached(c, c0):
            return lambda slot: KT[:, c, c0:c0 + 512]

        chunks = [(c0, 512, [(64 * r, 64, [(q(0), cached(0, c0 + r * half)), (q(1), cached(1, c0 + r * half)),
                                           (qr, lambda slot, c=c0 + r * half: KR[:, c:c + 512])])
                             for r in range(2)]) for c0 in range(0, half, 512)]
        chunks.append((half, DEC_S, [(64 * r, 64, [(q(0), lambda slot: knew[:, slot, 0, :]),
                                                   (q(1), lambda slot: knew[:, slot, 1, :]),
                                                   (qr, lambda slot: krnew[:, slot, :])]) for r in range(2)]))

        def page_block(j, c0, w):
            return lambda slot: pages[:, slot, j, c0:c0 + w]

        groups = []
        for j in range(0, N_PAGES, 4):
            for i in (j, j + 2):
                groups.append([(page_block(i + b, c * P, P), P) for c in range(2) for b in range(2)])
            groups.append([(page_block(j + b, 2 * P, ROPE), ROPE) for b in range(4)])

        def key_copies(g, bank):
            first, kind = 4 * (g // 3) * P, g % 3
            if kind < 2:
                c0 = first + 2 * kind * P
                yield KT[:, :, c0:c0 + 2 * P], bank.rearrange("p (a b) -> p a b", a=2)
            else:
                yield KR[:, first:first + 4 * P], bank[0:ROPE, :]

        def values(j, c):
            return lambda slot: pages[:, slot, j, c * P:(c + 1) * P]

        value_terms = [(64 * c, 64, P, j % 8, P, 64 * (j // 8), values(j, c)) for j in range(N_PAGES) for c in range(2)]
        value_terms += [(64 * c, 64, P, 8, DEC_S, 0, lambda slot, c=c: rnew[:, slot, c * P:(c + 1) * P])
                        for c in range(2)]

        attend_sample(k, "mls", {
            "halves": True, "cols": half + DEC_S, "scale": MLA_SCALE, "bias_scale": 1.0,
            "bias": lambda c0, n: mask[:, :] if c0 == half else None,
            "groups": groups, "key_copies": key_copies, "chunks": chunks,
            "blocks": [(j * P, P) for j in range(half // P)] + [(half, DEC_S)],
            "value_terms": value_terms, "out_cols": P,
            "key_parts": [3] * 4, "key_dmas": [4] * 4, "prepare_keys": prepare_keys, "load_keys": load_keys,
            "shared": True, "slots": 2, "load_values": load_values, "value_dmas": 1, "stage": stage, "n_stage": 4,
            "groups_for": lambda c: 12 if c >= half else 3 * (c // 512) + 6, "setup_count": 0,
            "out": lambda u, bank: (e["olatT"][:, :, :, ds(SEQ + DEC_S * u, DEC_S)],
                                    bank[:, 0:128].rearrange("p (c h s) -> p c h s", c=2, h=MLA_H)),
        })


def swa_sample(k, e, swa_qT, kT):
    nc, io = k.nc, k.io
    with ExitStack() as ctx:
        kcache = k.sb(ctx, "ss_kcache", [P, len(SWA_TILES), GW])
        vcache = k.sb(ctx, "ss_vcache", [P, len(SWA_TILES), GW])
        vnew = k.sb(ctx, "ss_vnew", [DEC_S, 3 * GW])
        KT = k.sb(ctx, "ss_kT", [P, SWA_H, SWA_CACHED])
        qst = k.sb(ctx, "ss_q", [P, 2, 12, PAD])
        knew = k.sb(ctx, "ss_knew", [P, 2, 12, DEC_S])

        def setup_pool(pool, done):
            pool.memset(qst[:, :, :, :], 0.0).then_inc(done, 1)
            pool.wait_ge(done, 1)

        def windows(eng, u, part, dst, landed, piece):
            c = [io[n][0, ds(u, 1), :, part].rearrange("b w h d -> (b w) (h d)") for n in
                 ("cache_swa_w128", "cache_swa_w512", "cache_swa_w2048")]
            if piece == 0:
                eng.dma_start(dst[:, 0, :], c[0]).then_inc(landed, 16)
                eng.dma_start(dst[:, 1:5, :], c[1].rearrange("(i p) n -> p i n", p=P)).then_inc(landed, 16)
                return
            wide = c[2].rearrange("(i a r) n -> i a r n", i=8, r=16)
            for i in range(4 * piece - 4, 4 * piece):
                eng.dma_start(dst[:, 5 + i, :], wide[i, :, 0:8, :]).then_inc(landed, 16)

        def load_keys(sp, u, slot, part, landed, _):
            windows(sp, u, 0, kcache, landed, part)

        def load_values(sp, u, slot, landed):
            for piece in range(3):
                windows(sp, u, 1, vcache, landed, piece)
            sp.dma_start(vnew[:, :], io["kv_new"][ds(u * DEC_S, DEC_S), 3 * GW:6 * GW]).then_inc(landed, 16)

        def stage(pool, u, slot, staged):
            t = ds(SEQ + DEC_S * u, DEC_S)
            pool.tensor_copy(qst[:, slot, :, 0:DEC_S], swa_qT[:, :, t]).then_inc(staged, 1)
            pool.tensor_copy(knew[:, slot, :, :], kT[:, :, t]).then_inc(staged, 1)

        def q(g, h):
            return lambda slot: qst[:, slot, 4 * g + h, :]

        chunks = []
        c0 = 0
        while c0 < SWA_CACHED:
            g = SWA_TILES[c0 // P][0]
            n = P
            while n < 512 and c0 + n < SWA_CACHED and SWA_TILES[(c0 + n) // P][0] == g:
                n += P
            chunks.append((c0, n, [(PAD * h, PAD, [(q(g, h), lambda slot, h=h, c0=c0, n=n: KT[:, h, c0:c0 + n])])
                                   for h in range(SWA_H)]))
            c0 += n
        for g in range(3):
            chunks.append((SWA_CACHED + g * DEC_S, DEC_S,
                           [(PAD * h, PAD, [(q(g, h), lambda slot, g=g, h=h: knew[:, slot, 4 * g + h, :])])
                            for h in range(SWA_H)]))

        def key_copies(g, bank):
            yield KT[:, :, g * P:(g + 1) * P], bank.rearrange("p (a b) -> p a b", a=4)

        def values(j, h):
            return lambda slot: vcache[:, j, h * P:(h + 1) * P]

        value_terms = [(PAD * h, PAD, SWA_D, j, P, PAD * h, values(j, h))
                       for j in range(len(SWA_TILES)) for h in range(SWA_H)]
        value_terms += [(PAD * h, PAD, SWA_D, len(SWA_TILES) + g, DEC_S, PAD * h,
                         lambda slot, g=g, h=h: vnew[:, g * GW + h * P:g * GW + (h + 1) * P])
                        for g in range(3) for h in range(SWA_H)]

        attend_sample(k, "sws", {
            "halves": False, "cols": SWA_KEYS, "scale": 1.0, "bias_scale": SWA_SCALE,
            "bias": lambda c0, n: e["bias_s"][:, c0:c0 + n],
            "groups": [[(lambda slot, j=j, h=h: kcache[:, j, h * P:(h + 1) * P], P) for h in range(SWA_H)]
                       for j in range(len(SWA_TILES))],
            "key_copies": key_copies, "chunks": chunks,
            "blocks": [(j * P, P) for j in range(len(SWA_TILES))]
            + [(SWA_CACHED + g * DEC_S, DEC_S) for g in range(3)],
            "value_terms": value_terms, "out_cols": SWA_D,
            "key_parts": [5, 4, 4], "key_dmas": [2, 4, 4], "load_keys": load_keys, "shared": False, "slots": 1,
            "load_values": load_values, "value_dmas": 11, "stage": stage, "n_stage": 2,
            "groups_for": lambda c: -(-c // P),
            "setup_pool": setup_pool, "setup_count": 1,
            "out": lambda u, bank: (e["oT"][:, 4:8, ds(SEQ + DEC_S * u, DEC_S)],
                                    bank[:, 0:P].rearrange("p (h s) -> p h s", h=SWA_H)[:, :, 0:DEC_S]),
        })


def memory_attention(k, layer):
    nc, io = k.nc, k.io
    n_ = f"m{layer}"
    with ExitStack() as ctx:
        qT = k.sb(ctx, n_ + "_qT", [P, 8, T])
        oT = k.sb(ctx, n_ + "_oT", [P, 8, T])
        with ExitStack() as c1:
            mkv = k.sb(c1, n_ + "_mkv", [P, 2, 2 * D])
            kT = k.sb(c1, n_ + "_kT", [P, 8, N_MEM])
            gemm_stage(k, n_ + "in", [
                ("feat", k.xT, io["mem_wq"][layer], 512, qT[:, :, :].rearrange("p a t -> p (a t)")),
                ("tok", k.memT, io["mem_wk"][layer], 512, mkv[:, :, 0:D]),
                ("tok", k.memT, io["mem_wv"][layer], 512, mkv[:, :, D:2 * D]),
            ])
            turn_stage(k, n_ + "kturn", [
                ([mkv[:, i, (4 * half + j) * P:(4 * half + j + 1) * P] for j in range(4)], P,
                 kT[:, 4 * half:4 * half + 4, i * P:(i + 1) * P]) for i in range(2) for half in range(2)])
            with ExitStack() as c2:
                stored = k.sem(n_ + "_kv_stored")
                block = c2.enter_context(k.block())

                @block.sync
                def _(sp):
                    sp.dma_start(io["mem_kv_prompt"][layer, 0].rearrange("(i p) c h d -> p i (c h d)", p=P),
                                 mkv[:, :, :]).then_inc(stored, 16)
                    sp.wait_ge(stored, 16)
            units = []
            for qb in range(2):
                qs = slice(qb * P, (qb + 1) * P)
                for h in range(MEM_H):
                    units.append({
                        "scores": [(0, N_MEM, [(qT[:, 2 * h + c, qs], kT[:, 2 * h + c, :]) for c in range(2)])],
                        "bias": None,
                        "keys": [(kb * P, [mkv[:, kb, D + (2 * h + c) * P:D + (2 * h + c + 1) * P] for c in range(2)])
                                 for kb in range(2)],
                        "outs": [oT[:, 2 * h + c, qs] for c in range(2)]})
            attend_prompt(k, n_ + "p", units, N_MEM, MEM_SCALE, 1.0)
        with ExitStack() as c1:
            cache = k.sb(c1, n_ + "_cache", [P, 2, 2, 2, D])
            KT = k.sb(c1, n_ + "_skT", [P, 8, N_MEM])
            qst = k.sb(c1, n_ + "_sq", [P, 2, 8, PAD])

            def setup_pool(pool, done):
                pool.memset(qst[:, :, :, :], 0.0).then_inc(done, 1)
                pool.wait_ge(done, 1)

            def load_part(sp, u, slot, part, landed):
                src = io["cache_mem_kv"][layer, ds(u, 1), :, part].rearrange("b (i p) h d -> p (b i) (h d)", p=P)
                sp.dma_start(cache[:, slot, part, :, :], src).then_inc(landed, 16)

            def load_keys(sp, u, slot, part, landed, _):
                load_part(sp, u, slot, 0, landed)

            def load_values(sp, u, slot, landed):
                load_part(sp, u, slot, 1, landed)

            def stage(pool, u, slot, staged):
                pool.tensor_copy(qst[:, slot, :, 0:DEC_S], qT[:, :, ds(SEQ + DEC_S * u, DEC_S)]).then_inc(staged, 1)

            def key_copies(g, bank):
                i, half = divmod(g, 2)
                yield KT[:, 4 * half:4 * half + 4, i * P:(i + 1) * P], bank.rearrange("p (a b) -> p a b", a=4)

            attend_sample(k, n_ + "s", {
                "halves": False, "cols": N_MEM, "scale": MEM_SCALE, "bias_scale": 1.0, "bias": lambda c0, n: None,
                "groups": [[(lambda slot, i=i, b=4 * half + j: cache[:, slot, 0, i, b * P:(b + 1) * P], P)
                            for j in range(4)] for i in range(2) for half in range(2)],
                "key_copies": key_copies,
                "chunks": [(0, N_MEM, [(PAD * h, PAD, [
                    (lambda slot, b=2 * h + c: qst[:, slot, b, :], lambda slot, b=2 * h + c: KT[:, b, :])
                    for c in range(2)]) for h in range(MEM_H)])],
                "blocks": [(i * P, P) for i in range(2)],
                "value_terms": [(PAD * h, PAD, MEM_D, i, P, PAD * h,
                                 lambda slot, i=i, h=h: cache[:, slot, 1, i, h * MEM_D:(h + 1) * MEM_D])
                                for i in range(2) for h in range(MEM_H)],
                "out_cols": MEM_D,
                "key_parts": [4], "key_dmas": [1], "load_keys": load_keys, "shared": False, "slots": 2,
                "load_values": load_values, "value_dmas": 1, "stage": stage, "n_stage": 1, "groups_for": lambda c: 4,
                "setup_pool": setup_pool, "setup_count": 1,
                "out": lambda u, bank: (
                    oT[:, :, ds(SEQ + DEC_S * u, DEC_S)].rearrange("p (h c) s -> p c h s", c=2),
                    bank[:, 0:MEM_D].rearrange("p (c h s) -> p c h s", c=2, h=MEM_H)[:, :, :, 0:DEC_S]),
            })
        gemm_stage(k, n_ + "out", [("tok", oT, io["mem_wo"][layer], 512, k.h)])


def odd_mixer(k):
    nc, io = k.nc, k.io
    with ExitStack() as ctx:
        prod = k.sb(ctx, "c_prod", [P, 24, T])
        cT = k.sb(ctx, "c_convT", [P, 8, T])
        gemm_stage(k, "cin", [("feat", k.xT, io["conv_w_in"][0], 512, prod[:, :, :].rearrange("p a t -> p (a t)"))])
        with ExitStack() as c1:
            up = k.sb(c1, "c_up", [P, 8, SEQ + 2])
            us = k.sb(c1, "c_us", [P, 8, DEC_B, DEC_S + 2])
            state = k.sb(c1, "c_state", [2 * DEC_B, D])
            taps = k.sb(c1, "c_taps", [3, D])
            tapT = k.sb(c1, "c_tapT", [P, 8, 3])
            tail = k.sb(c1, "c_tail", [P, 8, 32])
            tail_tok = k.sb(c1, "c_tail_tok", [18, D])
            landed, turned, taken = k.sem("c_landed"), k.sem("c_turned"), k.sem("c_taken")
            zeroed, u_ready, chain = k.sem("c_zeroed"), k.sem("c_u_ready"), k.sem("c_chain")
            tail_ready, tail_turned, tail_taken = k.sem("c_tail_ready"), k.sem("c_tail_turned"), k.sem("c_tail_taken")
            stored = k.sem("c_stored")
            block = c1.enter_context(k.block())

            @block.sync
            def _(sp):
                sp.dma_start(state[:, :], io["state_conv"][0].rearrange("b s d -> (b s) d")).then_inc(landed, 16)
                sp.dma_start(taps[:, :], io["conv_w"][0]).then_inc(landed, 16)
                sp.wait_ge(tail_taken, 2)
                sp.dma_start(io["conv_prompt"][0, 0], tail_tok[0:2, :]).then_inc(stored, 16)
                sp.dma_start(io["conv_sample"][0].rearrange("b s d -> (b s) d"), tail_tok[2:18, :]).then_inc(stored, 16)
                sp.wait_ge(stored, 32)

            @block.gpsimd
            def _(pool):
                pool.memset(up[:, :, 0:2], 0.0).then_inc(zeroed, 1)

            @block.tensor
            def _(pe):
                pe.wait_ge(landed, 32)
                for c in range(8):
                    pe.transpose(k.ps[:, 0, 16 * c:16 * c + 16], state[:, c * P:(c + 1) * P], k.ident[0:16, 0:16])
                for c in range(8):
                    mm = pe.transpose(k.ps[:, 1, 4 * c:4 * c + 3], taps[:, c * P:(c + 1) * P], k.ident[0:3, 0:3])
                mm.then_inc(turned, 1)
                pe.wait_ge(tail_ready, 1)
                for c in range(8):
                    mm = pe.transpose(k.ps[0:18, 2 + c // 4, (c % 4) * P:(c % 4 + 1) * P], tail[:, c, 0:18], k.ident[:, :])
                mm.then_inc(tail_turned, 1)

            @block.scalar
            def _(act):
                act.wait_ge(turned, 1)
                act.activation(us[:, :, :, 0:2], k.ps[:, 0, 0:128].rearrange("p (c b s) -> p c b s", c=8, b=DEC_B),
                               ACT.Copy).then_inc(taken, 1)
                act.activation(tapT[:, :, :], k.ps[:, 1, 0:32].rearrange("p (c s) -> p c s", c=8)[:, :, 0:3],
                               ACT.Copy).then_inc(taken, 1)
                act.wait_ge(tail_turned, 1)
                for half in range(2):
                    act.activation(tail_tok[:, half * 512:(half + 1) * 512], k.ps[0:18, 2 + half, :],
                                   ACT.Copy).then_inc(tail_taken, 1)

            @block.vector
            def _(dve):
                dve.tensor_tensor(out=up[:, :, 2:], in0=prod[:, 8:16, 0:SEQ], in1=prod[:, 16:24, 0:SEQ],
                                  op=ALU.mult).then_inc(u_ready, 1)
                for c in range(8):
                    dve.tensor_tensor(out=us[:, c, :, 2:],
                                      in0=prod[:, 8 + c, SEQ:T].rearrange("p (b s) -> p b s", b=DEC_B),
                                      in1=prod[:, 16 + c, SEQ:T].rearrange("p (b s) -> p b s", b=DEC_B),
                                      op=ALU.mult).then_inc(u_ready, 1)
                dve.wait_ge(u_ready, 9)
                dve.wait_ge(zeroed, 1)
                dve.wait_ge(taken, 2)
                dve.tensor_copy(tail[:, :, 0:2], up[:, :, SEQ:SEQ + 2])
                dve.tensor_copy(tail[:, :, 2:18].rearrange("p c (b s) -> p c b s", b=DEC_B),
                                us[:, :, :, DEC_S:DEC_S + 2]).then_inc(tail_ready, 1)
                n = 0
                for step in range(3):
                    for c in range(8):
                        w = tapT[:, c, step:step + 1]
                        outs = (cT[:, c, 0:SEQ], cT[:, c, SEQ:T].rearrange("p (b s) -> p b s", b=DEC_B))
                        ins = (up[:, c, step:step + SEQ], us[:, c, :, step:step + DEC_S])
                        for o, i_ in zip(outs, ins):
                            if step == 0:
                                last = dve.tensor_scalar(out=o, in0=i_, scalar1=w, scalar2=None, op0=ALU.mult)
                            else:
                                last = dve.scalar_tensor_tensor(out=o, in0=i_, scalar=w, in1=o, op0=ALU.mult, op1=ALU.add)
                    last.then_inc(chain, 1)
                    dve.wait_ge(chain, step + 1)
                dve.tensor_tensor(out=cT[:, :, :], in0=cT[:, :, :], in1=prod[:, 0:8, :], op=ALU.mult).then_inc(chain, 1)
        gemm_stage(k, "cout", [("tok", cT, io["conv_w_out"][0], 512, k.h)])


def peer_stage(k, name, layer, pqT):
    nc, io = k.nc, k.io
    H2 = 2 * PEER_H
    RING, PER = 8, 2
    GRP = RING // PER
    with ExitStack() as ctx:
        ur = k.sb(ctx, name + "_u", [P, RING, D])
        vr = k.sb(ctx, name + "_v", [P, RING, D])
        sub = ur[:, 0:2, :].rearrange("p a (b n) -> p (a b) n", n=P)
        subT = k.sb(ctx, name + "_subT", [P, H2, P])
        s = k.sb(ctx, name + "_s", [P, H2, N_KEYS])
        s2 = k.sb(ctx, name + "_s2", [P, H2, N_KEYS])
        v16 = k.sb(ctx, name + "_v16", [P, H2, TOPK])
        i16 = k.sb(ctx, name + "_i16", [P, H2, TOPK], U32)
        i16f = k.sb(ctx, name + "_i16f", [P, PEER_H, 2, TOPK])
        cand = k.sb(ctx, name + "_cand", [P, PEER_H, TOPK, TOPK])
        cand2 = k.sb(ctx, name + "_cand2", [P, PEER_H, TOPK, TOPK])
        best = k.sb(ctx, name + "_best", [P, PEER_H, TOPK])
        sel = k.sb(ctx, name + "_sel", [P, PEER_H, TOPK], U32)
        half = k.sb(ctx, name + "_half", [P, 2, HK], U32)
        halff = k.sb(ctx, name + "_halff", [P, 2, HK])
        part = k.sb(ctx, name + "_part", [P, 2, HK])
        iota16 = k.sb(ctx, name + "_iota16", [P, TOPK])
        den = k.sb(ctx, name + "_den", [P, PEER_H])
        expert = k.sb(ctx, name + "_expert", [P, 2, HK], I32)
        gate = k.sb(ctx, name + "_gate", [P, HK])
        dots = k.sb(ctx, name + "_dots", [P, 2, RING])
        weight = k.sb(ctx, name + "_weight", [P, HK])
        wst = k.sb(ctx, name + "_wst", [P, 2, RING])
        diag = k.sb(ctx, name + "_diag", [P, 2, RING, P])
        fold = k.sb(ctx, name + "_fold", [P, 64])
        zero = k.sb(ctx, name + "_zero", [P, P])
        acc = k.sb(ctx, name + "_acc", [P, PER, D])
        ist = k.sb(ctx, name + "_ist", [P, 2, 2, RING], I32)

        landed, turned, sub_ready = k.sem(name + "_landed"), k.sem(name + "_turned"), k.sem(name + "_sub_ready")
        scored, s_ready, chain = k.sem(name + "_scored"), k.sem(name + "_s_ready"), k.sem(name + "_chain")
        s_used, diff_ready, exp_ready = k.sem(name + "_s_used"), k.sem(name + "_diff"), k.sem(name + "_exp")
        chosen, prepared = k.sem(name + "_chosen"), k.sem(name + "_prepared")
        packed, gated, gate_packed = k.sem(name + "_packed"), k.sem(name + "_gated"), k.sem(name + "_gate_packed")
        u_staged, v_staged = k.sem(name + "_u_staged"), k.sem(name + "_v_staged")
        begun, begun_pe = k.sem(name + "_begun_pool"), k.sem(name + "_begun_pe")
        u_used = [k.sem(f"{name}_u_used{g}") for g in range(GRP)]
        v_used = [k.sem(f"{name}_v_used{g}") for g in range(GRP)]
        gelu_done, weight_ready = k.sem(name + "_gelu"), k.sem(name + "_weight")
        w_staged, diag_ready = k.sem(name + "_w_staged"), k.sem(name + "_diag")
        acc_ready, sum_ready, sum_taken = k.sem(name + "_acc_ready"), k.sem(name + "_sum"), k.sem(name + "_sum_taken")
        u_landed = [k.gathered[f"u_rows_landed{g}"] for g in range(GRP)]
        v_landed = [k.gathered[f"v_rows_landed{g}"] for g in range(GRP)]
        block = ctx.enter_context(k.block())
        u_rows = io["peer_u"].rearrange("l e d -> (l e) d")
        v_rows = io["peer_v"].rearrange("l e d -> (l e) d")
        rounds = [HK // RING, HK // RING, HK // 2 // RING]
        first = [0, rounds[0], rounds[0] + rounds[1]]
        before = layer * 16 * PER * sum(rounds)
        ALONE = 4

        def in_rounds(eng, i, body, r0=0, r1=None):
            r1 = rounds[i] if r1 is None else r1

            def pair(j):
                for par in range(2):
                    body(2 * j + par, first[i] + 2 * j + par, par)
            if r0 == r1:
                return
            lo, hi = r0 // 2, r1 // 2
            if i == 0 and lo == 0:
                pair(0)
                lo = 1
            if hi - lo == 1:
                pair(lo)
            elif hi > lo:
                with eng.Fori(lo, hi) as j:
                    pair(j)

        def value_rounds(eng, i, body):
            alone = ALONE if i < 2 else 0
            in_rounds(eng, i, lambda r, R, par: body(r, R, par, False), 0, alone)
            in_rounds(eng, i, lambda r, R, par: body(r, R, par, True), alone)

        @block.sync
        def _(sp):
            sp.dma_start(sub, io["peer_subkeys"][layer].rearrange("h a n k -> n (h a) k")).then_inc(landed, 16)
            sp.dma_start(iota16[:, :], bass.AP(io["iota16"].tensor, 0, [[0, P], [1, TOPK]])).then_inc(landed, 16)
            sp.dma_start(k.x[64:P, 2, :], k.x[0:64, 2, :]).then_inc(packed, 16)
            sp.wait_ge(chosen, 3)
            sp.dma_start(expert[64:P, 0, 0:64], expert[0:64, 0, 64:HK]).then_inc(packed, 16)
            sp.wait_ge(gated, 3)
            sp.dma_start(gate[64:P, 0:64], gate[0:64, 64:HK]).then_inc(gate_packed, 16)

        @block.gpsimd
        def _(pool):
            def gathers(i, which, rows, ring, landed_, used, staged):
                def body(r, R, par):
                    pool.tensor_copy(ist[:, which, par, :], expert[:, i % 2, ds(r * RING, RING)]).then_inc(staged, 1)
                    wait_apart(pool, staged, R + 1, begun)
                    for g in range(GRP):
                        wait_apart(pool, used[g], R, begun)
                        for m in range(PER):
                            j = g * PER + m
                            pool.indirect_dma_start(
                                out=ring[:, j, :], out_offset=None, in_=rows,
                                in_offset=bass.IndirectOffsetOnAxis(ap=ist[:, which, par, j:j + 1], axis=0),
                            ).then_inc(landed_[g], 16)
                in_rounds(pool, i, body)

            pool.memset(zero[:, :], 0.0).then_inc(prepared, 1)
            for i in range(3):
                pool.wait_ge(chosen, i + 1)
                if i == 0:
                    pool.wait_ge(sub_ready, 4)
                if i == 2:
                    pool.wait_ge(packed, 32)
                gathers(i, 0, u_rows, ur, u_landed, u_used, u_staged)
                gathers(i, 1, v_rows, vr, v_landed, v_used, v_staged)

        @block.vector
        def _(dve):
            link = Chain(dve, chain)

            def top16(n, groups, src, spare, val, ind):
                for g in range(groups):
                    last = dve.max(val[0:n, g, 0:8], src(g))
                link(last)
                for g in range(groups):
                    dve.max_index(ind[0:n, g, 0:8], val[0:n, g, 0:8], src(g))
                    last = dve.match_replace(spare(g), val[0:n, g, 0:8], src(g), LOWEST)
                link(last)
                for g in range(groups):
                    last = dve.max(val[0:n, g, 8:16], spare(g))
                link(last)
                for g in range(groups):
                    last = dve.max_index(ind[0:n, g, 8:16], val[0:n, g, 8:16], spare(g))
                link(last)

            def choose(i, n):
                dve.wait_ge(s_ready, 4 * (i + 1))
                top16(n, H2, lambda g: s[0:n, g, :], lambda g: s2[0:n, g, :], v16, i16)
                dve.tensor_copy(i16f[0:n].rearrange("p h a t -> p (h a t)"),
                                i16[0:n].rearrange("p g t -> p (g t)")).then_inc(s_used, 1)
                v4 = v16[0:n, :, :].rearrange("p (h a) t -> p h a t", a=2)
                top = v4[:, :, 0, :].unsqueeze(3).to_broadcast([n, PEER_H, TOPK, TOPK])
                low = v4[:, :, 1, :].unsqueeze(2).to_broadcast([n, PEER_H, TOPK, TOPK])
                link(dve.tensor_tensor(out=cand[0:n], in0=top, in1=low, op=ALU.add))
                flat = [x[0:n].rearrange("p h a b -> p h (a b)") for x in (cand, cand2)]
                top16(n, PEER_H, lambda g: flat[0][:, g, :], lambda g: flat[1][:, g, :], best, sel)
                link(dve.tensor_copy(den[0:n, :], best[0:n, :, 0]))
                dve.tensor_tensor(out=best[0:n], in0=best[0:n],
                                  in1=den[0:n, :].unsqueeze(2).to_broadcast([n, PEER_H, TOPK]),
                                  op=ALU.subtract).then_inc(diff_ready, 1)
                selv = sel[0:n].rearrange("p h t -> p (h t)")
                dve.tensor_scalar(out=half[0:n, 0, :], in0=selv, scalar1=4, scalar2=None, op0=ALU.logical_shift_right)
                link(dve.tensor_scalar(out=half[0:n, 1, :], in0=selv, scalar1=15, scalar2=None, op0=ALU.bitwise_and))
                link(dve.tensor_copy(halff[0:n], half[0:n]))
                dve.wait_ge(s_used, i + 1)
                hots = [x[0:n].rearrange("p h a b -> p (h a) b") for x in (cand, cand2)]
                for a in range(2):
                    last = dve.tensor_tensor(out=hots[a], in0=iota16[0:n, :].unsqueeze(1).to_broadcast([n, HK, TOPK]),
                                             in1=halff[0:n, a, :].unsqueeze(2).to_broadcast([n, HK, TOPK]),
                                             op=ALU.is_equal)
                link(last)
                for a in range(2):
                    hot4 = (cand, cand2)[a][0:n]
                    last = dve.tensor_tensor(out=hot4, in0=hot4,
                                             in1=i16f[0:n, :, a, :].unsqueeze(2).to_broadcast([n, PEER_H, TOPK, TOPK]),
                                             op=ALU.mult)
                link(last)
                for a in range(2):
                    last = dve.tensor_reduce(out=part[0:n, a, :], in_=hots[a], axis=AX, op=ALU.add)
                link(last)
                link(dve.scalar_tensor_tensor(out=part[0:n, 0, :], in0=part[0:n, 0, :], scalar=float(N_KEYS),
                                              in1=part[0:n, 1, :], op0=ALU.mult, op1=ALU.add))
                for staged in (u_staged, v_staged):
                    if i > 0:
                        wait(dve, staged, first[i - 1])
                dve.tensor_scalar(out=expert[0:n, i % 2, :], in0=part[0:n, 0, :], scalar1=float(N_EXPERTS * layer),
                                  scalar2=None, op0=ALU.add).then_inc(chosen, 1)

            def gates(i, n):
                dve.wait_ge(exp_ready, i + 1)
                link(dve.reduce_sum(den[0:n, :], best[0:n], AX))
                link(dve.reciprocal(den[0:n, :], den[0:n, :]))
                dve.tensor_tensor(out=gate[0:n, :].rearrange("p (h t) -> p h t", h=PEER_H), in0=best[0:n],
                                  in1=den[0:n, :].unsqueeze(2).to_broadcast([n, PEER_H, TOPK]),
                                  op=ALU.mult).then_inc(gated, 1)

            dve.tensor_tensor(out=fold[:, :], in0=k.ident[:, 0:64], in1=k.ident[:, 64:P], op=ALU.add).then_inc(prepared, 1)
            dve.wait_ge(landed, 32)
            choose(0, P)
            for i, (t0, n) in enumerate(TILES):
                if i == 2:
                    dve.wait_ge(packed, 32)

                def dot(_, R, par):
                    wait(dve, gelu_done, R - 1)
                    for g in range(GRP):
                        dve.wait_ge(u_landed[g], before + 16 * PER * (R + 1))
                        for m in range(PER):
                            j = g * PER + m
                            last = dve.tensor_tensor_reduce(
                                out=ur[:, j, :], in0=ur[:, j, :], in1=k.x[:, i, :], scale=1.0, scalar=0.0,
                                op0=ALU.mult, op1=ALU.add, accum_out=dots[:, par, j:j + 1])
                        last.then_inc(u_used[g], 1)
                in_rounds(dve, i, dot)
                w = rounds[i] * RING
                gates(i, n)
                dve.wait_ge(gated, i + 1)
                if i == 2:
                    dve.wait_ge(gate_packed, 16)
                dve.wait_ge(gelu_done, first[i] + rounds[i])
                dve.tensor_tensor(out=weight[:, 0:w], in0=weight[:, 0:w], in1=gate[:, 0:w],
                                  op=ALU.mult).then_inc(weight_ready, 1)
                wait(dve, sum_ready, i)
                link(dve.memset(acc[:, :, :], 0.0))
                if i < 2:
                    choose(i + 1, TILES[i + 1][1])

                def add(r, R, par, mixed):
                    if mixed:
                        dve.wait_ge(v_landed[GRP - 1], before + 16 * PER * (R + 1))
                        dve.wait_ge(w_staged, R + 1)
                        dve.wait_ge(v_used[GRP - 1], R)
                        for m in range(PER):
                            j = (GRP - 1) * PER + m
                            last = dve.scalar_tensor_tensor(out=acc[:, m, :], in0=vr[:, j, :], scalar=wst[:, par, j:j + 1],
                                                            in1=acc[:, m, :], op0=ALU.mult, op1=ALU.add)
                        last.then_inc(v_used[GRP - 1], 1)
                in_rounds(dve, i, lambda r, R, par: add(r, R, par, True), ALONE if i < 2 else 0)
                dve.wait_ge(v_used[GRP - 1], first[i] + rounds[i])
                dve.sem_inc(acc_ready, 1)

        @block.scalar
        def _(act):
            def take_scores(i):
                n = TILES[i][1]
                wait(act, s_used, i)
                for g in range(4):
                    act.wait_ge(scored, 4 * i + g + 1)
                    act.activation(s[0:n, 4 * g:4 * g + 4, :].rearrange("p a b -> p (a b)"), k.ps[0:n, 4 + g, :],
                                   ACT.Copy).then_inc(s_ready, 1)

            def exponentials(i):
                n = TILES[i][1]
                act.wait_ge(diff_ready, i + 1)
                act.activation(best[0:n, :, :], best[0:n, :, :], ACT.Exp).then_inc(exp_ready, 1)

            for g in range(4):
                act.wait_ge(turned, g + 1)
                act.activation(subT[:, 4 * g:4 * g + 4, :].rearrange("p a b -> p (a b)"), k.ps[:, g, :],
                               ACT.Copy).then_inc(sub_ready, 1)
            take_scores(0)
            act.wait_ge(prepared, 2)
            for i, (t0, n) in enumerate(TILES):
                if i < 2:
                    take_scores(i + 1)
                exponentials(i)

                def gelus(r, R, par):
                    act.wait_ge(u_used[GRP - 1], R + 1)
                    act.activation(weight[:, ds(r * RING, RING)], dots[:, par, :], ACT.Gelu).then_inc(gelu_done, 1)
                in_rounds(act, i, gelus)
                act.wait_ge(weight_ready, i + 1)

                def diagonals(r, R, par, mixed):
                    wait(act, v_used[GRP - 2], R - 1)
                    wait(act, v_used[GRP - 1], R - 1)
                    act.activation(wst[:, par, :], weight[:, ds(r * RING, RING)], ACT.Copy).then_inc(w_staged, 1)
                    act.wait_ge(w_staged, R + 1)
                    for j in range(RING - PER if mixed else RING):
                        one = k.ident[:, :] if n == P else fold[:, :]
                        last = act.activation(diag[:, par, j, 0:n], one, ACT.Copy, scale=wst[:, par, j:j + 1])
                    last.then_inc(diag_ready, 1)
                value_rounds(act, i, diagonals)
                act.wait_ge(sum_ready, i + 1)
                for part_ in range(2):
                    last = act.activation(k.h[0:n, i, part_ * 512:(part_ + 1) * 512], k.ps[0:n, part_, :], ACT.Copy)
                last.then_inc(sum_taken, 1)

        @block.tensor
        def _(pe):
            def score(i):
                t0, n = TILES[i]
                wait(pe, s_ready, 4 * i)
                for g in range(4):
                    for j in range(4):
                        hp = 4 * g + j
                        mm = pe.matmul(k.ps[0:n, 4 + g, j * P:(j + 1) * P], pqT[:, hp, t0:t0 + n], subT[:, hp, :],
                                       start=True, stop=True)
                    mm.then_inc(scored, 1)

            pe.wait_ge(landed, 32)
            for g in range(4):
                for j in range(4):
                    mm = pe.transpose(k.ps[:, g, j * P:(j + 1) * P], sub[:, 4 * g + j, :], k.ident[:, :])
                mm.then_inc(turned, 1)
            pe.wait_ge(sub_ready, 4)
            score(0)
            pe.wait_ge(prepared, 2)
            for i, (t0, n) in enumerate(TILES):
                if i < 2:
                    score(i + 1)
                wait(pe, sum_taken, i)
                outs = [k.ps[0:n, part_, :] for part_ in range(2)]
                for o in outs:
                    pe.matmul(o, zero[:, 0:n], subT[:, 0:4, :].rearrange("p a b -> p (a b)"), start=True, stop=False)

                def body(r, R, par, mixed):
                    wait_apart(pe, diag_ready, R + 1, begun_pe)
                    for g in range(GRP - 1 if mixed else GRP):
                        wait_apart(pe, v_landed[g], before + 16 * PER * (R + 1), begun_pe)
                        for m in range(PER):
                            j = g * PER + m
                            for part_ in range(2):
                                mm = pe.matmul(outs[part_], diag[:, par, j, 0:n], vr[:, j, part_ * 512:(part_ + 1) * 512],
                                               start=False, stop=False)
                        mm.then_inc(v_used[g], 1)
                value_rounds(pe, i, body)
                pe.wait_ge(acc_ready, i + 1)
                one = k.ident[:, :] if n == P else fold[:, :]
                for m in range(PER):
                    for part_ in range(2):
                        mm = pe.matmul(outs[part_], one, acc[:, m, part_ * 512:(part_ + 1) * 512], start=False,
                                       stop=(m == PER - 1))
                mm.then_inc(sum_ready, 1)


def peer(k, layer):
    io = k.io
    name = f"p{layer}"
    with ExitStack() as ctx:
        pqT = k.sb(ctx, name + "_qT", [P, 2 * PEER_H, T])
        gemm_stage(k, name + "q", [("feat", k.xT, io["peer_wq"][layer], 512,
                                    pqT[:, :, :].rearrange("p a t -> p (a t)"))])
        peer_stage(k, name + "e", layer, pqT)


def decode_step(nc, io):
    with ExitStack() as ctx:
        k = Kernel(nc, ctx, io)
        start_stage(k)
        y = [io["y_prompt"][0, 0:P], io["y_prompt"][0, P:SEQ], io["y_sample"].rearrange("b s d -> (b s) d")]
        for layer in range(DEPTH):
            even_mixer(k) if layer % 2 == 0 else odd_mixer(k)
            norm_stage(k, f"nx{layer}", io["ln_mix_g"][layer], io["ln_mix_b"][layer])
            memory_attention(k, layer)
            norm_stage(k, f"nm{layer}", io["ln_mem_g"][layer], io["ln_mem_b"][layer])
            peer(k, layer)
            norm_stage(k, f"nf{layer}", io["ln_ffn_g"][layer], io["ln_ffn_b"][layer], y if layer == DEPTH - 1 else None)
        with ExitStack() as c1:
            block = c1.enter_context(k.block())

            @block.scalar
            def _(act):
                k.copy_some(act, len(k.copies))
                act.wait_ge(k.copied, 16 * len(k.copies))


def constants():
    pos = np.concatenate([np.arange(SEQ), np.tile(PAST + np.arange(DEC_S), DEC_B)]).astype(np.float32)
    half = ROPE // 2
    inv = np.float32(10000.0) ** (-np.arange(half, dtype=np.float32) / np.float32(half))
    ang = (pos[:, None] * inv[None, :]).astype(np.float32)
    cos, sin = np.cos(ang), np.sin(ang)
    rope_tok = np.stack([cos, sin], axis=1)
    rope_feat = np.stack([np.concatenate([cos, cos], 1).T, np.concatenate([-sin, sin], 1).T], axis=1)
    dist = DIST_TOP - np.arange(N_DIST)
    exact = N_BUCKETS // 2
    d = np.maximum(dist, 1).astype(np.float32)
    large = exact + (np.log(d / exact) / np.float32(math.log(MAX_DIST / exact)) * (N_BUCKETS - exact)).astype(np.int32)
    bucket = np.where(dist < exact, dist, np.minimum(large, N_BUCKETS - 1))
    hot = np.zeros((N_BUCKETS + 1, 3, N_DIST), np.float32)
    for g, (w, dil) in enumerate(SWA_GROUPS):
        ok = (dist >= 0) & (dist <= w) & (dist % dil == 0)
        hot[np.where(ok, bucket, N_BUCKETS), g, np.arange(N_DIST)] = 1.0
    q = np.arange(P)[:, None, None] + P * np.arange(2)[None, :, None]
    causal = np.where(np.arange(SEQ)[None, None, :] <= q, 0.0, DISALLOWED)
    new = np.where(np.arange(DEC_S)[None, :] <= (np.arange(64) % DEC_S)[:, None], 0.0, DISALLOWED)
    out = {"ident": np.eye(P), "rope_tok": rope_tok, "rope_feat": rope_feat, "bucket_hot": hot, "causal": causal,
           "causal_new": new, "iota16": np.arange(TOPK)}
    return {n: np.ascontiguousarray(v.astype(np.float32)) for n, v in out.items()}


INPUTS = ["x_prompt", "x_sample", "cache_mla", "page_table", "cache_swa_w128", "cache_swa_w512", "cache_swa_w2048",
          "state_conv", "cache_mem_kv", "mem_prompt", "attn_w_in", "mla_q_norm", "mla_kv_norm", "mla_w_uq", "mla_w_uk",
          "mla_w_uv", "attn_w_out", "rel_bias", "conv_w_in", "conv_w", "conv_w_out", "mem_wq", "mem_wk", "mem_wv",
          "mem_wo", "ln_mix_g", "ln_mix_b", "ln_mem_g", "ln_mem_b", "ln_ffn_g", "ln_ffn_b", "peer_wq", "peer_subkeys",
          "peer_u", "peer_v"]
OUTPUTS = [("y_prompt", (1, SEQ, D)), ("y_sample", (DEC_B, DEC_S, D)), ("mla_rows_prompt", (1, 1, SEQ, MLA_ROW)),
           ("mla_rows_sample", (1, DEC_B, DEC_S, MLA_ROW))]
for _g, (_w, _) in enumerate(SWA_GROUPS):
    OUTPUTS += [(f"swa_prompt{_g}", (1, 1, _w, 2, SWA_H, SWA_D)), (f"swa_sample{_g}", (1, DEC_B, _w, 2, SWA_H, SWA_D))]
OUTPUTS += [("conv_prompt", (1, 1, 2, D)), ("conv_sample", (1, DEC_B, 2, D)),
            ("mem_kv_prompt", (DEPTH, 1, N_MEM, 2, MEM_H, MEM_D))]
SCRATCH = [("kv_new", (DEC_B * DEC_S, 6 * GW)), ("bias_by_dist", (3, SWA_H, N_DIST)), ("bias_rep", (3, SWA_H, P, REP_N))]


def kernel(**inputs):
    import numpy as _np
    import concourse.bacc as _bacc
    from concourse import mybir as _mybir
    from concourse.bass_utils import run_bass_kernel_spmd as _run

    nc = _bacc.Bacc("TRN2", target_bir_lowering=False, num_devices=1)
    arrays, io = {}, {}
    named = {n: _np.ascontiguousarray(inputs[n]) for n in INPUTS}
    named.update(constants())
    for n, a in named.items():
        arrays["in_" + n] = a
        io[n] = nc.dram_tensor("in_" + n, a.shape, _mybir.dt.from_np(a.dtype), kind="ExternalInput").ap()
    for n, shape in OUTPUTS:
        io[n] = nc.dram_tensor("out_" + n, shape, _mybir.dt.float32, kind="ExternalOutput").ap()
    for n, shape in SCRATCH:
        io[n] = nc.dram_tensor("scratch_" + n, shape, _mybir.dt.float32, kind="Internal").ap()
    decode_step(nc, io)
    r = _run(nc, [arrays], core_ids=[0])
    return tuple(r.results[0]["out_" + n] for n, _ in OUTPUTS)
```
